# Optimizing a Trainium2 kernel written in Bass

```python
import jax, jax.numpy as jnp
from jax import lax
import numpy as np

D_MODEL = 1024
BATCH = 1
SEQ = 1024
DEPTH = 1

EPS = 1e-6
CONV_DIM = 512
CONV_WIDTH = 31
NSA_HEADS = 8
NSA_KV_HEADS = 2
HEAD_DIM = 64
NSA_GROUP = NSA_HEADS // NSA_KV_HEADS
NSA_Q_DIM = NSA_HEADS * HEAD_DIM
NSA_KV_DIM = NSA_KV_HEADS * HEAD_DIM
CMP_LEN = 32
CMP_STRIDE = 16
CMP_HIDDEN = 128
SEL_BLOCK = 64
SEL_TOPK = 16
WINDOW = 512
Q_BLOCK = 128
FORCE_SCORE = 1e4
LRU_DIM = 512
LRU_HEADS = 8
LRU_BLOCK = LRU_DIM // LRU_HEADS
LRU_CONV_WIDTH = 4
LRU_C = 8.0
FFN_DIM = ((-(-8 * D_MODEL // 3)) + 255) // 256 * 256
IN_SIZES = [2 * CONV_DIM, NSA_Q_DIM, 6 * NSA_KV_DIM, 3 * NSA_HEADS, LRU_DIM, LRU_DIM]
IN_DIM = sum(IN_SIZES)
IN_SPLITS = [int(v) for v in np.cumsum(IN_SIZES)[:-1]]
N_BRANCH = 3

kernel_name = "hybrid_conv_nsa_rglru_adaln"

def rms_norm(x, g):
    xf = x.astype(jnp.float32)
    y = xf * lax.rsqrt(jnp.mean(xf * xf, axis=-1, keepdims=True) + EPS)
    return (y * g.astype(jnp.float32)).astype(x.dtype)

def layer_norm(x, g, b):
    xf = x.astype(jnp.float32)
    mu = jnp.mean(xf, axis=-1, keepdims=True)
    var = jnp.mean(jnp.square(xf - mu), axis=-1, keepdims=True)
    y = (xf - mu) * lax.rsqrt(var + EPS)
    return (y * g.astype(jnp.float32) + b.astype(jnp.float32)).astype(x.dtype)

def causal_depthwise_conv(x, w, b):
    k = w.shape[0]
    y = lax.conv_general_dilated(x, w[:, None, :].astype(x.dtype), window_strides=(1,),
                                 padding=((k - 1, 0),), dimension_numbers=('NWC', 'WIO', 'NWC'),
                                 feature_group_count=x.shape[-1])
    return y + b

def alibi_slopes(n):
    return jnp.asarray(np.array([2.0 ** (-8.0 * (h + 1) / n) for h in range(n)], dtype=np.float32))

def masked_softmax(s, mask):
    s = jnp.where(mask, s.astype(jnp.float32), -jnp.inf)
    m = jnp.max(s, axis=-1, keepdims=True)
    m = jnp.where(jnp.isfinite(m), m, 0.0)
    p = jnp.exp(s - m)
    den = jnp.sum(p, axis=-1, keepdims=True)
    return p / jnp.where(den > 0, den, 1.0)

def gather_blocks(blocks, ix):
    return jax.vmap(jax.vmap(lambda b_, i_: b_[i_]))(blocks, ix)

def conformer_conv(u, w_dw, b_dw, ln_g, ln_b, w_o):
    a, g = jnp.split(u, 2, axis=-1)
    v = a * jax.nn.sigmoid(g)
    v = causal_depthwise_conv(v, w_dw, b_dw)
    v = jax.nn.silu(layer_norm(v, ln_g, ln_b))
    return v @ w_o

def rglru_block(ux, ug, w_conv, b_conv, w_a, b_a, w_x, b_x, lam, w_o):
    bsz, s = ux.shape[0], ux.shape[1]
    xr = causal_depthwise_conv(ux, w_conv, b_conv)
    xh = xr.reshape(bsz, s, LRU_HEADS, LRU_BLOCK)
    r = jax.nn.sigmoid(jnp.einsum('bshi,hij->bshj', xh, w_a).reshape(bsz, s, LRU_DIM) + b_a)
    i = jax.nn.sigmoid(jnp.einsum('bshi,hij->bshj', xh, w_x).reshape(bsz, s, LRU_DIM) + b_x)
    log_a = -LRU_C * r.astype(jnp.float32) * jax.nn.softplus(-lam.astype(jnp.float32))
    a = jnp.exp(log_a)
    bterm = jnp.sqrt(-jnp.expm1(2.0 * log_a)) * (i * xr).astype(jnp.float32)

    def combine(left, right):
        a_l, b_l = left
        a_r, b_r = right
        return a_r * a_l, a_r * b_l + b_r

    _, h = lax.associative_scan(combine, (a, bterm), axis=1)
    y = h.astype(ux.dtype) * jax.nn.gelu(ug)
    return y @ w_o

def compress_blocks(k, cidx, pe, w1, w2):
    bsz, n_cmp = k.shape[0], cidx.shape[0]
    blk = k[:, cidx] + pe[:, None, :]
    blk = blk.transpose(0, 1, 3, 2, 4).reshape(bsz, n_cmp, NSA_KV_HEADS, CMP_LEN * HEAD_DIM)
    return jax.nn.gelu(blk @ w1) @ w2

def nsa_mixer(q, k_c, v_c, k_s, v_s, k_w, v_w, gate_logits, pe_k, w_ck1, w_ck2, pe_v, w_cv1, w_cv2, w_o):
    bsz, s = q.shape[0], q.shape[1]
    n_cmp = (s - CMP_LEN) // CMP_STRIDE + 1
    n_sel = s // SEL_BLOCK
    k_top = min(SEL_TOPK, n_sel)
    n_qb = s // Q_BLOCK
    scale = HEAD_DIM ** -0.5

    cidx = jnp.arange(n_cmp)[:, None] * CMP_STRIDE + jnp.arange(CMP_LEN)[None, :]
    kc = compress_blocks(k_c, cidx, pe_k, w_ck1, w_ck2)
    vc = compress_blocks(v_c, cidx, pe_v, w_cv1, w_cv2)
    cmp_start = jnp.arange(n_cmp) * CMP_STRIDE
    cmp_end = cmp_start + CMP_LEN - 1
    sel_start = jnp.arange(n_sel) * SEL_BLOCK
    ov = jnp.clip(jnp.minimum(cmp_start[:, None] + CMP_LEN, sel_start[None, :] + SEL_BLOCK)
                  - jnp.maximum(cmp_start[:, None], sel_start[None, :]), 0).astype(jnp.float32) / CMP_LEN

    kb = k_s.reshape(bsz, n_sel, SEL_BLOCK, NSA_KV_HEADS, HEAD_DIM).transpose(0, 3, 1, 2, 4)
    vb = v_s.reshape(bsz, n_sel, SEL_BLOCK, NSA_KV_HEADS, HEAD_DIM).transpose(0, 3, 1, 2, 4)
    kwp = jnp.pad(k_w, ((0, 0), (WINDOW, 0), (0, 0), (0, 0)))
    vwp = jnp.pad(v_w, ((0, 0), (WINDOW, 0), (0, 0), (0, 0)))
    slopes = alibi_slopes(NSA_HEADS).reshape(NSA_KV_HEADS, NSA_GROUP)
    gates = jax.nn.sigmoid(gate_logits.astype(jnp.float32)).reshape(bsz, s, NSA_KV_HEADS, NSA_GROUP, 3)
    jsel = jnp.arange(n_sel)
    sub = jnp.arange(SEL_BLOCK)

    def attend_block(qb):
        q0 = qb * Q_BLOCK
        qpos = q0 + jnp.arange(Q_BLOCK)
        qblk = lax.dynamic_slice_in_dim(q, q0, Q_BLOCK, axis=1) * scale
        gblk = lax.dynamic_slice_in_dim(gates, q0, Q_BLOCK, axis=1)
        dist_c = qpos[:, None] - cmp_end[None, :]
        s_c = jnp.einsum('bqgrd,bcgd->bgrqc', qblk, kc) - slopes[:, :, None, None] * dist_c
        p_c = masked_softmax(s_c, dist_c >= 0)
        o_c = jnp.einsum('bgrqc,bcgd->bqgrd', p_c.astype(vc.dtype), vc)
        imp = jnp.einsum('bgrqc,cj->bgqj', p_c, ov)
        qblk_id = qpos // SEL_BLOCK
        forced = (jsel[None, :] == 0) | (jsel[None, :] == qblk_id[:, None]) | (jsel[None, :] == qblk_id[:, None] - 1)
        valid = sel_start[None, :] <= qpos[:, None]
        imp = jnp.where(forced, FORCE_SCORE, jnp.where(valid, imp, -1.0))
        _, top = lax.top_k(imp, k_top)
        ks = gather_blocks(kb, top).reshape(bsz, NSA_KV_HEADS, Q_BLOCK, k_top * SEL_BLOCK, HEAD_DIM)
        vs = gather_blocks(vb, top).reshape(bsz, NSA_KV_HEADS, Q_BLOCK, k_top * SEL_BLOCK, HEAD_DIM)
        spos = (top[..., None] * SEL_BLOCK + sub).reshape(bsz, NSA_KV_HEADS, Q_BLOCK, k_top * SEL_BLOCK)
        dist_s = qpos[None, None, :, None] - spos
        s_s = jnp.einsum('bqgrd,bgqkd->bgrqk', qblk, ks) - slopes[None, :, :, None, None] * dist_s[:, :, None]
        p_s = masked_softmax(s_s, (dist_s >= 0)[:, :, None])
        o_s = jnp.einsum('bgrqk,bgqkd->bqgrd', p_s.astype(vs.dtype), vs)
        kw = lax.dynamic_slice_in_dim(kwp, q0, Q_BLOCK + WINDOW, axis=1)
        vw = lax.dynamic_slice_in_dim(vwp, q0, Q_BLOCK + WINDOW, axis=1)
        kpos = q0 - WINDOW + jnp.arange(Q_BLOCK + WINDOW)
        dist_w = qpos[:, None] - kpos[None, :]
        mask_w = (dist_w >= 0) & (dist_w < WINDOW) & (kpos[None, :] >= 0)
        s_w = jnp.einsum('bqgrd,bkgd->bgrqk', qblk, kw) - slopes[:, :, None, None] * dist_w
        p_w = masked_softmax(s_w, mask_w)
        o_w = jnp.einsum('bgrqk,bkgd->bqgrd', p_w.astype(vw.dtype), vw)
        o = gblk[..., 0:1] * o_c + gblk[..., 1:2] * o_s + gblk[..., 2:3] * o_w
        return o.astype(q.dtype)

    o = lax.map(attend_block, jnp.arange(n_qb))
    o = jnp.moveaxis(o, 0, 1).reshape(bsz, s, NSA_Q_DIM)
    return o @ w_o

def setup_inputs(seed: int = 0) -> dict:
    key = jax.random.key(seed)
    ks = jax.random.split(key, 33)
    f32 = jnp.float32

    def nrm(k, shape, scale):
        return jax.random.normal(k, shape, f32) * scale

    u = jax.random.uniform(ks[22], (DEPTH, LRU_DIM), f32, minval=0.9, maxval=0.999)
    sa = u ** (1.0 / LRU_C)
    lam = jnp.log(sa) - jnp.log1p(-sa)
    return {
        "x": nrm(ks[0], (BATCH, SEQ, D_MODEL), 1.0),
        "c": nrm(ks[1], (BATCH, D_MODEL), 1.0),
        "w_mod": nrm(ks[2], (DEPTH, D_MODEL, 6 * D_MODEL), 0.5 * D_MODEL ** -0.5),
        "b_mod": nrm(ks[3], (DEPTH, 6 * D_MODEL), 0.01),
        "norm_mix": 1.0 + nrm(ks[4], (DEPTH, D_MODEL), 0.05),
        "norm_ffn": 1.0 + nrm(ks[5], (DEPTH, D_MODEL), 0.05),
        "w_in": nrm(ks[6], (DEPTH, D_MODEL, IN_DIM), D_MODEL ** -0.5),
        "conv_w_dw": nrm(ks[7], (DEPTH, CONV_WIDTH, CONV_DIM), CONV_WIDTH ** -0.5),
        "conv_b_dw": nrm(ks[8], (DEPTH, CONV_DIM), 0.01),
        "conv_ln_g": 1.0 + nrm(ks[9], (DEPTH, CONV_DIM), 0.05),
        "conv_ln_b": nrm(ks[10], (DEPTH, CONV_DIM), 0.01),
        "conv_w_out": nrm(ks[11], (DEPTH, CONV_DIM, D_MODEL), CONV_DIM ** -0.5),
        "nsa_pe_k": nrm(ks[12], (DEPTH, CMP_LEN, HEAD_DIM), 0.02),
        "nsa_w_ck1": nrm(ks[13], (DEPTH, CMP_LEN * HEAD_DIM, CMP_HIDDEN), (CMP_LEN * HEAD_DIM) ** -0.5),
        "nsa_w_ck2": nrm(ks[14], (DEPTH, CMP_HIDDEN, HEAD_DIM), CMP_HIDDEN ** -0.5),
        "nsa_pe_v": nrm(ks[15], (DEPTH, CMP_LEN, HEAD_DIM), 0.02),
        "nsa_w_cv1": nrm(ks[16], (DEPTH, CMP_LEN * HEAD_DIM, CMP_HIDDEN), (CMP_LEN * HEAD_DIM) ** -0.5),
        "nsa_w_cv2": nrm(ks[17], (DEPTH, CMP_HIDDEN, HEAD_DIM), CMP_HIDDEN ** -0.5),
        "nsa_w_out": nrm(ks[18], (DEPTH, NSA_Q_DIM, D_MODEL), NSA_Q_DIM ** -0.5),
        "lru_w_conv": nrm(ks[19], (DEPTH, LRU_CONV_WIDTH, LRU_DIM), LRU_CONV_WIDTH ** -0.5),
        "lru_b_conv": nrm(ks[20], (DEPTH, LRU_DIM), 0.01),
        "lru_w_a": nrm(ks[21], (DEPTH, LRU_HEADS, LRU_BLOCK, LRU_BLOCK), LRU_BLOCK ** -0.5),
        "lru_b_a": nrm(ks[23], (DEPTH, LRU_DIM), 0.01),
        "lru_w_x": nrm(ks[24], (DEPTH, LRU_HEADS, LRU_BLOCK, LRU_BLOCK), LRU_BLOCK ** -0.5),
        "lru_b_x": nrm(ks[25], (DEPTH, LRU_DIM), 0.01),
        "lru_lam": lam,
        "lru_w_out": nrm(ks[26], (DEPTH, LRU_DIM, D_MODEL), LRU_DIM ** -0.5),
        "w_merge": nrm(ks[27], (DEPTH, D_MODEL, N_BRANCH * D_MODEL), D_MODEL ** -0.5),
        "b_merge": nrm(ks[28], (DEPTH, N_BRANCH * D_MODEL), 0.01),
        "w_out": nrm(ks[29], (DEPTH, D_MODEL, D_MODEL), D_MODEL ** -0.5),
        "w_ffn_in": nrm(ks[30], (DEPTH, D_MODEL, 2 * FFN_DIM), D_MODEL ** -0.5),
        "w_ffn_out": nrm(ks[31], (DEPTH, FFN_DIM, D_MODEL), FFN_DIM ** -0.5),
        "final_norm": 1.0 + nrm(ks[32], (D_MODEL,), 0.05),
    }

def reference(x, c, w_mod, b_mod, norm_mix, norm_ffn, w_in, conv_w_dw, conv_b_dw, conv_ln_g, conv_ln_b,
              conv_w_out, nsa_pe_k, nsa_w_ck1, nsa_w_ck2, nsa_pe_v, nsa_w_cv1, nsa_w_cv2, nsa_w_out,
              lru_w_conv, lru_b_conv, lru_w_a, lru_b_a, lru_w_x, lru_b_x, lru_lam, lru_w_out,
              w_merge, b_merge, w_out, w_ffn_in, w_ffn_out, final_norm):
    bsz, s = x.shape[0], x.shape[1]
    for l in range(DEPTH):
        mod = (c @ w_mod[l] + b_mod[l])[:, None, :]
        sh1, sc1, g1, sh2, sc2, g2 = jnp.split(mod, 6, axis=-1)
        h = rms_norm(x, norm_mix[l]) * (1.0 + sc1) + sh1
        u = h @ w_in[l]
        u_conv, u_q, u_kv, u_gate, u_lx, u_lg = jnp.split(u, IN_SPLITS, axis=-1)
        y_conv = conformer_conv(u_conv, conv_w_dw[l], conv_b_dw[l], conv_ln_g[l], conv_ln_b[l], conv_w_out[l])
        q = u_q.reshape(bsz, s, NSA_KV_HEADS, NSA_GROUP, HEAD_DIM)
        k_c, v_c, k_s, v_s, k_w, v_w = [t.reshape(bsz, s, NSA_KV_HEADS, HEAD_DIM) for t in jnp.split(u_kv, 6, axis=-1)]
        y_nsa = nsa_mixer(q, k_c, v_c, k_s, v_s, k_w, v_w, u_gate, nsa_pe_k[l], nsa_w_ck1[l], nsa_w_ck2[l],
                          nsa_pe_v[l], nsa_w_cv1[l], nsa_w_cv2[l], nsa_w_out[l])
        y_lru = rglru_block(u_lx, u_lg, lru_w_conv[l], lru_b_conv[l], lru_w_a[l], lru_b_a[l], lru_w_x[l],
                            lru_b_x[l], lru_lam[l], lru_w_out[l])
        gm_conv, gm_nsa, gm_lru = jnp.split(jax.nn.sigmoid(h @ w_merge[l] + b_merge[l]), N_BRANCH, axis=-1)
        merged = gm_conv * y_conv + gm_nsa * y_nsa + gm_lru * y_lru
        x = x + g1 * (merged @ w_out[l])
        h2 = rms_norm(x, norm_ffn[l]) * (1.0 + sc2) + sh2
        a, b = jnp.split(h2 @ w_ffn_in[l], 2, axis=-1)
        x = x + g2 * ((jax.nn.silu(a) * b) @ w_ffn_out[l])
    return rms_norm(x, final_norm)


_drawn_inputs = setup_inputs


def setup_inputs(seed=0):
    import zlib

    import numpy as np

    out = dict(_drawn_inputs(seed))
    spreads = {}
    factors = {'b_mod': 2.845,
     'conv_b_dw': 8.0,
     'conv_ln_g': 6.409,
     'conv_ln_b': 46.171,
     'nsa_pe_k': 45.724,
     'nsa_w_ck1': 2.935,
     'nsa_w_ck2': 2.937,
     'nsa_pe_v': 48.488,
     'lru_b_conv': 5.301,
     'lru_b_a': 64.0,
     'lru_b_x': 43.559,
     'b_merge': 8.0,
     'norm_ffn': 3.246}
    for name, (base, spread) in spreads.items():
        noise = np.random.default_rng([zlib.crc32(name.encode()), seed]).standard_normal(out[name].shape)
        drawn = base * np.exp(spread * noise) if base else spread * noise
        out[name] = __import__('jax').numpy.asarray(drawn.astype(out[name].dtype))
    for name, factor in factors.items():
        out[name] = (out[name] * factor).astype(out[name].dtype)
    return out
```

```python
from contextlib import ExitStack

import numpy as np
import concourse.bass as bass
from concourse import mybir

F32 = mybir.dt.float32
F32R = mybir.dt.float32r
ALU = mybir.AluOpType
ACT = mybir.ActivationFunctionType
AX = mybir.AxisListType

P = 128
S = 1024
D = 1024
KT = D // P
TT = S // P
HW = 512
EPS = 1e-6
CONV = 512
CC = CONV // P
TAPS = 31
LTAPS = 4
HD = 64
HEADS = 8
CMP_LEN, CMP_STRIDE = 32, 16
NCMP = (S - CMP_LEN) // CMP_STRIDE + 1
WIN = 512
FFN = 2816
FP = FFN // (2 * P)
NEG = -1e30
SLOPES = [2.0 ** (-8.0 * (h + 1) / HEADS) for h in range(HEADS)]

ROWS = {}
_n = 0
for _name, _len in (("b_mod", 48), ("norm_mix", 8), ("norm_ffn", 8), ("conv_b_dw", 4), ("conv_ln_g", 4),
                    ("conv_ln_b", 4), ("lru_b_conv", 4), ("lru_b_a", 4), ("lru_b_x", 4), ("lru_lam", 4),
                    ("b_merge", 24), ("c", 8)):
    ROWS[_name] = (_n, _len)
    _n += _len
NROWS = _n

LX, KC_, VC_, KS_, KW_, LG, QQ, VS_, VW_, GA_ = 0, 4, 5, 6, 7, 8, 12, 16, 17, 18
NUX = 19
KB = 1024
LINKS = 16 * 5 + 2


def build(nc, t, out, stop=None):
    ctx = ExitStack()
    with ctx:
        base = 16512

        def at(name, shape, dt, kb):
            return nc.alloc_sbuf_tensor_at(name, shape, dt, offset=base + int(kb * KB))

        def sem(name):
            return ctx.enter_context(nc.semaphore(name))

        PS = ctx.enter_context(nc.psum_tensor("PS", [P, 8, HW], F32))

        HH = at("HH", [P, KT, S], F32R, 0)
        HL = at("HL", [P, KT, S], F32R, 32)
        CV = at("CV", [P, CC + 1, S], F32, 64)
        UX = at("UX", [P, NUX, S], F32, 84)
        WR = at("WR", [P, 2, KT, P], F32, 160)
        WH = at("WH", [P, 2, KT, P], F32R, 168)
        WL = at("WL", [P, 2, KT, P], F32R, 176)
        X = at("X", [P, TT, D], F32, 84)
        WM = at("WM", [P, 4, 2 * D], F32, 116)
        ACC0 = at("ACC0", [P, 2 * D], F32, 148)
        HT = at("HT", [P, 2, HW], F32, 156)
        STK = at("STK", [P, 3, P], F32, 184)
        JUNK = at("JUNK", [P, D], F32, 188)
        SG = at("SG", [P, 2, HW], F32, 184)
        MP = at("MP", [P, 2, D], F32, 188)
        ACC = at("ACC", [P, D], F32, 196)
        XR = at("XR", [P, S], F32, 184)
        RA = at("RA", [P, S], F32, 188)
        RI = at("RI", [P, S], F32, 192)
        RT = at("RT", [P, S], F32, 196)
        WAX = at("WAX", [P, 2, CC, P], F32, 200)
        V = at("V", [P, TT, 2, P], F32, 160)
        W1 = at("W1", [P, CMP_LEN, P], F32, 168)
        ST = at("ST", [P, CMP_LEN, HD], F32, 148)
        GT = at("GT", [P, TT, 3 * HEADS], F32, 156)
        KC = at("KC", [P, HD], F32, 157)
        VC = at("VC", [P, P], F32, 157.25)
        HID = at("HID", [P, 2, HD], F32, 157.75)
        W2 = at("W2", [P, 2, HD], F32, 158.25)
        PEROW = at("PEROW", [P, 2, P], F32, 158.75)
        SQ = at("SQ", [P, 2, CC, HW], F32, 184)
        RS = at("RS", [P, 2, HW], F32, 200)
        BS = at("BS", [P, 2, S], F32, 84)
        BW = at("BW", [P, 2, 640], F32, 92)
        BC = at("BC", [P, 2, TT, HD], F32, 148)
        PB = at("PB", [P, 2, 1728], F32, 168)
        PT = at("PT", [P, 2, 14, P], F32, 184)
        QS = at("QS", [P, S], F32, 80)
        OT = at("OT", [P, 2, P], F32, 182)
        WB = at("WB", [P, 2, CC, P], F32, 184)
        GM = at("GM", [P, 2, S], F32, 188)
        YT = at("YT", [P, 2, HW], F32, 156)
        DG = at("DG", [P, KT, P], F32, 200)
        G1B = at("G1B", [P, D], F32, 80)
        G2B = at("G2B", [P, D], F32, 196)
        WOR = at("WOR", [P, 2, 4, HW], F32, 180)
        WOH = at("WOH", [P, KT, D], F32R, 116)
        WOL = at("WOL", [P, KT, D], F32R, 148)
        X1 = at("X1", [P, TT, D], F32, 84)
        XN = at("XN", [P, 4, D], F32, 64)
        HT2 = at("HT2", [P, 2, HW], F32, 80)
        JUNK2 = at("JUNK2", [P, D], F32, 184)
        WR3 = at("WR3", [P, 2, KT, P], F32, 188)
        WFR = at("WFR", [P, 2, D], F32, 116)
        WFH = at("WFH", [P, 2, D], F32R, 124)
        WFL = at("WFL", [P, 2, D], F32R, 132)
        FH = at("FH", [P, 2, S], F32R, 140)
        FL = at("FL", [P, 2, S], F32R, 148)
        SA = at("SA", [P, 2, HW], F32, 156)
        FT = at("FT", [P, 2, HW], F32, 64)
        FNB = at("FNB", [P, D], F32, 72)
        CO = 204.0
        IDENT = at("IDENT", [P, P], F32, CO)
        ONES = at("ONES", [P, P], F32, CO + 0.5)
        COLS = at("COLS", [P, NROWS], F32, CO + 1.0)
        CW = at("CW", [P, CC, TAPS], F32, CO + 1.5)
        LCW = at("LCW", [P, CC, LTAPS], F32, CO + 2.0)
        MODC = at("MODC", [P, 48], F32, CO + 2.0625)
        SM = at("SM", [P, 192], F32, CO + 2.25)

        def sm(a, n):
            return SM[:, a:a + n]

        SSQ, RSTD, RTMP = sm(0, 8), sm(8, 8), sm(16, 8)
        GSC, GSH = sm(24, 8), sm(32, 8)
        SPT = [sm(40 + 4 * i, 4) for i in range(6)]
        SP8, NSP8 = sm(64, 4), sm(68, 4)
        ROWOK = sm(72, 1)
        CB = sm(73, 4)
        GSC2, GSH2 = sm(100, 8), sm(108, 8)
        NM = [sm(80, 3), sm(83, 3)]
        DEN = [sm(86, 3), sm(89, 3)]
        RR = [sm(92, 3), sm(95, 3)]

        def col(name, i=0, n=1):
            a = ROWS[name][0] + i
            return COLS[:, a:a + n]

        ident_zero, const_set = sem("ident_zero"), sem("const_set")
        stack_loaded, wax_zero, wax_loaded = sem("stack_loaded"), sem("wax_zero"), sem("wax_loaded")
        x_loaded = [sem(f"x_loaded{i}") for i in range(4)]
        wm_loaded = [sem(f"wm_loaded{i}") for i in range(4)]
        wm_used, acc0_ready, mod0_mm, mod_ready = sem("wm_used"), sem("acc0_ready"), sem("mod0_mm"), sem("mod_ready")
        stack_t, cols_ready = sem("stack_t"), sem("cols_ready")
        dve_step = sem("dve_step")

        class FormSems:

            def __init__(s, n):
                s.square, s.recip, s.rstd = sem(n + "_square"), sem(n + "_recip"), sem(n + "_rstd")
                s.xhat, s.turned, s.plain = sem(n + "_xhat"), sem(n + "_turned"), sem(n + "_plain")
                s.hi, s.ready = sem(n + "_hi"), sem(n + "_ready")

        f1 = FormSems("h1")

        class RingSems:

            def __init__(s, n):
                s.loaded = [sem(n + "_loaded0"), sem(n + "_loaded1")]
                s.hi, s.lo, s.mm, s.out = sem(n + "_hi"), sem(n + "_lo"), sem(n + "_mm"), sem(n + "_out")

        r1, r2, r3 = RingSems("in"), RingSems("merge"), RingSems("ffn")
        f2, f3 = FormSems("h2"), FormSems("final")
        wb_loaded = [sem("wb_loaded0"), sem("wb_loaded1")]
        y_mm, y_used, m_step, merged = sem("y_mm"), sem("y_used"), sem("m_step"), sem("merged")
        dg_ready, gb_mm, gb_ready = sem("dg_ready"), sem("gb_mm"), sem("gb_ready")
        m_hi, m_ready = sem("m_hi"), sem("m_ready")
        wo_loaded = [sem("wo_loaded0"), sem("wo_loaded1")]
        wo_scaled, wo_hi, wo_lo, wo_mm, x1_done = (sem("wo_" + n) for n in ("scaled", "hi", "lo", "mm", "x1"))
        x1_loaded = [sem(f"x1_loaded{i}") for i in range(4)]
        wf_loaded, wf_scaled, wf_hi, wf_lo = (sem("wf_" + n) for n in ("loaded", "scaled", "hi", "lo"))
        f_gate, f_prod, f_hi, f_lo = (sem("f_" + n) for n in ("gate", "prod", "hi", "lo"))
        o_mm, o_added = sem("o_mm"), sem("o_added")
        fn_loaded, rows_ready = sem("fn_loaded"), sem("rows_ready")
        sig_done = sem("sig_done")
        mp_loaded = [sem("mp_loaded0"), sem("mp_loaded1")]
        mp_used, mod_mm, modc_done = sem("mp_used"), sem("mod_mm"), sem("modc_done")
        out_stored = sem("out_stored")
        conv_steps = sem("conv_steps")
        vt_turned, v_ready = sem("vt_turned"), sem("v_ready")
        lam_abs, lam_exp = sem("lam_abs"), sem("lam_exp")
        lru_step, act_step = sem("lru_step"), sem("act_step")
        lru_x, lru_mm, lru_ab, lru_v, lru_sq, lru_gelu = (sem("lru_" + n) for n in ("x", "mm", "ab", "v", "sq", "gelu"))
        y_lru_ready = sem("y_lru_ready")
        ln_sum, ln_cent, ln_sq, ln_var, ln_rec, ln_rstd, ln_norm, y_conv_ready = (
            sem("ln_" + n) for n in ("sum", "cent", "sq", "var", "rec", "rstd", "norm", "y"))
        w1_loaded, w2_loaded = [sem("w1_loaded_k"), sem("w1_loaded_v")], sem("w2_loaded")
        pe_turned, st_ready, cmp_mm, hid_ready, cmp2_mm, kvc_ready = (
            sem("cmp_" + n) for n in ("pe_turned", "st", "mm", "hid", "mm2", "ready"))
        bias_made, bias_ready = sem("bias_made"), sem("att_bias")
        att_q, att_sc, att_mx, att_ex, att_tg, att_ev, att_pv, att_oo, att_ot, att_oc = (
            sem("att_" + n) for n in ("q", "sc", "mx", "ex", "tg", "ev", "pv", "oo", "ot", "oc"))
        att_step, gated = sem("att_step"), sem("gated")

        dbg = sem("dbg")
        PASSES = ((WH, HH), (WH, HL), (WL, HH))

        def chunk_mm(pe, slot, r):
            for half in range(2):
                n = 0
                for w, h in PASSES:
                    for k in range(KT):
                        last = pe.matmul(PS[:, 2 * slot + half, :], w[:, slot, k, :], h[:, k, half * HW:(half + 1) * HW],
                                         start=(n == 0), stop=(n == 3 * KT - 1))
                        n += 1
                last.then_inc(r.mm, 1)

        def gate(eng, s, value):
            eng.wait_ge(s, value)
            eng.sem_inc(gated, 1)

        class Chain:

            def __init__(c, eng, s, base=0):
                c.eng, c.s, c.base, c.n = eng, s, base, 0

            def link(c, ins):
                c.n += 1
                ins.then_inc(c.s, 1)
                c.eng.wait_ge(c.s, c.base + c.n)

        STEPS = [(qi, g) for qi in range(TT) for g in range(2)]

        def tiles(qi):
            lo = max(0, qi - WIN // P)
            return [(0, k, P * k) for k in range(qi + 1)] + \
                   [(1, k, S + P * (k - lo)) for k in range(lo, qi + 1)] + [(2, 0, S + 640)]

        GROUPS = [-(-len(tiles(qi)) // 4) for qi, g in STEPS]
        GEND = [sum(GROUPS[:u + 1]) for u in range(len(STEPS))]
        NG = GEND[-1]
        assert NG % 2 == 0

        w_in = t["w_in"][0].rearrange("(k p) n -> p k n", p=P)
        w_mod = t["w_mod"][0].rearrange("(k p) n -> k p n", p=P)
        x_t = t["x"][0].rearrange("(t p) d -> p t d", p=P)

        block = ctx.enter_context(nc.Block())

        @block.sync
        def _(sp):
            for name, (a, n) in ROWS.items():
                src = t[name] if name == "c" else t[name][0:1, :]
                sp.dma_start(STK[a:a + n, 0, :], src.rearrange("a (r p) -> (a r) p", p=P)).then_inc(stack_loaded, 16)
            for c in range(CC):
                sp.dma_start(STK[TAPS * c:TAPS * (c + 1), 1, :], t["conv_w_dw"][0, :, c * P:(c + 1) * P]).then_inc(stack_loaded, 16)
                sp.dma_start(STK[LTAPS * c:LTAPS * (c + 1), 2, :], t["lru_w_conv"][0, :, c * P:(c + 1) * P]).then_inc(stack_loaded, 16)
            for i in range(4):
                sp.dma_start(X[:, 2 * i:2 * i + 2, :], x_t[:, 2 * i:2 * i + 2, :]).then_inc(x_loaded[i], 16)
            for k in range(KT):
                if k >= 4:
                    sp.wait_ge(wm_used, k - 3)
                sp.dma_start(WM[:, k % 4, :], w_mod[k, :, 0:2 * D]).then_inc(wm_loaded[k % 4], 16)

            def load_chunk(slot, columns):
                sp.dma_start(WR[:, slot], columns).then_inc(r1.loaded[slot], 16)

            def pair(m, first):
                for slot in range(2):
                    if not first:
                        sp.wait_ge(r1.lo, 2 * m + slot - 1)
                    load_chunk(slot, w_in[:, :, bass.ds(m * P + slot * CONV, P)])
                for k in range(KT):
                    if not (first and k < 2):
                        sp.wait_ge(mp_used, KT * m + k - 1)
                    elif k == 0:
                        sp.wait_ge(stack_t, 1)
                        sp.wait_ge(f1.square, TT)
                    sp.dma_start(MP[:, k % 2, :], w_mod[k, :, bass.ds((m + 2) * D, D)]).then_inc(mp_loaded[k % 2], 16)

            pair(0, True)
            with sp.Fori(1, CC) as m:
                pair(m, False)
            KV = 2 * CONV + HEADS * HD
            places = [2328 + P * c for c in range(CC)] + [KV, KV + P, KV + 2 * P, KV + 4 * P] + \
                     [2328 + CONV + P * c for c in range(CC)] + [None] * 4 + [KV + 3 * P, KV + 5 * P, KV + 6 * P]
            for u, c0 in enumerate(places):
                i = 2 * CC + u
                sp.wait_ge(r1.lo, i - 1)
                if c0 is None:
                    j = u - QQ
                    for g in range(2):
                        a = 2 * CONV + g * 4 * HD + j * HD
                        sp.dma_start(WR[:, i % 2, :, g * HD:(g + 1) * HD], w_in[:, :, a:a + HD]).then_inc(r1.loaded[i % 2], 16)
                else:
                    load_chunk(i % 2, w_in[:, :, c0:c0 + P])
            sp.wait_ge(vt_turned, 5)
            sp.wait_ge(r1.mm, 54)
            for a, kv in enumerate("kv"):
                sp.dma_start(W2[:, a, :], t[f"nsa_w_c{kv}2"][0]).then_inc(w2_loaded, 16)
                for g in range(2):
                    sp.dma_start(PEROW[0:CMP_LEN, a, g * HD:(g + 1) * HD], t[f"nsa_pe_{kv}"][0]).then_inc(w2_loaded, 16)
            for a, kv in enumerate("kv"):
                if a:
                    sp.wait_ge(cmp_mm, 1)
                for g in range(2):
                    sp.dma_start(W1[g * HD:(g + 1) * HD, :, :],
                                 t[f"nsa_w_c{kv}1"][0].rearrange("(l d) n -> d l n", d=HD)).then_inc(w1_loaded[a], 16)
            wm = t["w_merge"][0].rearrange("(k p) n -> p k n", p=P)
            wy = [t[n][0].rearrange("(k p) n -> p k n", p=P) for n in ("conv_w_out", "nsa_w_out", "lru_w_out")]
            wg = t["nsa_w_out"][0].rearrange("(g j d) n -> g d j n", g=2, d=HD)
            sp.wait_ge(att_oc, 4 * TT)

            def load_merge(m, first):
                for q in range(6):
                    nn, br, slot = q // 3, q % 3, q % 2
                    if not (first and q < 2):
                        sp.wait_ge(r2.lo, 6 * m + q - 1)
                    sp.dma_start(WR[:, slot], wm[:, :, bass.ds((2 * m + nn) * P + br * D, P)]).then_inc(r2.loaded[slot], 16)
                    if not (first and q < 2):
                        sp.wait_ge(y_mm, 6 * m + q - 1)
                    cols = bass.ds((2 * m + nn) * P, P)
                    if br == 1:
                        for g in range(2):
                            sp.dma_start(WB[g * HD:(g + 1) * HD, slot], wg[g, :, :, cols]).then_inc(wb_loaded[slot], 16)
                    else:
                        sp.dma_start(WB[:, slot], wy[br][:, :, cols]).then_inc(wb_loaded[slot], 16)

            load_merge(0, True)
            with sp.Fori(1, 4) as m:
                load_merge(m, False)
            wo = t["w_out"][0].rearrange("(k p) n -> p k n", p=P)
            sp.wait_ge(merged, 48)
            for q in range(4):
                if q >= 2:
                    sp.wait_ge(wo_lo, q - 1)
                sp.dma_start(WOR[:, q % 2], wo[:, 4 * (q % 2):4 * (q % 2) + 4, (q // 2) * HW:(q // 2 + 1) * HW]).then_inc(wo_loaded[q % 2], 16)
            sp.wait_ge(m_ready, KT)
            for i in range(4):
                sp.dma_start(X1[:, 2 * i:2 * i + 2, :], x_t[:, 2 * i:2 * i + 2, :]).then_inc(x1_loaded[i], 16)
            wfi = t["w_ffn_in"][0].rearrange("(k p) n -> p k n", p=P)
            wfo = t["w_ffn_out"][0].rearrange("(m f p) n -> m p f n", f=2, p=P)
            sp.wait_ge(wo_lo, 4)

            def load_ffn(m, first):
                for q in range(4):
                    if not (first and q < 2):
                        sp.wait_ge(r3.lo, 4 * m + q - 1)
                    sp.dma_start(WR3[:, q % 2], wfi[:, :, bass.ds((2 * m + q // 2) * P + (q % 2) * FFN, P)]).then_inc(r3.loaded[q % 2], 16)
                    if q == 1:
                        if first:
                            sp.wait_ge(wo_mm, 16)
                        else:
                            sp.wait_ge(wf_lo, m)
                        sp.dma_start(WFR[:], wfo[m] if first else wfo[bass.ds(m, 1), :, :, :].rearrange("a p f n -> p (a f) n")).then_inc(wf_loaded, 16)

            load_ffn(0, True)
            with sp.Fori(1, FP) as m:
                load_ffn(m, False)
            sp.wait_ge(f2.turned, 16)
            sp.dma_start(FNB[:], t["final_norm"].partition_broadcast(P)).then_inc(fn_loaded, 16)
            o_t = out[0].rearrange("(t p) d -> p t d", p=P)
            for i in range(4):
                sp.wait_ge(rows_ready, 2 * i + 2)
                sp.dma_start(o_t[:, 2 * i:2 * i + 2, :], X1[:, 2 * i:2 * i + 2, :]).then_inc(out_stored, 16)
            sp.wait_ge(out_stored, 64)
            if stop == "mix":
                sp.wait_ge(dbg, 1)
                o = out[0].rearrange("(t p) d -> p t d", p=P)
                sp.dma_start(o[:, 0:4, :], (UX[:, LG:LG + 4, :] if 0 else CV[:, 0:4, :])).then_inc(out_stored, 16)
                sp.dma_start(o[:, 4:8, :], UX[:, QQ:QQ + 4, :]).then_inc(out_stored, 16)
                sp.wait_ge(out_stored, 32)
            if stop == "in":
                sp.wait_ge(dbg, 1)
                sp.dma_start(out[0].rearrange("(t p) d -> p t d", p=P), UX[:, 0:8, :]).then_inc(out_stored, 16)
                sp.wait_ge(out_stored, 16)
            if stop == "h":
                sp.wait_ge(f1.ready, 16)
                sp.dma_start(out[0].rearrange("(t p) d -> p t d", p=P), HH[:].bitcast(F32)).then_inc(out_stored, 16)
                sp.wait_ge(out_stored, 16)

        @block.gpsimd
        def _(pool):
            pool.memset(IDENT[:], 0.0).then_inc(ident_zero, 1)
            pool.wait_ge(ident_zero, 1)
            pool.affine_select(out=IDENT[:], in_=IDENT[:], compare_op=ALU.not_equal, fill=1.0, base=0,
                               pattern=[[-1, P]], channel_multiplier=1).then_inc(const_set, 1)
            pool.memset(ONES[:], 1.0).then_inc(const_set, 1)
            pool.memset(ROWOK, 1.0).then_inc(const_set, 1)
            pool.wait_ge(const_set, 3)
            pool.affine_select(out=ROWOK, in_=ROWOK, compare_op=ALU.is_ge, fill=0.0, base=-(CMP_LEN - 1),
                               pattern=[[0, 1]], channel_multiplier=1).then_inc(const_set, 1)
            pool.memset(WAX[:], 0.0).then_inc(wax_zero, 1)
            pool.wait_ge(wax_zero, 1)
            for a, w in enumerate((t["lru_w_a"], t["lru_w_x"])):
                for c in range(CC):
                    for i in range(2):
                        pool.dma_start(WAX[i * HD:(i + 1) * HD, a, c, i * HD:(i + 1) * HD], w[0, 2 * c + i]).then_inc(wax_loaded, 16)

            def lo(i, slot, r, raw=WR):
                pool.wait_ge(r.hi, i + 1)
                pool.tensor_tensor(WL[:, slot], raw[:, slot], WH[:, slot].bitcast(F32), ALU.subtract).then_inc(r.lo, 1)

            with pool.Fori(0, 13) as m:
                lo(2 * m, 0, r1)
                lo(2 * m + 1, 1, r1)
            lo(26, 0, r1)

            pool.wait_ge(y_lru_ready, CC)
            pool.wait_ge(cmp_mm, 2)
            pool.iota(BS[:, 0, :], [[1, S]], base=-(S - P), channel_multiplier=-1,
                      allow_small_or_imprecise_dtypes=True).then_inc(bias_made, 1)
            pool.iota(BW[:, 0, :], [[1, 640]], base=-WIN, channel_multiplier=-1,
                      allow_small_or_imprecise_dtypes=True).then_inc(bias_made, 1)
            pool.iota(BC[:, 0, :, 0:NCMP], [[-P, TT], [CMP_STRIDE, NCMP]], base=CMP_LEN - 1, channel_multiplier=-1,
                      allow_small_or_imprecise_dtypes=True).then_inc(bias_made, 1)
            pool.wait_ge(bias_made, 3)
            pool.affine_select(out=BS[:, 0, :], in_=BS[:, 0, :], compare_op=ALU.is_ge, fill=NEG, base=S - P,
                               pattern=[[-1, S]], channel_multiplier=1).then_inc(bias_made, 1)
            pool.affine_select(out=BW[:, 0, :], in_=BW[:, 0, :], compare_op=ALU.is_ge, fill=NEG, base=WIN,
                               pattern=[[-1, 640]], channel_multiplier=1).then_inc(bias_made, 1)
            pool.affine_select(out=BC[:, 0, :, 0:NCMP], in_=BC[:, 0, :, 0:NCMP], compare_op=ALU.is_ge, fill=NEG,
                               base=-(CMP_LEN - 1), pattern=[[P, TT], [-CMP_STRIDE, NCMP]],
                               channel_multiplier=1).then_inc(bias_made, 1)
            pool.wait_ge(bias_made, 6)
            pool.affine_select(out=BW[:, 0, :], in_=BW[:, 0, :], compare_op=ALU.is_ge, fill=NEG, base=-1,
                               pattern=[[1, 640]], channel_multiplier=-1).then_inc(bias_made, 1)
            pool.wait_ge(bias_made, 7)

            def tables(g):
                return BS[:, g, :], BW[:, g, :], BC[:, g, :, 0:NCMP]

            for g, f in ((1, SLOPES[4]), (0, SLOPES[0])):
                for a, b in zip(tables(g), tables(0)):
                    pool.tensor_scalar(a, b, f, None, ALU.mult).then_inc(bias_ready, 1)
                pool.wait_ge(bias_ready, 3 if g else 6)
            with pool.Fori(1, 4) as j:
                gate(pool, att_mx, 16 * j)
                for g in range(2):
                    for a in tables(g):
                        pool.tensor_scalar(a, a, SLOPES[1] / SLOPES[0], None, ALU.mult).then_inc(bias_ready, 1)

            with pool.Fori(0, 12) as m:
                lo(2 * m, 0, r2)
                lo(2 * m + 1, 1, r2)

            def scale(m):
                pool.wait_ge(wf_loaded, 16 * m + 16)
                pool.tensor_tensor(WFR[:], WFR[:], G2B[:].unsqueeze(1).to_broadcast([P, 2, D]), ALU.mult).then_inc(wf_scaled, 1)

            lo(0, 0, r3, WR3)
            lo(1, 1, r3, WR3)
            scale(0)

            def ffn(m, last):
                for fi in range(2):
                    if not (last and fi):
                        lo(4 * m + 2 * fi + 2, 0, r3, WR3)
                        lo(4 * m + 2 * fi + 3, 1, r3, WR3)
                    pool.wait_ge(f_hi, 2 * m + fi + 1)
                    pool.tensor_tensor(FL[:, fi, :], FT[:].rearrange("p a b -> p (a b)"), FH[:, fi, :].bitcast(F32),
                                       ALU.subtract).then_inc(f_lo, 1)
                    if fi == 0:
                        pool.wait_ge(wf_hi, m + 1)
                        pool.tensor_tensor(WFL[:], WFR[:], WFH[:].bitcast(F32), ALU.subtract).then_inc(wf_lo, 1)
                    elif not last:
                        scale(m + 1)

            with pool.Fori(0, FP - 1) as m:
                ffn(m, False)
            ffn(FP - 1, True)

        @block.scalar
        def _(act):
            def stats(src, f, half, junk, waits):
                for i in range(4 * half, 4 * half + 4):
                    waits(i)
                    if i:
                        act.wait_ge(f.square, i)
                    act.activation(junk[:], src[:, i, :], ACT.Square, accum_out=SSQ[:, i:i + 1]).then_inc(f.square, 1)
                act.wait_ge(f.recip, half + 1)
                act.activation(RSTD[:, 4 * half:4 * half + 4], RTMP[:, 4 * half:4 * half + 4], ACT.Sqrt).then_inc(f.rstd, 1)

            def form(f, half, GSC, GSH, HT):
                for b in range(8 * half, 8 * half + 8):
                    k = b % KT
                    act.wait_ge(f.turned, b + 1)
                    if b >= 2:
                        act.wait_ge(f.ready, b - 1)
                    act.activation(HT[:, b % 2, :], PS[:, 4 + b % 4, :], ACT.Identity,
                                   bias=GSH[:, k:k + 1], scale=GSC[:, k:k + 1]).then_inc(f.plain, 1)

            for half in range(2):
                stats(X, f1, half, JUNK, lambda i: act.wait_ge(x_loaded[i // 2], 16))
            act.wait_ge(mod_ready, 2)
            for half in range(2):
                form(f1, half, GSC, GSH, HT)

            def hi(r, slot, loaded, mm=None, raw=WR):
                act.wait_ge(r.loaded[slot], loaded)
                if mm is not None:
                    act.wait_ge(r.mm, mm)
                act.activation(WH[:, slot], raw[:, slot], ACT.Copy).then_inc(r.hi, 1)

            hi(r1, 0, 16)
            hi(r1, 1, 16)

            def conv_pair(m, first):
                hi(r1, 0, 16 * m + 32, 4 * m + 2)
                for half in range(2):
                    act.wait_ge(r1.mm, 4 * m + 3 + half)
                    if not first:
                        act.wait_ge(r1.out, 2 * m - 1 + half)
                    act.activation(SG[:, half, :], PS[:, 2 + half, :], ACT.Sigmoid).then_inc(sig_done, 1)
                hi(r1, 1, 16 * m + 32, 4 * m + 4)

            act.wait_ge(stack_t, 1)
            conv_pair(0, True)
            with act.Fori(1, CC) as m:
                conv_pair(m, False)

            def put(i, u, slot):
                for half in range(2):
                    act.wait_ge(r1.mm, 2 * i + 1 + half)
                    act.activation(UX[:, u, half * HW:(half + 1) * HW], PS[:, 2 * slot + half, :], ACT.Copy).then_inc(r1.out, 1)

            act.wait_ge(r1.out, 2 * CC)
            with act.Fori(0, 5) as m:
                put(2 * m + 8, 2 * m, 0)
                hi(r1, 0, 16 * m + 96, 4 * m + 18)
                put(2 * m + 9, 2 * m + 1, 1)
                hi(r1, 1, 16 * m + 96, 4 * m + 20)
            lands = [16 * (i // 2 + 1) for i in range(27)]
            for i in range(27):
                lands[i] += 16 * sum(1 for q in range(20, 24) if q <= i and q % 2 == i % 2)
            for i in range(18, 27):
                put(i, i - 8, i % 2)
                if i + 2 < 27:
                    hi(r1, i % 2, lands[i + 2], 2 * i + 2)
            if stop == "in":
                act.wait_ge(r1.out, 8 + 38)
                act.sem_inc(dbg, 1)

            for b in range(4):
                act.wait_ge(vt_turned, b + 1)
                act.activation(V[:, 4 * (b % 2):4 * (b % 2) + 4, b // 2, :], PS[:, 4 + b, :].rearrange("p (t f) -> p t f", t=4),
                               ACT.Copy).then_inc(v_ready, 1)
            act.wait_ge(vt_turned, 5)
            logits = PS[:, 0, 0:TT * 3 * HEADS].rearrange("p (a b) -> p a b", b=3)
            gates = GT[:].rearrange("p t (h b) -> p (t h) b", b=3)
            act.activation(gates[:, :, 0:2], logits[:, :, 1:3], ACT.Sigmoid).then_inc(v_ready, 1)
            act.activation(gates[:, :, 2:3], logits[:, :, 0:1], ACT.Sigmoid).then_inc(v_ready, 1)

            act.wait_ge(lam_abs, 1)
            act.activation(SPT[2], SPT[1], ACT.Exp, scale=-1.0).then_inc(lam_exp, 1)
            ch = Chain(act, act_step)
            for c in range(CC):
                act.wait_ge(lru_mm, c + 1)
                ch.link(act.activation(RA[:], PS[:, 4:6, :], ACT.Sigmoid, bias=col("lru_b_a", c)))
                act.activation(RI[:], PS[:, 6:8, :], ACT.Sigmoid, bias=col("lru_b_x", c)).then_inc(lru_ab, 1)
                ch.link(act.activation(RT[:], RA[:], ACT.Tanh, scale=SP8[:, c:c + 1]))
                act.activation(RA[:], RA[:], ACT.Exp, scale=NSP8[:, c:c + 1]).then_inc(lru_ab, 1)
                act.wait_ge(lru_v, c + 1)
                act.activation(RT[:], RT[:], ACT.Sqrt).then_inc(lru_sq, 1)
                act.activation(UX[:, LG + c, :], UX[:, LG + c, :], ACT.Gelu_apprx_tanh).then_inc(lru_gelu, 1)

            for half in range(2):
                cols = slice(half * HW, (half + 1) * HW)
                act.wait_ge(ln_cent, half + 1)
                act.activation(SQ[:, half], CV[:, 0:CC, cols], ACT.Square).then_inc(ln_sq, 1)
            for half in range(2):
                act.wait_ge(ln_rec, half + 1)
                act.activation(RS[:, half, :], RS[:, half, :], ACT.Sqrt).then_inc(ln_rstd, 1)
            act.wait_ge(ln_norm, 2)
            for c in range(CC):
                act.activation(CV[:, c, :], CV[:, c, :], ACT.Silu, bias=col("conv_ln_b", c),
                               scale=col("conv_ln_g", c)).then_inc(y_conv_ready, 1)

            for a in range(2):
                act.wait_ge(cmp_mm, a + 1)
                ch.link(act.activation(CB[:, 2 * a:2 * a + 2], PS[:, 2:4, HD - 1], ACT.Copy))
                if a:
                    act.wait_ge(cmp2_mm, 1)
                for g in range(2):
                    act.activation(HID[:, g, 0:NCMP], PS[:, 2 + g, 0:NCMP], ACT.Gelu_apprx_tanh,
                                   bias=CB[:, 2 * a + g:2 * a + g + 1]).then_inc(hid_ready, 1)
                act.wait_ge(cmp2_mm, a + 1)
                if a == 0:
                    act.activation(KC[:, 0:NCMP], PS[:, 1, 0:NCMP], ACT.Copy).then_inc(kvc_ready, 1)
                else:
                    act.activation(VC[0:NCMP, :], PS[0:NCMP, 1, 0:P], ACT.Copy).then_inc(kvc_ready, 1)

            with act.Fori(0, 4) as j:
                act.activation(QS[:], UX[:, bass.ds(j + QQ, 1), :], ACT.Copy, scale=HD ** -0.5).then_inc(att_q, 1)

                def exps(u):
                    qi, g = STEPS[u]
                    b, K, Kw = u % 2, P * (qi + 1), P * (min(qi, WIN // P) + 1)
                    act.wait_ge(att_mx, 16 * j + u + 1)
                    for n, (a, e) in enumerate(((0, K), (S, S + Kw), (S + 640, S + 640 + NCMP))):
                        act.activation(PB[:, b, a:e], PB[:, b, a:e], ACT.Exp, bias=NM[b][:, n:n + 1],
                                       accum_out=DEN[b][:, n:n + 1]).then_inc(att_ex, 1)

                def evac(u):
                    qi, g = STEPS[u]
                    n = len(tiles(qi))
                    if u >= 2:
                        act.wait_ge(att_pv, 16 * j + u - 1)
                    for k in range(GROUPS[u]):
                        m = min(4, n - 4 * k)
                        G = GEND[u] - GROUPS[u] + k
                        act.wait_ge(att_tg, NG * j + G + 1)
                        act.activation(PT[:, u % 2, 4 * k:4 * k + m, :], PS[:, 4 + G % 2, 0:m * P].rearrange("p (a b) -> p a b", b=P),
                                       ACT.Copy).then_inc(att_ev, 1)

                def put_o(qi):
                    gate(act, att_ot, TT * j + qi + 1)
                    act.activation(UX[:, bass.ds(j + QQ, 1), qi * P:(qi + 1) * P], PS[:, 7, 0:P], ACT.Copy).then_inc(att_oc, 1)

                exps(0)
                for u in range(16):
                    evac(u)
                    if u % 2 == 0 and u:
                        put_o(u // 2 - 1)
                    if u < 15:
                        exps(u + 1)
                put_o(TT - 1)
                act.wait_ge(att_oc, TT * j + TT)
            def merge(m, first, last):
                for q in range(6):
                    nn, br, slot = q // 3, q % 3, q % 2
                    bias = col("b_merge", br * KT, KT)[:, bass.ds(2 * m + nn, 1)]
                    for half in range(2):
                        if not (first and q < 2):
                            act.wait_ge(y_used, 12 * m + 2 * q - 3 + half)
                        gate(act, r2.mm, 12 * m + 2 * q + half + 1)
                        act.activation(GM[:, slot, half * HW:(half + 1) * HW], PS[:, 2 * slot + half, :], ACT.Sigmoid,
                                       bias=bias).then_inc(r2.out, 1)
                    if not (last and q >= 4):
                        hi(r2, slot, 48 * m + 16 * (q // 2) + 32)

            hi(r2, 0, 16)
            hi(r2, 1, 16)
            merge(0, True, False)
            with act.Fori(1, 3) as m:
                merge(m, False, False)
            merge(3, False, True)

            act.wait_ge(merged, 48)
            for k in range(KT):
                act.activation(HH[:, k, :], UX[:, k, :], ACT.Copy).then_inc(m_hi, 1)
            for q in range(4):
                act.wait_ge(wo_scaled, q + 1)
                act.activation(WOH[:, 4 * (q % 2):4 * (q % 2) + 4, (q // 2) * HW:(q // 2 + 1) * HW], WOR[:, q % 2], ACT.Copy).then_inc(wo_hi, 1)
            for half in range(2):
                stats(X1, f2, half, JUNK2, lambda i: act.wait_ge(x1_done, 2 * i + 2))
                form(f2, half, GSC2, GSH2, HT2)

            act.wait_ge(wo_mm, 16)
            hi(r3, 0, 16, raw=WR3)
            hi(r3, 1, 16, raw=WR3)

            def ffn(m, first, last):
                for fi in range(2):
                    for half in range(2):
                        act.wait_ge(r3.mm, 8 * m + 4 * fi + half + 1)
                        if not (first and fi == 0):
                            act.wait_ge(f_prod, 4 * m + 2 * fi - 1 + half)
                        act.activation(SA[:, half, :], PS[:, half, :], ACT.Silu).then_inc(f_gate, 1)
                    if not (last and fi):
                        hi(r3, 0, 32 * m + 16 * fi + 32, raw=WR3)
                        hi(r3, 1, 32 * m + 16 * fi + 32, 8 * m + 4 * fi + 4, raw=WR3)
                    act.wait_ge(f_prod, 4 * m + 2 * fi + 2)
                    if not first:
                        act.wait_ge(o_mm, 16 * m)
                    act.activation(FH[:, fi, :], FT[:].rearrange("p a b -> p (a b)"), ACT.Copy).then_inc(f_hi, 1)
                    if fi == 0:
                        act.wait_ge(wf_scaled, m + 1)
                        act.activation(WFH[:], WFR[:], ACT.Copy).then_inc(wf_hi, 1)

            ffn(0, True, False)
            with act.Fori(1, FP - 1) as m:
                ffn(m, False, False)
            ffn(FP - 1, False, True)
            for half in range(2):
                stats(X1, f3, half, JUNK2, lambda i: act.wait_ge(o_added, 16 * (FP - 1) + 2 * i + 2))

        @block.tensor
        def _(pe):
            pe.wait_ge(stack_loaded, 16 * (len(ROWS) + 2 * CC))
            pe.wait_ge(const_set, 2)
            pe.transpose(PS[:, 0, 0:NROWS], STK[0:NROWS, 0, :], IDENT[0:NROWS, 0:NROWS])
            pe.transpose(PS[:, 1, 0:CC * TAPS], STK[0:CC * TAPS, 1, :], IDENT[0:CC * TAPS, 0:CC * TAPS])
            pe.transpose(PS[:, 2, 0:CC * LTAPS], STK[0:CC * LTAPS, 2, :], IDENT[0:CC * LTAPS, 0:CC * LTAPS]).then_inc(stack_t, 1)
            pe.wait_ge(acc0_ready, 1)
            for j in range(16):
                last = pe.matmul(PS[:, 3, j:j + 1], ACC0[:, j * P:(j + 1) * P], ONES[:, 0:1], start=True, stop=True)
            last.then_inc(mod0_mm, 1)

            def turn(src, f, half, at0):
                pe.wait_ge(f.xhat, 4 * half + 4)
                for b in range(8 * half, 8 * half + 8):
                    k = b % KT
                    if b >= 4:
                        pe.wait_ge(f.plain, b - 3)
                    for i in range(4):
                        last = pe.transpose(PS[:, 4 + b % 4, i * P:(i + 1) * P], src[:, at0 + i, k * P:(k + 1) * P], IDENT[:])
                    last.then_inc(f.turned, 1)

            turn(X, f1, 0, 0)
            turn(X, f1, 1, 4)
            pe.wait_ge(f1.ready, 16)

            def conv_pair(m, first):
                for slot in range(2):
                    pe.wait_ge(r1.lo, 2 * m + slot + 1)
                    if not first and slot == 0:
                        pe.wait_ge(r1.out, 2 * m)
                    chunk_mm(pe, slot, r1)
                pe.wait_ge(mp_used, KT * (m + 1))
                for j in range(KT):
                    last = pe.matmul(PS[:, 4, j:j + 1], ACC[:, j * P:(j + 1) * P], ONES[:, 0:1], start=True, stop=True)
                last.then_inc(mod_mm, 1)

            pe.wait_ge(cols_ready, 1)
            conv_pair(0, True)
            with pe.Fori(1, CC) as m:
                conv_pair(m, False)
            with pe.Fori(0, 9) as m:
                for slot in range(2):
                    pe.wait_ge(r1.lo, 2 * m + slot + 9)
                    pe.wait_ge(r1.out, 4 * m + 2 * slot + (8 if slot == 0 else 6))
                    chunk_mm(pe, slot, r1)
            pe.wait_ge(r1.lo, 27)
            pe.wait_ge(r1.out, 8 + 34)
            chunk_mm(pe, 0, r1)

            pe.wait_ge(r1.out, 8 + 38)
            pe.wait_ge(modc_done, 4)
            for b in range(4):
                for i in range(4):
                    tok = 4 * (b % 2) + i
                    last = pe.transpose(PS[:, 4 + b, i * P:(i + 1) * P], UX[:, VS_ + b // 2, tok * P:(tok + 1) * P], IDENT[:])
                last.then_inc(vt_turned, 1)
            n = 3 * HEADS
            for tok in range(TT):
                last = pe.transpose(PS[:, 0, tok * n:(tok + 1) * n], UX[0:n, GA_, tok * P:(tok + 1) * P], IDENT[0:n, 0:n])
            last.then_inc(vt_turned, 1)

            pe.wait_ge(wax_loaded, 16 * 2 * 2 * CC)
            pe.wait_ge(v_ready, 4)
            for c in range(CC):
                pe.wait_ge(lru_x, c + 1)
                if c:
                    pe.wait_ge(lru_ab, 2 * c)
                for a in range(2):
                    for half in range(2):
                        last = pe.matmul(PS[:, 4 + 2 * a + half, :], WAX[:, a, c, :], XR[:, half * HW:(half + 1) * HW],
                                         start=True, stop=True)
                last.then_inc(lru_mm, 1)

            pe.wait_ge(conv_steps, TAPS * CC)
            pe.wait_ge(v_ready, 6)
            for half in range(2):
                for c in range(CC):
                    last = pe.matmul(PS[:, half, :], ONES[:], CV[:, c, half * HW:(half + 1) * HW], start=(c == 0), stop=(c == CC - 1))
                last.then_inc(ln_sum, 1)
            for half in range(2):
                pe.wait_ge(ln_sq, half + 1)
                for c in range(CC):
                    last = pe.matmul(PS[:, 2 + half, :], ONES[:], SQ[:, half, c, :], start=(c == 0), stop=(c == CC - 1))
                last.then_inc(ln_var, 1)

            pe.wait_ge(w2_loaded, 16 * 6)
            pe.wait_ge(ln_norm, 2)
            for a in range(2):
                if a:
                    pe.wait_ge(st_ready, 3)
                pe.transpose(PS[:, 0, 0:CMP_LEN], PEROW[0:CMP_LEN, a, :], IDENT[0:CMP_LEN, 0:CMP_LEN]).then_inc(pe_turned, 1)
                pe.wait_ge(w1_loaded[a], 32)
                pe.wait_ge(st_ready, 3 * a + 3)
                if a:
                    pe.wait_ge(hid_ready, 2)
                for g in range(2):
                    rows = slice(g * HD, (g + 1) * HD)
                    for l in range(CMP_LEN):
                        last = pe.matmul(PS[:, 2 + g, 0:HD], W1[rows, l, :], ST[rows, l, :], start=(l == 0), stop=(l == CMP_LEN - 1))
                last.then_inc(cmp_mm, 1)
                pe.wait_ge(hid_ready, 2 * a + 2)
                if a:
                    pe.wait_ge(kvc_ready, 1)
                for g in range(2):
                    if a == 0:
                        last = pe.matmul(PS[g * HD:(g + 1) * HD, 1, 0:NCMP], W2[:, 0, :], HID[:, g, 0:NCMP], start=True, stop=True)
                    else:
                        last = pe.matmul(PS[0:NCMP, 1, g * HD:(g + 1) * HD], HID[:, g, 0:NCMP], W2[:, 1, :], start=True, stop=True)
                last.then_inc(cmp2_mm, 1)

            pe.wait_ge(kvc_ready, 2)
            with pe.Fori(0, 4) as j:
                pe.wait_ge(att_q, j + 1)

                def scores(u):
                    qi, g = STEPS[u]
                    rows = slice(g * HD, (g + 1) * HD)
                    q = QS[rows, qi * P:(qi + 1) * P]
                    K, Kw = P * (qi + 1), P * (min(qi, WIN // P) + 1)
                    if u:
                        pe.wait_ge(att_mx, 16 * j + u)
                    for b, (a, e) in enumerate(((0, min(K, HW)), (HW, K))):
                        if e > a:
                            pe.matmul(PS[:, b, 0:e - a], q, UX[rows, KS_, a:e], start=True, stop=True)
                    for b, (a, e) in enumerate(((K - Kw, K - Kw + min(Kw, HW)), (K - Kw + HW, K))):
                        if e > a:
                            pe.matmul(PS[:, 2 + b, 0:e - a], q, UX[rows, KW_, a:e], start=True, stop=True)
                    pe.matmul(PS[:, 3, P:P + NCMP], q, KC[rows, 0:NCMP], start=True, stop=True).then_inc(att_sc, 1)

                def turn_p(u):
                    qi, g = STEPS[u]
                    pe.wait_ge(att_ex, 48 * j + 3 * u + 3)
                    ts = tiles(qi)
                    for k in range(GROUPS[u]):
                        G = GEND[u] - GROUPS[u] + k
                        if G >= 2:
                            gate(pe, att_ev, NG * j + G - 1)
                        for i, (br, kt, a) in enumerate(ts[4 * k:4 * k + 4]):
                            m = NCMP if br == 2 else P
                            last = pe.transpose(PS[0:m, 4 + G % 2, i * P:(i + 1) * P], PB[:, u % 2, a:a + m], IDENT[:])
                        last.then_inc(att_tg, 1)

                def turn_o(qi):
                    pe.wait_ge(att_oo, 16 * j + 2 * qi + 2)
                    if qi:
                        pe.wait_ge(att_oc, TT * j + qi)
                    pe.transpose(PS[:, 7, 0:P], OT[:, qi % 2, :], IDENT[:]).then_inc(att_ot, 1)

                def pv(u):
                    qi, g = STEPS[u]
                    pe.wait_ge(att_ev, NG * j + GEND[u])
                    if u:
                        pe.wait_ge(att_oo, 16 * j + u)
                    ts = tiles(qi)
                    for i, (br, kt, a) in enumerate(ts):
                        o = PS[:, 6, br * HD:(br + 1) * HD]
                        first = i == 0 or ts[i - 1][0] != br
                        stop_ = i + 1 == len(ts) or ts[i + 1][0] != br
                        if br == 2:
                            last = pe.matmul(o, PT[0:NCMP, u % 2, i, :], VC[0:NCMP, g * HD:(g + 1) * HD], start=True, stop=True)
                        else:
                            last = pe.matmul(o, PT[:, u % 2, i, :], V[:, kt, br, g * HD:(g + 1) * HD], start=first, stop=stop_)
                    last.then_inc(att_pv, 1)

                scores(0)
                for u in range(16):
                    if u < 15:
                        scores(u + 1)
                    turn_p(u)
                    if u % 2 == 0 and u:
                        turn_o(u // 2 - 1)
                    pv(u)
                turn_o(TT - 1)
                pe.wait_ge(att_mx, 16 * j + 16)
                pe.wait_ge(att_ev, NG * j + NG)
                pe.wait_ge(att_oc, TT * j + TT)

            for n in range(2):
                pe.wait_ge(dg_ready, 8 * n + 8)
                if n:
                    pe.wait_ge(gb_ready, 1)
                for b in range(2):
                    last = pe.matmul(PS[:, b, :], ONES[:], DG[:, 4 * b:4 * b + 4, :].rearrange("p a b -> p (a b)"), start=True, stop=True)
                last.then_inc(gb_mm, 1)
            pe.wait_ge(gb_ready, 2)

            Y = [[CV[:, k, :] for k in range(CC)], [UX[:, QQ + k, :] for k in range(CC)], [UX[:, LG + k, :] for k in range(CC)]]
            WBL = [[16, 32, 64], [32, 48, 64]]

            def merge(m, first):
                for q in range(6):
                    nn, br, slot = q // 3, q % 3, q % 2
                    pe.wait_ge(r2.lo, 6 * m + q + 1)
                    if not (first and q < 2):
                        pe.wait_ge(r2.out, 12 * m + 2 * q - 2)
                    chunk_mm(pe, slot, r2)
                    pe.wait_ge(wb_loaded[slot], 64 * m + WBL[slot][q // 2])
                    if not (first and q < 2):
                        pe.wait_ge(y_used, 12 * m + 2 * q - 2)
                    for half in range(2):
                        for k in range(CC):
                            last = pe.matmul(PS[:, 4 + 2 * slot + half, :], WB[:, slot, k, :], Y[br][k][:, half * HW:(half + 1) * HW],
                                             start=(k == 0), stop=(k == CC - 1))
                    last.then_inc(y_mm, 1)

            merge(0, True)
            with pe.Fori(1, 4) as m:
                merge(m, False)

            pe.wait_ge(m_ready, KT)
            pe.wait_ge(wo_lo, 4)
            pe.wait_ge(r2.out, 48)
            for tok in range(TT):
                rows = slice(tok * P, (tok + 1) * P)
                for nh in range(2):
                    i = 2 * tok + nh
                    if i >= 4:
                        pe.wait_ge(x1_done, i - 3)
                    n = 0
                    for h, w in ((HH, WOH), (HH, WOL), (HL, WOH)):
                        for k in range(KT):
                            last = pe.matmul(PS[:, i % 4, :], h[:, k, rows], w[:, k, nh * HW:(nh + 1) * HW],
                                             start=(n == 0), stop=(n == 3 * KT - 1))
                            n += 1
                    last.then_inc(wo_mm, 1)
                if tok == 5:
                    pe.wait_ge(y_used, 48)
                    turn(XN, f2, 0, 0)
            turn(XN, f2, 1, 0)
            pe.wait_ge(f2.ready, 16)
            pe.wait_ge(x1_done, 16)

            def out_mm(m):
                pe.wait_ge(f_lo, 2 * m + 2)
                pe.wait_ge(wf_lo, m + 1)
                for tok in range(TT):
                    rows = slice(tok * P, (tok + 1) * P)
                    for nh in range(2):
                        i = 2 * tok + nh
                        if i >= 4:
                            pe.wait_ge(o_added, 16 * m + i - 3)
                        n = 0
                        for h, w in ((FH, WFH), (FH, WFL), (FL, WFH)):
                            for fi in range(2):
                                last = pe.matmul(PS[:, 4 + i % 4, :], h[:, fi, rows], w[:, fi, nh * HW:(nh + 1) * HW],
                                                 start=(n == 0), stop=(n == 5))
                                n += 1
                        last.then_inc(o_mm, 1)

            def ffn(m, first):
                for q in range(4):
                    pe.wait_ge(r3.lo, 4 * m + q + 1)
                    if not (first and q < 2):
                        pe.wait_ge(f_prod, 4 * m + 2 * (q // 2))
                    chunk_mm(pe, q % 2, r3)
                    if q == 1 and not first:
                        if not (isinstance(m, int) and m == 1):
                            pass
                        out_mm(m - 1)
                        pe.wait_ge(o_added, 16 * m)

            ffn(0, True)
            with pe.Fori(1, FP) as m:
                ffn(m, False)
            out_mm(FP - 1)

        @block.vector
        def _(dve):
            steps = [0]

            def link(ins):
                steps[0] += 1
                ins.then_inc(dve_step, 1)
                dve.wait_ge(dve_step, steps[0])

            dve.wait_ge(stack_t, 1)
            dve.tensor_copy(COLS[:], PS[:, 0, 0:NROWS])
            dve.tensor_copy(CW[:], PS[:, 1, 0:CC * TAPS].rearrange("p (c t) -> p c t", c=CC))
            link(dve.tensor_copy(LCW[:], PS[:, 2, 0:CC * LTAPS].rearrange("p (c t) -> p c t", c=CC)))
            dve.sem_inc(cols_ready, 1)
            ccol = col("c", 0, 8)

            def mod0(k):
                dve.wait_ge(wm_loaded[k % 4], 16 * (k // 4 + 1))
                if k == 0:
                    ins = dve.tensor_scalar(ACC0[:], WM[:, 0, :], ccol[:, 0:1], None, ALU.mult)
                else:
                    dve.wait_ge(wm_used, k)
                    ins = dve.scalar_tensor_tensor(ACC0[:], WM[:, k % 4, :], ccol[:, k:k + 1], ACC0[:], ALU.mult, ALU.add)
                ins.then_inc(wm_used, 1)

            def rstd(f, half):
                a = slice(4 * half, 4 * half + 4)
                dve.wait_ge(f.square, 4 * half + 4)
                link(dve.tensor_scalar(RTMP[:, a], SSQ[:, a], 1.0 / D, EPS, ALU.mult, ALU.add))
                dve.reciprocal(RTMP[:, a], RTMP[:, a]).then_inc(f.recip, 1)
                dve.wait_ge(f.rstd, half + 1)

            def split(f, half0, HT):
                for b in range(8 * half0, 8 * half0 + 8):
                    half, k = b // KT, b % KT
                    cols = slice(half * HW, (half + 1) * HW)
                    dve.wait_ge(f.plain, b + 1)
                    dve.tensor_copy(HH[:, k, cols], HT[:, b % 2, :]).then_inc(f.hi, 1)
                    dve.wait_ge(f.hi, b + 1)
                    dve.tensor_tensor(HL[:, k, cols], HT[:, b % 2, :], HH[:, k, cols].bitcast(F32), ALU.subtract).then_inc(f.ready, 1)

            for k in range(2):
                mod0(k)
            for i in range(TT):
                if i % 4 == 0:
                    rstd(f1, i // 4)
                dve.tensor_scalar(X[:, i, :], X[:, i, :], RSTD[:, i:i + 1], None, ALU.mult).then_inc(f1.xhat, 1)
            for k in range(2, KT):
                mod0(k)
            dve.wait_ge(wm_used, KT)
            dve.sem_inc(acc0_ready, 1)
            dve.wait_ge(mod0_mm, 1)
            link(dve.tensor_tensor(MODC[:, 0:16], PS[:, 3, 0:16], col("b_mod", 0, 16), ALU.add))
            dve.tensor_copy(GSH, MODC[:, 0:8]).then_inc(mod_ready, 1)
            dve.scalar_tensor_tensor(GSC, MODC[:, 8:16], 1.0, col("norm_mix", 0, 8), ALU.add, ALU.mult).then_inc(mod_ready, 1)
            split(f1, 0, HT)
            split(f1, 1, HT)

            def taps(c, lo, hi, at0):
                n = at0
                for j in range(lo, hi):
                    shift = j
                    w = CW[:, c, TAPS - 1 - shift:TAPS - shift]
                    if not (shift == 0 and isinstance(c, int)):
                        dve.wait_ge(conv_steps, n)
                    if shift == 0:
                        ins = dve.tensor_scalar(CV[:, c, :], CV[:, c + 1, :], w, CBIAS(c), ALU.mult, ALU.add)
                    else:
                        ins = dve.scalar_tensor_tensor(CV[:, c, shift:S], CV[:, c + 1, 0:S - shift], w,
                                                       CV[:, c, shift:S], ALU.mult, ALU.add)
                    ins.then_inc(conv_steps, 1)
                    n = n + 1

            def CBIAS(c):
                a = ROWS["conv_b_dw"][0]
                return COLS[:, bass.ds(c + a, 1)]

            def conv_pair(m, first):
                for k in range(KT):
                    dve.wait_ge(mp_loaded[k % 2], 64 * m + 16 * (k // 2 + 1))
                    if k == 0:
                        if not first:
                            dve.wait_ge(mod_mm, m)
                        ins = dve.tensor_scalar(ACC[:], MP[:, 0, :], ccol[:, 0:1], None, ALU.mult)
                    else:
                        dve.wait_ge(mp_used, KT * m + k)
                        ins = dve.scalar_tensor_tensor(ACC[:], MP[:, k % 2, :], ccol[:, k:k + 1], ACC[:], ALU.mult, ALU.add)
                    ins.then_inc(mp_used, 1)
                for half in range(2):
                    dve.wait_ge(sig_done, 2 * m + half + 1)
                    dve.tensor_tensor(CV[:, m + 1, half * HW:(half + 1) * HW], PS[:, half, :], SG[:, half, :], ALU.mult).then_inc(r1.out, 1)
                dve.wait_ge(mod_mm, m + 1)
                dve.tensor_tensor(MODC[:, bass.ds(8 * m + 16, 8)], PS[:, 4, 0:8],
                                  COLS[:, bass.ds(8 * m + 16, 8)], ALU.add).then_inc(modc_done, 1)

            conv_pair(0, True)
            with dve.Fori(1, CC) as m:
                conv_pair(m, False)
            dve.wait_ge(r1.out, 2 * CC)
            taps(0, 0, TAPS, 0)
            dve.wait_ge(conv_steps, TAPS)
            with dve.Fori(1, CC) as c:
                taps(c, 0, TAPS, TAPS * c)
            dve.wait_ge(conv_steps, TAPS * CC)

            lam = col("lru_lam", 0, 4)
            link(dve.tensor_scalar(SPT[0], lam, -1.0, None, ALU.mult))
            dve.tensor_tensor(SPT[1], lam, SPT[0], ALU.max).then_inc(lam_abs, 1)
            dve.wait_ge(lam_exp, 1)
            e, z, z2, p = SPT[2], SPT[3], SPT[4], SPT[5]
            link(dve.tensor_scalar(z, e, 2.0, None, ALU.add))
            link(dve.reciprocal(z, z))
            link(dve.tensor_tensor(z, z, e, ALU.mult))
            link(dve.tensor_tensor(z2, z, z, ALU.mult))
            link(dve.tensor_scalar(p, z2, 1.0 / 19, None, ALU.mult))
            for n in range(17, 1, -2):
                link(dve.scalar_tensor_tensor(p, p, 1.0 / n, z2, ALU.add, ALU.mult))
            link(dve.scalar_tensor_tensor(p, p, 1.0, z, ALU.add, ALU.mult))
            link(dve.tensor_scalar(z, SPT[0], 0.0, None, ALU.max))
            link(dve.scalar_tensor_tensor(p, p, 2.0, z, ALU.mult, ALU.add))
            dve.tensor_scalar(NSP8, p, -8.0, None, ALU.mult)
            link(dve.tensor_scalar(SP8, p, 8.0, None, ALU.mult))

            dve.wait_ge(mod_mm, 4)
            for c in range(CC):
                x0 = UX[:, LX + c, :]
                link(dve.tensor_scalar(XR[:], x0, LCW[:, c, 3:4], col("lru_b_conv", c), ALU.mult, ALU.add))
                for sh in range(1, LTAPS):
                    ins = dve.scalar_tensor_tensor(XR[:, sh:S], x0[:, 0:S - sh], LCW[:, c, 3 - sh:4 - sh], XR[:, sh:S], ALU.mult, ALU.add)
                    if sh < LTAPS - 1:
                        link(ins)
                    else:
                        ins.then_inc(lru_x, 1)
                        dve.wait_ge(lru_x, c + 1)
                dve.wait_ge(lru_ab, 2 * c + 2)
                link(dve.tensor_tensor(x0, RA[:], RA[:], ALU.mult))
                dve.scalar_tensor_tensor(RT[:], x0, 1.0, RT[:], ALU.add, ALU.mult).then_inc(lru_v, 1)
                link(dve.tensor_tensor(RI[:], RI[:], XR[:], ALU.mult))
                dve.wait_ge(lru_sq, c + 1)
                link(dve.tensor_tensor(RI[:], RI[:], RT[:], ALU.mult))
                link(dve.tensor_tensor_scan(XR[:], RA[:], RI[:], 0.0, ALU.mult, ALU.add))
                dve.wait_ge(lru_gelu, c + 1)
                dve.tensor_tensor(UX[:, LG + c, :], UX[:, LG + c, :], XR[:], ALU.mult).then_inc(y_lru_ready, 1)
                dve.wait_ge(y_lru_ready, c + 1)

            def over_c(ap):
                return ap.unsqueeze(1).to_broadcast([P, CC, HW])

            for half in range(2):
                cols = slice(half * HW, (half + 1) * HW)
                dve.wait_ge(ln_sum, half + 1)
                dve.scalar_tensor_tensor(CV[:, 0:CC, cols], over_c(PS[:, half, :]), -1.0 / CONV, CV[:, 0:CC, cols],
                                         ALU.mult, ALU.add).then_inc(ln_cent, 1)
            for half in range(2):
                dve.wait_ge(ln_var, half + 1)
                link(dve.tensor_scalar(RS[:, half, :], PS[:, 2 + half, :], 1.0 / CONV, EPS, ALU.mult, ALU.add))
                dve.reciprocal(RS[:, half, :], RS[:, half, :]).then_inc(ln_rec, 1)
            for half in range(2):
                cols = slice(half * HW, (half + 1) * HW)
                dve.wait_ge(ln_rstd, half + 1)
                dve.tensor_tensor(CV[:, 0:CC, cols], CV[:, 0:CC, cols], over_c(RS[:, half, :]), ALU.mult).then_inc(ln_norm, 1)

            for a in range(2):
                src = UX[:, KC_ + a, :].rearrange("p (c l) -> p l c", l=CMP_STRIDE)
                dve.wait_ge(vt_turned, 5)
                if a:
                    dve.wait_ge(cmp_mm, 1)
                dve.tensor_copy(ST[:, 0:CMP_STRIDE, 0:NCMP], src[:, :, 0:NCMP]).then_inc(st_ready, 1)
                dve.tensor_copy(ST[:, CMP_STRIDE:CMP_LEN, 0:NCMP], src[:, :, 1:NCMP + 1]).then_inc(st_ready, 1)
                dve.wait_ge(pe_turned, a + 1)
                dve.tensor_copy(ST[:, :, NCMP], PS[:, 0, 0:CMP_LEN]).then_inc(st_ready, 1)

            with dve.Fori(0, 4) as j:
                dve.wait_ge(bias_ready, 6 * j + 6)
                ch = Chain(dve, att_step, LINKS * j)

                def maxima(u):
                    qi, g = STEPS[u]
                    b, K, Kw = u % 2, P * (qi + 1), P * (min(qi, WIN // P) + 1)
                    if u >= 2:
                        dve.wait_ge(att_tg, NG * j + GEND[u - 2])
                    gate(dve, att_sc, 16 * j + u + 1)
                    flat = PS[:].rearrange("p b n -> p (b n)")
                    for n, (o, s_, bias) in enumerate((
                            (PB[:, b, 0:K], flat[:, 0:K], BS[:, g, S - K:S]),
                            (PB[:, b, S:S + Kw], flat[:, 2 * HW:2 * HW + Kw], BW[:, g, 640 - Kw:640]),
                            (PB[:, b, S + 640:S + 640 + NCMP], PS[:, 3, P:P + NCMP], BC[:, g, qi, 0:NCMP]))):
                        ins = dve.tensor_tensor_reduce(o, s_, bias, 1.0, -3e38, ALU.add, ALU.max, NM[b][:, n:n + 1])
                    ch.link(ins)
                    dve.tensor_scalar(NM[b], NM[b], -1.0, None, ALU.mult).then_inc(att_mx, 1)

                def outputs(u):
                    qi, g = STEPS[u]
                    b = u % 2
                    r = RR[b]
                    dve.wait_ge(att_ex, 48 * j + 3 * u + 3)
                    ch.link(dve.reciprocal(r, DEN[b]))
                    ch.link(dve.tensor_tensor(r, r, GT[:, qi, bass.ds(3 * j + 12 * g, 3)], ALU.mult))
                    if qi == 0:
                        ch.link(dve.tensor_tensor(r[:, 2:3], r[:, 2:3], ROWOK, ALU.mult))
                    dve.wait_ge(att_pv, 16 * j + u + 1)
                    o = OT[:, qi % 2, g * HD:(g + 1) * HD]
                    if qi >= 2:
                        dve.wait_ge(att_ot, TT * j + qi - 1)
                    ch.link(dve.tensor_scalar(o, PS[:, 6, 0:HD], r[:, 0:1], None, ALU.mult))
                    ch.link(dve.scalar_tensor_tensor(o, PS[:, 6, HD:2 * HD], r[:, 1:2], o, ALU.mult, ALU.add))
                    dve.scalar_tensor_tensor(o, PS[:, 6, 2 * HD:3 * HD], r[:, 2:3], o, ALU.mult, ALU.add).then_inc(att_oo, 1)

                maxima(0)
                for u in range(16):
                    if u < 15:
                        maxima(u + 1)
                    outputs(u)
                dve.wait_ge(att_ot, TT * j + TT)
                assert ch.n == LINKS

            for n, (a, gb) in enumerate(((16, G1B), (40, G2B))):
                if n:
                    dve.wait_ge(gb_mm, 1)
                for k in range(KT):
                    dve.tensor_scalar(DG[:, k, :], IDENT[:], MODC[:, a + k:a + k + 1], None, ALU.mult).then_inc(dg_ready, 1)
                dve.wait_ge(gb_mm, n + 1)
                dve.tensor_copy(gb[:], PS[:, 0:2, :].rearrange("p a b -> p (a b)")).then_inc(gb_ready, 1)
            dve.tensor_copy(GSH2, MODC[:, 24:32])
            link(dve.scalar_tensor_tensor(GSC2, MODC[:, 32:40], 1.0, col("norm_ffn", 0, 8), ALU.add, ALU.mult))

            def merge(m):
                ch = Chain(dve, m_step, 12 * m)
                for q in range(6):
                    nn, br, slot = q // 3, q % 3, q % 2
                    for half in range(2):
                        cols = slice(half * HW, (half + 1) * HW)
                        dst = UX[:, bass.ds(2 * m + nn, 1), cols]
                        dve.wait_ge(r2.out, 12 * m + 2 * q + half + 1)
                        dve.wait_ge(y_mm, 6 * m + q + 1)
                        o = dst if br == 0 else YT[:, half, :]
                        dve.tensor_tensor(o, GM[:, slot, cols], PS[:, 4 + 2 * slot + half, :], ALU.mult).then_inc(y_used, 1)
                        if br:
                            dve.wait_ge(y_used, 12 * m + 2 * q + half + 1)
                            ins = dve.tensor_tensor(dst, dst, YT[:, half, :], ALU.add)
                            ins.then_inc(merged, 1)
                        else:
                            dve.sem_inc(merged, 1)
                        dve.wait_ge(merged, 12 * m + 2 * q + half + 1)

            with dve.Fori(0, 4) as m:
                merge(m)

            def scale_wo(q):
                dve.wait_ge(wo_loaded[q % 2], 16 * (q // 2) + 16)
                g = G1B[:, (q // 2) * HW:(q // 2 + 1) * HW].unsqueeze(1).to_broadcast([P, 4, HW])
                dve.tensor_tensor(WOR[:, q % 2], WOR[:, q % 2], g, ALU.mult).then_inc(wo_scaled, 1)

            for k in range(KT):
                dve.wait_ge(m_hi, k + 1)
                dve.tensor_tensor(HL[:, k, :], UX[:, k, :], HH[:, k, :].bitcast(F32), ALU.subtract).then_inc(m_ready, 1)
                if k % 4 == 0:
                    q = k // 4
                    scale_wo(q)
            for q in range(4):
                if q >= 2:
                    scale_wo(q)
                dve.wait_ge(wo_hi, q + 1)
                dst = (slice(None), slice(4 * (q % 2), 4 * (q % 2) + 4), slice((q // 2) * HW, (q // 2 + 1) * HW))
                dve.tensor_tensor(WOL[dst], WOR[:, q % 2], WOH[dst].bitcast(F32), ALU.subtract).then_inc(wo_lo, 1)

            def add_out(tok):
                for nh in range(2):
                    dve.wait_ge(wo_mm, 2 * tok + nh + 1)
                    cols = slice(nh * HW, (nh + 1) * HW)
                    dve.tensor_tensor(X1[:, tok, cols], X1[:, tok, cols], PS[:, (2 * tok + nh) % 4, :], ALU.add).then_inc(x1_done, 1)

            def xhat(half):
                rstd(f2, half)
                for i in range(4):
                    if half and i == 0:
                        dve.wait_ge(f2.turned, 8)
                    dve.tensor_scalar(XN[:, i, :], X1[:, 4 * half + i, :], RSTD[:, 4 * half + i:4 * half + i + 1], None,
                                      ALU.mult).then_inc(f2.xhat, 1)

            for tok in range(TT):
                dve.wait_ge(x1_loaded[tok // 2], 16)
                add_out(tok)
                if tok == 3:
                    xhat(0)
                if tok == 5:
                    split(f2, 0, HT2)
            xhat(1)
            split(f2, 1, HT2)

            def product(m, fi, first):
                for half in range(2):
                    dve.wait_ge(f_gate, 4 * m + 2 * fi + half + 1)
                    dve.wait_ge(r3.mm, 8 * m + 4 * fi + 3 + half)
                    if not (first and fi == 0):
                        dve.wait_ge(f_lo, 2 * m + fi)
                    dve.tensor_tensor(FT[:, half, :], SA[:, half, :], PS[:, 2 + half, :], ALU.mult).then_inc(f_prod, 1)

            def add_ffn(m):
                for i in range(16):
                    tok, cols = i // 2, slice((i % 2) * HW, (i % 2 + 1) * HW)
                    dve.wait_ge(o_mm, 16 * m + i + 1)
                    dve.tensor_tensor(X1[:, tok, cols], X1[:, tok, cols], PS[:, 4 + i % 4, :], ALU.add).then_inc(o_added, 1)

            product(0, 0, True)
            product(0, 1, True)
            with dve.Fori(1, FP) as m:
                product(m, 0, False)
                add_ffn(m - 1)
                product(m, 1, False)
                dve.wait_ge(o_added, 16 * m)
            add_ffn(FP - 1)
            dve.wait_ge(fn_loaded, 16)
            for i in range(TT):
                if i % 4 == 0:
                    rstd(f3, i // 4)
                dve.scalar_tensor_tensor(X1[:, i, :], X1[:, i, :], RSTD[:, i:i + 1], FNB[:], ALU.mult, ALU.mult).then_inc(rows_ready, 1)


_INS = ["x", "c", "w_mod", "b_mod", "norm_mix", "norm_ffn", "w_in", "conv_w_dw", "conv_b_dw", "conv_ln_g",
        "conv_ln_b", "conv_w_out", "nsa_pe_k", "nsa_w_ck1", "nsa_w_ck2", "nsa_pe_v", "nsa_w_cv1", "nsa_w_cv2",
        "nsa_w_out", "lru_w_conv", "lru_b_conv", "lru_w_a", "lru_b_a", "lru_w_x", "lru_b_x", "lru_lam",
        "lru_w_out", "w_merge", "b_merge", "w_out", "w_ffn_in", "w_ffn_out", "final_norm"]
STOP = None


def kernel(**inputs):
    import concourse.bacc as _bacc
    from concourse.bass_utils import run_bass_kernel_spmd as _run

    nc = _bacc.Bacc("TRN2", target_bir_lowering=False, num_devices=1)
    arrays, aps = {}, {}
    for name in _INS:
        a = np.ascontiguousarray(inputs[name])
        arrays[f"in_{name}"] = a
        aps[name] = nc.dram_tensor(f"in_{name}", a.shape, mybir.dt.from_np(a.dtype), kind="ExternalInput").ap()
    out = nc.dram_tensor("out_0", (1, S, D), F32, kind="ExternalOutput").ap()
    build(nc, aps, out, STOP)
    r = _run(nc, [arrays], core_ids=[0])
    return r.results[0]["out_0"]
```

```python
from contextlib import ExitStack

import numpy as np
import concourse.bass as bass
from concourse import mybir

F32 = mybir.dt.float32
F32R = mybir.dt.float32r
ALU = mybir.AluOpType
ACT = mybir.ActivationFunctionType
AX = mybir.AxisListType

P = 128
S = 1024
D = 1024
KT = D // P
TT = S // P
HW = 512
EPS = 1e-6
CONV = 512
CC = CONV // P
TAPS = 31
LTAPS = 4
HD = 64
HEADS = 8
CMP_LEN, CMP_STRIDE = 32, 16
NCMP = (S - CMP_LEN) // CMP_STRIDE + 1
WIN = 512
FFN = 2816
FP = FFN // (2 * P)
NEG = -1e30
SLOPES = [2.0 ** (-8.0 * (h + 1) / HEADS) for h in range(HEADS)]

ROWS = {}
_n = 0
for _name, _len in (("b_mod", 48), ("norm_mix", 8), ("norm_ffn", 8), ("conv_b_dw", 4), ("conv_ln_g", 4),
                    ("conv_ln_b", 4), ("lru_b_conv", 4), ("lru_b_a", 4), ("lru_b_x", 4), ("lru_lam", 4),
                    ("b_merge", 24), ("c", 8)):
    ROWS[_name] = (_n, _len)
    _n += _len
NROWS = _n

LX, LG, QQ, KS_, KW_ = 0, 4, 8, 12, 13
KC_, VC_, VS_, VW_, GA_ = 0, 1, 2, 3, 4
NUX = 14
FIRST = 11
LOOPED = 4
KB = 1024


def build(nc, t, out):
    ctx = ExitStack()
    with ctx:
        base = 16512

        def at(name, shape, dt, kb):
            return nc.alloc_sbuf_tensor_at(name, shape, dt, offset=base + int(kb * KB))

        def sem(name):
            return ctx.enter_context(nc.semaphore(name))

        PS = ctx.enter_context(nc.psum_tensor("PS", [P, 8, HW], F32))

        HH = at("HH", [P, KT, S], F32R, 0)
        HL = at("HL", [P, KT, S], F32R, 32)
        CV = at("CV", [P, CC + 1, S], F32, 64)
        UX = at("UX", [P, NUX, S], F32, 84)
        WR = at("WR", [P, KT, P], F32, 158)
        WH = at("WH", [P, 2, KT, P], F32R, 162)
        WL = at("WL", [P, 2, KT, P], F32R, 170)
        X = at("X", [P, TT, D], F32, 84)
        WM = at("WM", [P, 4, 2 * D], F32, 116)
        ACC0 = at("ACC0", [P, 2 * D], F32, 196)
        HT = at("HT", [P, 2, HW], F32, 190)
        STK = at("STK", [P, 3, P], F32, 194)
        JUNK = at("JUNK", [P, D], F32, 64)
        MP = at("MP", [P, 2, D], F32, 178)
        ACC = at("ACC", [P, D], F32, 186)
        W1 = at("W1", [P, CMP_LEN, P], F32, 64)
        ST = at("ST", [P, CMP_LEN, HD], F32, 104)
        HID = at("HID", [P, 2, HD], F32, 112)
        W2 = at("W2", [P, 2, HD], F32, 112.5)
        PEROW = at("PEROW", [P, 2, P], F32, 113)
        V = at("V", [P, TT, 2, P], F32, 140)
        GT = at("GT", [P, TT, 3 * HEADS], F32, 148)
        KC = at("KC", [P, HD], F32, 148.75)
        VC = at("VC", [P, P], F32, 149)
        BC = at("BC", [P, TT, NCMP], F32, 149.5)
        BS = at("BS", [P, S], F32, 151.5)
        BW = at("BW", [P, WIN + P], F32, 155.5)
        PB = at("PB", [P, 2, 1728], F32, 178)
        QS = at("QS", [P, S], F32, 191.5)
        OT = at("OT", [P, 2, P], F32, 195.5)
        PT = at("PT", [P, 2, 4, P], F32, 196.5)
        SG = at("SG", [P, 2, HW], F32, 112)
        GM = at("GM", [P, S], F32, 80)
        WB = at("WB", [P, 2, CC, P], F32, 148)
        YT = at("YT", [P, HW], F32, 156)
        MA = at("MA", [P, 4, S], F32, 132)
        MB = at("MB", [P, 4, S], F32, 178)
        XR = at("XR", [P, S], F32, 152)
        RA = at("RA", [P, S], F32, 194)
        RI = at("RI", [P, S], F32, 198)
        SQ = at("SQ", [P, CC, HW], F32, 194)
        RS = at("RS", [P, 2, HW], F32, 152)
        DG = at("DG", [P, KT, P], F32, 152)
        G1B = at("G1B", [P, D], F32, 196)
        G2B = at("G2B", [P, D], F32, 200)
        WOR = at("WOR", [P, 2, 4, HW], F32, 116)
        WOH = [at("WOH0", [P, KT, HW], F32R, 84), at("WOH1", [P, KT, HW], F32R, 132)]
        WOL = [at("WOL0", [P, KT, HW], F32R, 100), at("WOL1", [P, KT, HW], F32R, 180)]
        X1 = at("X1", [P, TT, D], F32, 148)
        XN = at("XN", [P, 4, D], F32, 64)
        HT2 = at("HT2", [P, 2, HW], F32, 80)
        JUNK2 = at("JUNK2", [P, D], F32, 124)
        WR3 = at("WR3", [P, 2, KT, P], F32, 116)
        WH3 = at("WH3", [P, 2, KT, P], F32R, 84)
        WL3 = at("WL3", [P, 2, KT, P], F32R, 92)
        WFR = at("WFR", [P, 2, D], F32, 100)
        WFH = at("WFH", [P, 2, D], F32R, 108)
        WFL = at("WFL", [P, 2, D], F32R, 132)
        FH = at("FH", [P, 2, S], F32R, 140)
        FL = at("FL", [P, 2, S], F32R, 180)
        SA = at("SA", [P, 2, HW], F32, 188)
        FT = at("FT", [P, 2, HW], F32, 192)
        FNB = at("FNB", [P, D], F32, 64)
        CO = 204.0
        IDENT = at("IDENT", [P, P], F32, CO)
        ONES = at("ONES", [P, P], F32, CO + 0.5)
        COLS = at("COLS", [P, NROWS], F32, CO + 1.0)
        CW = at("CW", [P, CC, TAPS], F32, CO + 1.5)
        LCW = at("LCW", [P, CC, LTAPS], F32, CO + 2.0)
        MODC = at("MODC", [P, 48], F32, CO + 2.0625)
        SM = at("SM", [P, 128], F32, CO + 2.25)
        WAX = at("WAX", [P, 2, P], F32, CO + 2.78125)

        def sm(a, n):
            return SM[:, a:a + n]

        SSQ, RSTD, RTMP = sm(0, 8), sm(8, 8), sm(16, 8)
        GSC, GSH = sm(24, 8), sm(32, 8)
        SPT = [sm(40 + 4 * i, 4) for i in range(6)]
        SP8, NSP8 = sm(64, 4), sm(68, 4)
        ROWOK = sm(72, 1)
        CB = sm(73, 4)
        SLOPE, NSLOPE, QSC = sm(77, 2), sm(98, 2), sm(79, 1)
        NM = [sm(80, 3), sm(83, 3)]
        DEN = [sm(86, 3), sm(89, 3)]
        RR = [sm(92, 3), sm(95, 3)]
        GSC2, GSH2 = sm(100, 8), sm(108, 8)

        def col(name, i=0, n=1):
            a = ROWS[name][0] + i
            return COLS[:, a:a + n]

        const_zero, const_set, table_made, wax_loaded = sem("const_zero"), sem("const_set"), sem("table_made"), sem("wax_loaded")
        stack_loaded, stack_t, cols_ready = sem("stack_loaded"), sem("stack_t"), sem("cols_ready")
        x_loaded = [sem(f"x_loaded{i}") for i in range(4)]
        wm_loaded = [sem(f"wm_loaded{i}") for i in range(4)]
        wm_used, acc0_ready, mod0_mm, mod_ready = sem("wm_used"), sem("acc0_ready"), sem("mod0_mm"), sem("mod_ready")
        dve_step, act_step = sem("dve_step"), sem("act_step")

        class FormSems:

            def __init__(s, n):
                s.square, s.recip, s.rstd = sem(n + "_square"), sem(n + "_recip"), sem(n + "_rstd")
                s.xhat, s.turned, s.plain = sem(n + "_xhat"), sem(n + "_turned"), sem(n + "_plain")
                s.hi, s.ready = sem(n + "_hi"), sem(n + "_ready")

        f1, f2, f3 = FormSems("h1"), FormSems("h2"), FormSems("final")

        class RingSems:

            def __init__(s, n):
                s.loaded = [sem(n + "_loaded0"), sem(n + "_loaded1")]
                s.hi, s.lo, s.mm, s.out = sem(n + "_hi"), sem(n + "_lo"), sem(n + "_mm"), sem(n + "_out")

        r1, r3 = RingSems("in"), RingSems("ffn")
        mp_loaded = [sem("mp_loaded0"), sem("mp_loaded1")]
        mp_used, mod_mm, modc_done = sem("mp_used"), sem("mod_mm"), sem("modc_done")
        vt_turned, v_ready = sem("vt_turned"), sem("v_ready")
        w1_loaded, w2_loaded = [sem("w1_loaded_k"), sem("w1_loaded_v")], sem("w2_loaded")
        pe_turned, st_ready, cmp_mm, hid_ready, cmp2_mm, kvc_ready = (
            sem("cmp_" + n) for n in ("pe_turned", "st", "mm", "hid", "mm2", "ready"))
        att_q, att_qsc, att_sc, att_mx, att_ex, att_tg, att_ev, att_pg, att_oo = (
            sem("att_" + n) for n in ("q", "qsc", "sc", "mx", "ex", "tg", "ev", "pg", "oo"))
        att_step, gated, glu_done, conv_steps = sem("att_step"), sem("gated"), sem("glu_done"), sem("conv_steps")
        lam_abs, lam_exp = sem("lam_abs"), sem("lam_exp")
        lru_x, lru_r, lru_rr, lru_i, lru_ab, lru_v, lru_sq, lru_gelu, y_lru_ready = (
            sem("lru_" + n) for n in ("x", "r", "rr", "i", "ab", "v", "sq", "gelu", "y"))
        ln_sum, ln_cent, ln_sq, ln_var, ln_rec, ln_rstd, ln_norm, y_conv_ready = (
            sem("ln_" + n) for n in ("sum", "cent", "sq", "var", "rec", "rstd", "norm", "y"))
        wb_loaded = [sem("wb_loaded0"), sem("wb_loaded1")]
        y_mm, y_used, sum_done, lru_step = sem("y_mm"), sem("y_used"), sem("sum_done"), sem("lru_step")
        dg_ready, gb_mm, gb_ready = sem("dg_ready"), sem("gb_mm"), sem("gb_ready")
        m_hi, m_ready = sem("m_hi"), sem("m_ready")
        wo_loaded = [sem("wo_loaded0"), sem("wo_loaded1")]
        wo_scaled, wo_hi, wo_lo, wo_mm, x1_done = (sem("wo_" + n) for n in ("scaled", "hi", "lo", "mm", "x1"))
        x1_loaded = [sem(f"x1_loaded{i}") for i in range(4)]
        wf_loaded, wf_scaled, wf_hi, wf_lo = (sem("wf_" + n) for n in ("loaded", "scaled", "hi", "lo"))
        f_gate, f_prod, f_hi, f_lo = (sem("f_" + n) for n in ("gate", "prod", "hi", "lo"))
        o_mm, o_added = sem("o_mm"), sem("o_added")
        fn_loaded, rows_ready, out_stored = sem("fn_loaded"), sem("rows_ready"), sem("out_stored")

        def products(pe, bank, w, wl, slot, half, r, a=0, e=3 * KT):
            for n in range(a, e):
                wt, h = ((w, HH), (w, HL), (wl, HH))[n // KT]
                k = n % KT
                last = pe.matmul(PS[:, bank, :], wt[:, slot, k, :], h[:, k, half * HW:(half + 1) * HW],
                                 start=(n == 0), stop=(n == 3 * KT - 1))
            if e == 3 * KT:
                last.then_inc(r.mm, 1)

        def gate(eng, s, value):
            eng.wait_ge(s, value)
            eng.sem_inc(gated, 1)

        class Chain:

            def __init__(c, eng, s, base=0):
                c.eng, c.s, c.base, c.n = eng, s, base, 0

            def link(c, ins):
                c.n += 1
                ins.then_inc(c.s, 1)
                c.eng.wait_ge(c.s, c.base + c.n)

        STEPS = [(qi, g) for qi in reversed(range(TT)) for g in range(2)]
        NST = len(STEPS)

        def tiles(qi):
            lo = max(0, qi - WIN // P)
            return [(0, k, P * k) for k in range(qi + 1)] + \
                   [(1, k, S + P * (k - lo)) for k in range(lo, qi + 1)] + [(2, 0, S + WIN + P)]

        NGR = [-(-len(tiles(qi)) // 4) for qi, g in STEPS]
        GI, TI, OI = [], [], {}
        ng = nt = 0
        for u in range(NST):
            GI.append(list(range(ng, ng + NGR[u])))
            TI.append(list(range(nt, nt + NGR[u])))
            ng, nt = ng + NGR[u], nt + NGR[u]
            if u % 2 == 0 and u:
                OI[u - 1] = nt
                nt += 1
        OI[NST - 1] = nt
        nt += 1
        assert ng % 2 == 0 and nt % 2 == 0
        BESIDE = [(1 + u // 2, 12 * (u % 2), 12 * (u % 2) + 12) for u in range(12)] + [(7, 6 * v, 6 * v + 6) for v in range(4)]
        ENDS = {u: h for u, (h, a, e) in enumerate(BESIDE) if e == 3 * KT}
        LINKS = 5 * NST + 2 + 2
        TAPS_AT = {u: n for u, n in zip(range(7, NST), (4, 4, 4, 4, 3, 3, 3, 3, 3))}
        assert sum(TAPS_AT.values()) == TAPS
        for h in range(HEADS):
            assert SLOPES[h] == 2.0 ** round(np.log2(SLOPES[h]))

        w_in = t["w_in"][0].rearrange("(k p) n -> p k n", p=P)
        w_mod = t["w_mod"][0].rearrange("(k p) n -> k p n", p=P)
        x_t = t["x"][0].rearrange("(t p) d -> p t d", p=P)
        KV = 2 * CONV + HEADS * HD
        LCOL = KV + 6 * P + 3 * HEADS
        CHUNKS = [(KV, KC_), (KV + P, VC_), (KV + 3 * P, VS_), (KV + 5 * P, VW_), (KV + 6 * P, GA_), (KV + 2 * P, KS_),
                  (KV + 4 * P, KW_)] + [(None, QQ + j) for j in range(4)]
        LANDS = [16 * (i + 1) + 16 * max(0, i - 6) for i in range(FIRST)]
        EXTRA = 16 * 4

        block = ctx.enter_context(nc.Block())

        @block.sync
        def _(sp):
            for name, (a, n) in ROWS.items():
                src = t[name] if name == "c" else t[name][0:1, :]
                sp.dma_start(STK[a:a + n, 0, :], src.rearrange("a (r p) -> (a r) p", p=P)).then_inc(stack_loaded, 16)
            for c in range(CC):
                sp.dma_start(STK[TAPS * c:TAPS * (c + 1), 1, :], t["conv_w_dw"][0, :, c * P:(c + 1) * P]).then_inc(stack_loaded, 16)
                sp.dma_start(STK[LTAPS * c:LTAPS * (c + 1), 2, :], t["lru_w_conv"][0, :, c * P:(c + 1) * P]).then_inc(stack_loaded, 16)
            for i in range(4):
                sp.dma_start(X[:, 2 * i:2 * i + 2, :], x_t[:, 2 * i:2 * i + 2, :]).then_inc(x_loaded[i], 16)
            for k in range(KT):
                if k >= 4:
                    sp.wait_ge(wm_used, k - 3)
                sp.dma_start(WM[:, k % 4, :], w_mod[k, :, 0:2 * D]).then_inc(wm_loaded[k % 4], 16)

            def load_first(i):
                c0, u = CHUNKS[i]
                if i:
                    sp.wait_ge(r1.lo, i)
                if c0 is None:
                    for g in range(2):
                        a = 2 * CONV + g * 4 * HD + (u - QQ) * HD
                        sp.dma_start(WR[:, :, g * HD:(g + 1) * HD], w_in[:, :, a:a + HD]).then_inc(r1.loaded[0], 16)
                else:
                    sp.dma_start(WR[:], w_in[:, :, c0:c0 + P]).then_inc(r1.loaded[0], 16)

            def load_mod(m):
                for k in range(KT):
                    if m or k >= 2:
                        sp.wait_ge(mp_used, KT * m + k - 1)
                    sp.dma_start(MP[:, k % 2, :], w_mod[k, :, (m + 2) * D:(m + 3) * D]).then_inc(mp_loaded[k % 2], 16)

            def load_w1(a):
                for g in range(2):
                    sp.dma_start(W1[g * HD:(g + 1) * HD, :, :],
                                 t[f"nsa_w_c{'kv'[a]}1"][0].rearrange("(l d) n -> d l n", d=HD)).then_inc(w1_loaded[a], 16)

            for i in range(FIRST):
                load_first(i)
                if i % 2 and i < 8:
                    load_mod(i // 2)
                if i == 3:
                    sp.wait_ge(f1.square, TT)
                    load_w1(0)
                    sp.wait_ge(f1.turned, 16)
                    for a, kv in enumerate("kv"):
                        sp.dma_start(W2[:, a, :], t[f"nsa_w_c{kv}2"][0]).then_inc(w2_loaded, 16)
                        for g in range(2):
                            sp.dma_start(PEROW[0:CMP_LEN, a, g * HD:(g + 1) * HD], t[f"nsa_pe_{kv}"][0]).then_inc(w2_loaded, 16)
                if i == 8:
                    sp.wait_ge(cmp_mm, 1)
                    load_w1(1)

            with sp.Fori(0, 4) as j:
                for q, c0 in enumerate((0, CONV, LCOL, LCOL + CONV)):
                    sp.wait_ge(r1.lo, LOOPED * j + FIRST + q)
                    sp.dma_start(WR[:], w_in[:, :, bass.ds(j * P + c0, P)]).then_inc(r1.loaded[0], 16)

            wm = t["w_merge"][0].rearrange("(k p) n -> p k n", p=P)
            wy = [None] + [t[n][0].rearrange("(k p) n -> p k n", p=P) for n in ("lru_w_out", "conv_w_out")]
            wg = t["nsa_w_out"][0].rearrange("(g j d) n -> g d j n", g=2, d=HD)

            def load_gate_chunk(br, c, s_):
                gate(sp, r1.lo, 2 * c + (8 * br + s_ + 27))
                sp.dma_start(WR[:], wm[:, :, bass.ds(c * P + (s_ * 4 * P + (1, 2, 0)[br] * D), P)]).then_inc(r1.loaded[0], 16)

            def load_output_chunk(br, c, s_, first=False):
                if not first:
                    gate(sp, y_mm, 2 * c + (8 * br + s_ - 1))
                cols = bass.ds(c * P + s_ * 4 * P, P)
                if br == 0:
                    for g in range(2):
                        sp.dma_start(WB[g * HD:(g + 1) * HD, s_], wg[g, :, :, cols]).then_inc(wb_loaded[s_], 16)
                else:
                    sp.dma_start(WB[:, s_], wy[br][:, :, cols]).then_inc(wb_loaded[s_], 16)

            def load_merge(br, c):
                for s_ in range(2):
                    load_gate_chunk(br, c, s_)
                    load_output_chunk(br, c, s_)

            def load_wax(c, first=False):
                if first:
                    sp.wait_ge(const_zero, 2)
                else:
                    sp.wait_ge(lru_i, c)
                for a, w in enumerate((t["lru_w_a"], t["lru_w_x"])):
                    for i in range(2):
                        src = w[0, bass.ds(2 * c + i, 1)].rearrange("a i j -> (a i) j")
                        sp.dma_start(WAX[i * HD:(i + 1) * HD, a, i * HD:(i + 1) * HD], src).then_inc(wax_loaded, 16)

            load_wax(0, True)
            load_gate_chunk(0, 0, 0)
            load_gate_chunk(0, 0, 1)
            sp.wait_ge(att_ev, 4 * nt)
            load_output_chunk(0, 0, 0, True)
            load_output_chunk(0, 0, 1, True)
            with sp.Fori(1, 4) as c:
                load_gate_chunk(0, c, 0)
                load_wax(c)
                load_output_chunk(0, c, 0)
                load_gate_chunk(0, c, 1)
                load_output_chunk(0, c, 1)
            with sp.Fori(0, 4) as c:
                load_merge(1, c)
            wo = t["w_out"][0].rearrange("(k p) n -> p k n", p=P)

            def load_wo(q):
                sp.dma_start(WOR[:, q % 2], wo[:, 4 * (q % 2):4 * (q % 2) + 4, (q // 2) * HW:(q // 2 + 1) * HW]).then_inc(wo_loaded[q % 2], 16)

            sp.wait_ge(y_mm, 8)
            load_wo(0)
            load_wo(1)
            with sp.Fori(0, 4) as c:
                load_merge(2, c)
            for q in (2, 3):
                sp.wait_ge(wo_lo, q - 1)
                load_wo(q)
            sp.wait_ge(m_ready, KT)
            for i in range(4):
                sp.dma_start(X1[:, 2 * i:2 * i + 2, :], x_t[:, 2 * i:2 * i + 2, :]).then_inc(x1_loaded[i], 16)
            wfi = t["w_ffn_in"][0].rearrange("(k p) n -> p k n", p=P)
            wfo = t["w_ffn_out"][0].rearrange("(m f p) n -> m p f n", f=2, p=P)
            sp.wait_ge(wo_lo, 4)

            def load_ffn(m, first):
                for q in range(4):
                    if not (first and q < 2):
                        gate(sp, r3.lo, 4 * m + q - 1)
                    sp.dma_start(WR3[:, q % 2], wfi[:, :, bass.ds((2 * m + q // 2) * P + (q % 2) * FFN, P)]).then_inc(r3.loaded[q % 2], 16)
                    if q == 1:
                        if first:
                            sp.wait_ge(wo_mm, TT)
                        else:
                            sp.wait_ge(wf_lo, m)
                        sp.dma_start(WFR[:], wfo[bass.ds(m, 1), :, :, :].rearrange("a p f n -> p (a f) n")).then_inc(wf_loaded, 16)

            load_ffn(0, True)
            with sp.Fori(1, FP) as m:
                load_ffn(m, False)
            sp.wait_ge(f2.turned, 16)
            sp.dma_start(FNB[:], t["final_norm"].partition_broadcast(P)).then_inc(fn_loaded, 16)
            o_t = out[0].rearrange("(t p) d -> p t d", p=P)
            for i in range(4):
                sp.wait_ge(rows_ready, 2 * i + 2)
                sp.dma_start(o_t[:, 2 * i:2 * i + 2, :], X1[:, 2 * i:2 * i + 2, :]).then_inc(out_stored, 16)
            sp.wait_ge(out_stored, 64)

        @block.gpsimd
        def _(pool):
            pool.memset(IDENT[:], 0.0).then_inc(const_zero, 1)
            pool.memset(WAX[:], 0.0).then_inc(const_zero, 1)
            pool.memset(ONES[:], 1.0).then_inc(const_set, 1)
            pool.memset(ROWOK, 1.0).then_inc(const_set, 1)
            for g in range(2):
                pool.memset(SLOPE[:, g:g + 1], SLOPES[4 * g]).then_inc(const_set, 1)
                pool.memset(NSLOPE[:, g:g + 1], -SLOPES[4 * g]).then_inc(const_set, 1)
            for g in range(2):
                pool.wait_ge(const_set, 6 + g)
                pool.memset(QSC[g * HD:(g + 1) * HD, :], HD ** -0.5 / SLOPES[4 * g]).then_inc(const_set, 1)
            pool.wait_ge(const_set, 8)
            pool.wait_ge(const_zero, 2)
            pool.affine_select(out=IDENT[:], in_=IDENT[:], compare_op=ALU.not_equal, fill=1.0, base=0,
                               pattern=[[-1, P]], channel_multiplier=1).then_inc(const_set, 1)
            pool.wait_ge(const_set, 9)
            pool.affine_select(out=ROWOK, in_=ROWOK, compare_op=ALU.is_ge, fill=0.0, base=-(CMP_LEN - 1),
                               pattern=[[0, 1]], channel_multiplier=1).then_inc(const_set, 1)
            for o, pat, b in ((BS[:], [[1, S]], -(S - P)), (BW[:], [[1, WIN + P]], -WIN),
                              (BC[:], [[-P, TT], [CMP_STRIDE, NCMP]], CMP_LEN - 1)):
                pool.iota(o, pat, base=b, channel_multiplier=-1, allow_small_or_imprecise_dtypes=True).then_inc(table_made, 1)
            pool.wait_ge(table_made, 3)
            for o, pat, b in ((BS[:], [[-1, S]], S - P), (BW[:], [[-1, WIN + P]], WIN),
                              (BC[:], [[P, TT], [-CMP_STRIDE, NCMP]], -(CMP_LEN - 1))):
                pool.affine_select(out=o, in_=o, compare_op=ALU.is_ge, fill=NEG, base=b, pattern=pat,
                                   channel_multiplier=1).then_inc(table_made, 1)
            pool.wait_ge(table_made, 6)
            pool.affine_select(out=BW[:], in_=BW[:], compare_op=ALU.is_ge, fill=NEG, base=-1,
                               pattern=[[1, WIN + P]], channel_multiplier=-1).then_inc(table_made, 1)

            def lo(i, slot):
                pool.wait_ge(r1.hi, i + 1)
                pool.tensor_tensor(WL[:, slot], WR[:], WH[:, slot].bitcast(F32), ALU.subtract).then_inc(r1.lo, 1)

            with pool.Fori(0, 25) as m:
                lo(2 * m, 0)
                lo(2 * m + 1, 1)
            lo(50, 0)

            def lo3(i, slot):
                pool.wait_ge(r3.hi, i + 1)
                pool.tensor_tensor(WL3[:, slot], WR3[:, slot], WH3[:, slot].bitcast(F32), ALU.subtract).then_inc(r3.lo, 1)

            def scale(m):
                pool.wait_ge(wf_loaded, 16 * m + 16)
                pool.tensor_tensor(WFR[:], WFR[:], G2B[:].unsqueeze(1).to_broadcast([P, 2, D]), ALU.mult).then_inc(wf_scaled, 1)

            lo3(0, 0)
            lo3(1, 1)
            pool.wait_ge(gb_ready, 2)
            scale(0)

            def ffn(m, last):
                for fi in range(2):
                    if not (last and fi):
                        lo3(4 * m + 2 * fi + 2, 0)
                        lo3(4 * m + 2 * fi + 3, 1)
                    pool.wait_ge(f_hi, 2 * m + fi + 1)
                    pool.tensor_tensor(FL[:, fi, :], FT[:].rearrange("p a b -> p (a b)"), FH[:, fi, :].bitcast(F32),
                                       ALU.subtract).then_inc(f_lo, 1)
                    if fi == 0:
                        pool.wait_ge(wf_hi, m + 1)
                        pool.tensor_tensor(WFL[:], WFR[:], WFH[:].bitcast(F32), ALU.subtract).then_inc(wf_lo, 1)
                    elif not last:
                        scale(m + 1)

            with pool.Fori(0, FP - 1) as m:
                ffn(m, False)
            ffn(FP - 1, True)

        @block.scalar
        def _(act):
            def stats(src, f, half, junk, waits):
                for i in range(4 * half, 4 * half + 4):
                    waits(i)
                    if i:
                        act.wait_ge(f.square, i)
                    act.activation(junk[:], src[:, i, :], ACT.Square, accum_out=SSQ[:, i:i + 1]).then_inc(f.square, 1)
                act.wait_ge(f.recip, half + 1)
                act.activation(RSTD[:, 4 * half:4 * half + 4], RTMP[:, 4 * half:4 * half + 4], ACT.Sqrt).then_inc(f.rstd, 1)

            def form(f, half, scale, shift, ht):
                for b in range(8 * half, 8 * half + 8):
                    k = b % KT
                    act.wait_ge(f.turned, b + 1)
                    if b >= 2:
                        act.wait_ge(f.ready, b - 1)
                    act.activation(ht[:, b % 2, :], PS[:, 4 + b % 4, :], ACT.Identity,
                                   bias=shift[:, k:k + 1], scale=scale[:, k:k + 1]).then_inc(f.plain, 1)

            for half in range(2):
                stats(X, f1, half, JUNK, lambda i: act.wait_ge(x_loaded[i // 2], 16))
            act.wait_ge(mod_ready, 2)
            for half in range(2):
                form(f1, half, GSC, GSH, HT)

            def hi(i, slot, loaded):
                act.wait_ge(r1.loaded[0], loaded)
                act.activation(WH[:, slot], WR[:], ACT.Copy).then_inc(r1.hi, 1)

            def put(i, dst, bank, func=ACT.Copy):
                for half in range(2):
                    act.wait_ge(r1.mm, 2 * i + 1 + half)
                    act.activation(dst[:, half * HW:(half + 1) * HW], PS[:, bank + half, :], func).then_inc(r1.out, 1)

            hi(0, 0, LANDS[0])
            hi(1, 1, LANDS[1])
            ch = Chain(act, act_step)

            def hidden(a):
                act.wait_ge(cmp_mm, a + 1)
                ch.link(act.activation(CB[:, 2 * a:2 * a + 2], PS[:, 6:8, HD - 1], ACT.Copy))
                if a:
                    act.wait_ge(cmp2_mm, 1)
                for g in range(2):
                    act.activation(HID[:, g, 0:NCMP], PS[:, 6 + g, 0:NCMP], ACT.Gelu_apprx_tanh,
                                   bias=CB[:, 2 * a + g:2 * a + g + 1]).then_inc(hid_ready, 1)

            for i in range(FIRST):
                put(i, UX[:, CHUNKS[i][1], :], 2 * (i % 2))
                hi(i + 2, i % 2, LANDS[i + 2] if i + 2 < FIRST else 16 * (i + 3) + EXTRA)
                if i == 5:
                    for b in range(4):
                        act.wait_ge(vt_turned, b + 1)
                        act.activation(V[:, 4 * (b % 2):4 * (b % 2) + 4, b // 2, :], PS[:, 4 + b, :].rearrange("p (t f) -> p t f", t=4),
                                       ACT.Copy).then_inc(v_ready, 1)
                    act.wait_ge(vt_turned, 5)
                    logits = PS[:, 4, 0:TT * 3 * HEADS].rearrange("p (a b) -> p a b", b=3)
                    gates = GT[:].rearrange("p t (h b) -> p (t h) b", b=3)
                    act.activation(gates[:, :, 0:2], logits[:, :, 1:3], ACT.Sigmoid).then_inc(v_ready, 1)
                    act.activation(gates[:, :, 2:3], logits[:, :, 0:1], ACT.Sigmoid).then_inc(v_ready, 1)
                    hidden(0)
                if i == 6:
                    act.wait_ge(cmp2_mm, 1)
                    act.activation(KC[:, 0:NCMP], PS[:, 5, 0:NCMP], ACT.Copy).then_inc(kvc_ready, 1)
                if i == 9:
                    hidden(1)
            act.wait_ge(cmp2_mm, 2)
            act.activation(VC[0:NCMP, :], PS[0:NCMP, 5, 0:P], ACT.Copy).then_inc(kvc_ready, 1)

            act.wait_ge(r1.out, 2 * FIRST)
            act.wait_ge(const_set, 10)
            act.activation(QS[:], UX[:, QQ, :], ACT.Copy, scale=QSC).then_inc(att_q, 1)
            act.wait_ge(att_q, 1)
            with act.Fori(0, 4) as j:
                def exps(u):
                    qi, g = STEPS[u]
                    b, K, Kw = u % 2, P * (qi + 1), P * (min(qi, WIN // P) + 1)
                    act.wait_ge(att_mx, NST * j + u + 1)
                    for n, (a, e) in enumerate(((0, K), (S, S + Kw), (S + WIN + P, S + WIN + P + NCMP))):
                        act.activation(PB[:, b, a:e], PB[:, b, a:e], ACT.Exp, bias=NM[b][:, n:n + 1], scale=SLOPE[:, g:g + 1],
                                       accum_out=DEN[b][:, n:n + 1]).then_inc(att_ex, 1)

                def evac(u):
                    qi, g = STEPS[u]
                    n = len(tiles(qi))
                    for k in range(NGR[u]):
                        m = min(4, n - 4 * k)
                        if GI[u][k] >= 2:
                            act.wait_ge(att_pg, ng * j + GI[u][k] - 1)
                        act.wait_ge(att_tg, nt * j + TI[u][k] + 1)
                        act.activation(PT[:, GI[u][k] % 2, 0:m, :], PS[:, 4 + TI[u][k] % 2, 0:m * P].rearrange("p (a b) -> p a b", b=P),
                                       ACT.Copy).then_inc(att_ev, 1)

                def put_o(u):
                    qi = STEPS[u][0]
                    gate(act, att_tg, nt * j + OI[u] + 1)
                    act.activation(UX[:, bass.ds(j + QQ, 1), qi * P:(qi + 1) * P], PS[:, 4 + OI[u] % 2, 0:P], ACT.Copy).then_inc(att_ev, 1)

                def put_half(h):
                    q, half = h // 2, h % 2
                    if q == 1 and half == 0:
                        act.wait_ge(glu_done, 2 * j + 1)
                    if q == 3 and half == 0:
                        act.wait_ge(glu_done, 2 * j + 3)
                    cols = slice(half * HW, (half + 1) * HW)
                    dst = (CV[:, bass.ds(j + 1, 1), cols], SG[:, half, :], UX[:, bass.ds(j + LX, 1), cols], UX[:, bass.ds(j + LG, 1), cols])[q]
                    gate(act, r1.mm, 8 * j + (2 * FIRST + h + 1))
                    act.activation(dst, PS[:, 7, :], ACT.Sigmoid if q == 1 else ACT.Copy).then_inc(r1.out, 1)
                    if half:
                        hi(None, (FIRST + q) % 2, 64 * j + (16 * (FIRST + q + 3) + EXTRA))

                put_half(0)
                exps(0)
                for u in range(NST):
                    if u and u - 1 in ENDS:
                        put_half(ENDS[u - 1])
                    evac(u)
                    if u - 1 in OI:
                        put_o(u - 1)
                    if u < NST - 1:
                        exps(u + 1)
                put_half(7)
                put_o(NST - 1)
                act.activation(QSC, QSC, ACT.Copy, scale=SLOPES[0] / SLOPES[1]).then_inc(att_qsc, 1)
                act.wait_ge(att_sc, NST * j + NST)
                gate(act, att_qsc, j + 1)
                act.activation(QS[:], UX[:, bass.ds(j + QQ + 1, 1), :], ACT.Copy, scale=QSC).then_inc(att_q, 1)
                act.wait_ge(att_q, j + 2)

            def sig(br, c, s_, first=False):
                e = 2 * c + (8 * br + s_)
                name_at = (1, 2, 0)[br] * KT + 4 * s_ + ROWS["b_merge"][0]
                bias = COLS[:, bass.ds(c + name_at, 1)]
                for half in range(2):
                    if not first:
                        act.wait_ge(y_used, 2 * e + half - 1)
                    gate(act, r1.mm, 2 * e + (54 + half + 1))
                    act.activation(GM[:, half * HW:(half + 1) * HW], PS[:, 2 * ((27 + s_) % 2) + half, :], ACT.Sigmoid,
                                   bias=bias).then_inc(r1.out, 1)
                if not (br == 2 and isinstance(c, int) and c == 3):
                    hi(None, (27 + s_) % 2, 16 * e + (16 * 30 + EXTRA))

            act.wait_ge(lam_abs, 1)
            act.activation(SPT[2], SPT[1], ACT.Exp, scale=-1.0).then_inc(lam_exp, 1)

            def lru(c, first=False):
                sig(0, c, 0, first)
                gate(act, lru_r, c + 1)
                ba, bx = ROWS["lru_b_a"][0], ROWS["lru_b_x"][0]
                act.activation(RA[:], PS[:, 6:8, :], ACT.Sigmoid, bias=COLS[:, bass.ds(c + ba, 1)]).then_inc(lru_rr, 1)
                gate(act, lru_i, c + 1)
                act.activation(RI[:], PS[:, 6:8, :], ACT.Sigmoid, bias=COLS[:, bass.ds(c + bx, 1)]).then_inc(lru_ab, 1)
                x0 = UX[:, bass.ds(c + LX, 1), :]
                act.activation(x0, RA[:], ACT.Tanh, scale=SP8[:, bass.ds(c, 1)]).then_inc(lru_ab, 1)
                gate(act, lru_ab, 3 * c + 2)
                act.activation(RA[:], RA[:], ACT.Exp, scale=NSP8[:, bass.ds(c, 1)]).then_inc(lru_ab, 1)
                lg = UX[:, bass.ds(c + LG, 1), :]
                act.activation(lg, lg, ACT.Gelu_apprx_tanh).then_inc(lru_gelu, 1)
                gate(act, lru_v, c + 1)
                act.activation(x0, x0, ACT.Sqrt).then_inc(lru_sq, 1)
                sig(0, c, 1)

            act.wait_ge(lru_x, 1)
            lru(0, True)
            with act.Fori(1, 4) as c:
                lru(c)

            sig(1, 0, 0)
            for half in range(2):
                cols = slice(half * HW, (half + 1) * HW)
                act.wait_ge(ln_cent, half + 1)
                if half:
                    act.wait_ge(ln_var, 1)
                act.activation(SQ[:], CV[:, 0:CC, cols], ACT.Square).then_inc(ln_sq, 1)
            sig(1, 0, 1)
            for half in range(2):
                act.wait_ge(ln_rec, half + 1)
                act.activation(RS[:, half, :], RS[:, half, :], ACT.Sqrt).then_inc(ln_rstd, 1)
            with act.Fori(1, 4) as c:
                sig(1, c, 0)
                sig(1, c, 1)
            for c in range(CC):
                act.wait_ge(ln_norm, 2)
                act.activation(CV[:, c, :], CV[:, c, :], ACT.Silu, bias=col("conv_ln_b", c),
                               scale=col("conv_ln_g", c)).then_inc(y_conv_ready, 1)

            def wo_hi_part(q):
                act.wait_ge(wo_scaled, q + 1)
                act.activation(WOH[q // 2][:, 4 * (q % 2):4 * (q % 2) + 4, :], WOR[:, q % 2], ACT.Copy).then_inc(wo_hi, 1)

            sig(2, 0, 0)
            sig(2, 0, 1)
            wo_hi_part(0)
            wo_hi_part(1)
            with act.Fori(1, 3) as c:
                sig(2, c, 0)
                sig(2, c, 1)
            for s_ in range(2):
                sig(2, 3, s_)

            act.wait_ge(y_mm, 24)
            act.wait_ge(sum_done, 32)
            for k in range(KT):
                m = (MA, MB)[k // 4][:, k % 4, :]
                act.activation(HH[:, k, :], m, ACT.Copy).then_inc(m_hi, 1)
            act.wait_ge(m_ready, KT)
            wo_hi_part(2)
            wo_hi_part(3)

            def ffn_hi(slot, loaded, mm=None):
                act.wait_ge(r3.loaded[slot], loaded)
                if mm is not None:
                    act.wait_ge(r3.mm, mm)
                act.activation(WH3[:, slot], WR3[:, slot], ACT.Copy).then_inc(r3.hi, 1)

            for half in range(2):
                stats(X1, f2, half, JUNK2, lambda i: act.wait_ge(x1_done, TT + i + 1))
                form(f2, half, GSC2, GSH2, HT2)
                if half == 0:
                    ffn_hi(0, 16)
                    ffn_hi(1, 16)

            def ffn(m, first, last):
                for fi in range(2):
                    for half in range(2):
                        act.wait_ge(r3.mm, 8 * m + 4 * fi + half + 1)
                        if not (first and fi == 0):
                            act.wait_ge(f_prod, 4 * m + 2 * fi - 1 + half)
                        act.activation(SA[:, half, :], PS[:, half, :], ACT.Silu).then_inc(f_gate, 1)
                    if not (last and fi):
                        ffn_hi(0, 32 * m + 16 * fi + 32)
                        ffn_hi(1, 32 * m + 16 * fi + 32, 8 * m + 4 * fi + 4)
                    act.wait_ge(f_prod, 4 * m + 2 * fi + 2)
                    if not first:
                        act.wait_ge(o_mm, 16 * m)
                    act.activation(FH[:, fi, :], FT[:].rearrange("p a b -> p (a b)"), ACT.Copy).then_inc(f_hi, 1)
                    if fi == 0:
                        act.wait_ge(wf_scaled, m + 1)
                        act.activation(WFH[:], WFR[:], ACT.Copy).then_inc(wf_hi, 1)

            ffn(0, True, False)
            with act.Fori(1, FP - 1) as m:
                ffn(m, False, False)
            ffn(FP - 1, False, True)
            for half in range(2):
                stats(X1, f3, half, JUNK2, lambda i: act.wait_ge(o_added, 16 * (FP - 1) + 2 * i + 2))

        @block.tensor
        def _(pe):
            pe.wait_ge(stack_loaded, 16 * (len(ROWS) + 2 * CC))
            pe.wait_ge(const_set, 9)
            pe.transpose(PS[:, 0, 0:NROWS], STK[0:NROWS, 0, :], IDENT[0:NROWS, 0:NROWS])
            pe.transpose(PS[:, 1, 0:CC * TAPS], STK[0:CC * TAPS, 1, :], IDENT[0:CC * TAPS, 0:CC * TAPS])
            pe.transpose(PS[:, 2, 0:CC * LTAPS], STK[0:CC * LTAPS, 2, :], IDENT[0:CC * LTAPS, 0:CC * LTAPS]).then_inc(stack_t, 1)

            def turn(src, f, half, at0, blocks=range(KT)):
                pe.wait_ge(f.xhat, 4 * half + 4)
                for b in (8 * half + k for k in blocks):
                    k = b % KT
                    if b >= 4:
                        pe.wait_ge(f.plain, b - 3)
                    for i in range(4):
                        last = pe.transpose(PS[:, 4 + b % 4, i * P:(i + 1) * P], src[:, at0 + i, k * P:(k + 1) * P], IDENT[:])
                    last.then_inc(f.turned, 1)

            pe.wait_ge(acc0_ready, 1)
            for j in range(16):
                last = pe.matmul(PS[:, 3, j:j + 1], ACC0[:, j * P:(j + 1) * P], ONES[:, 0:1], start=True, stop=True)
            last.then_inc(mod0_mm, 1)
            turn(X, f1, 0, 0)
            turn(X, f1, 1, 4)
            pe.wait_ge(f1.ready, 16)
            pe.wait_ge(cols_ready, 1)

            def compress_in(a):
                pe.wait_ge(w2_loaded, 16 * 6)
                pe.wait_ge(v_ready, 4)
                if a:
                    pe.wait_ge(kvc_ready, 1)
                    pe.wait_ge(hid_ready, 2)
                pe.transpose(PS[:, 5, 0:CMP_LEN], PEROW[0:CMP_LEN, a, :], IDENT[0:CMP_LEN, 0:CMP_LEN]).then_inc(pe_turned, 1)
                pe.wait_ge(w1_loaded[a], 32)
                pe.wait_ge(st_ready, 3 * a + 3)
                for g in range(2):
                    rows = slice(g * HD, (g + 1) * HD)
                    for l in range(CMP_LEN):
                        last = pe.matmul(PS[:, 6 + g, 0:HD], W1[rows, l, :], ST[rows, l, :], start=(l == 0), stop=(l == CMP_LEN - 1))
                last.then_inc(cmp_mm, 1)

            def compress_out(a):
                pe.wait_ge(hid_ready, 2 * a + 2)
                for g in range(2):
                    if a == 0:
                        last = pe.matmul(PS[g * HD:(g + 1) * HD, 5, 0:NCMP], W2[:, 0, :], HID[:, g, 0:NCMP], start=True, stop=True)
                    else:
                        last = pe.matmul(PS[0:NCMP, 5, g * HD:(g + 1) * HD], HID[:, g, 0:NCMP], W2[:, 1, :], start=True, stop=True)
                last.then_inc(cmp2_mm, 1)

            for i in range(FIRST):
                pe.wait_ge(r1.lo, i + 1)
                if i >= 2:
                    pe.wait_ge(r1.out, 2 * (i - 1))
                for half in range(2):
                    products(pe, 2 * (i % 2) + half, WH, WL, i % 2, half, r1)
                if i % 2 and i < 8:
                    m = i // 2
                    pe.wait_ge(mp_used, KT * (m + 1))
                    if m == 3:
                        pe.wait_ge(v_ready, 6)
                    for k in range(KT):
                        last = pe.matmul(PS[:, 4, k:k + 1], ACC[:, k * P:(k + 1) * P], ONES[:, 0:1], start=True, stop=True)
                    last.then_inc(mod_mm, 1)
                if i == 5:
                    pe.wait_ge(r1.out, 10)
                    pe.wait_ge(modc_done, 3)
                    for b in range(4):
                        for k in range(4):
                            tok = 4 * (b % 2) + k
                            last = pe.transpose(PS[:, 4 + b, k * P:(k + 1) * P], UX[:, VS_ + b // 2, tok * P:(tok + 1) * P], IDENT[:])
                        last.then_inc(vt_turned, 1)
                    n = 3 * HEADS
                    pe.wait_ge(v_ready, 1)
                    for tok in range(TT):
                        last = pe.transpose(PS[:, 4, tok * n:(tok + 1) * n], UX[0:n, GA_, tok * P:(tok + 1) * P], IDENT[0:n, 0:n])
                    last.then_inc(vt_turned, 1)
                    compress_in(0)
                if i == 6:
                    compress_out(0)
                if i == 9:
                    compress_in(1)
            compress_out(1)

            pe.wait_ge(kvc_ready, 2)
            pe.wait_ge(r1.out, 2 * FIRST)
            pe.wait_ge(modc_done, 4)
            pe.wait_ge(table_made, 7)
            with pe.Fori(0, 4) as j:
                def scores(u):
                    qi, g = STEPS[u]
                    rows = slice(g * HD, (g + 1) * HD)
                    q = QS[rows, qi * P:(qi + 1) * P]
                    K, Kw = P * (qi + 1), P * (min(qi, WIN // P) + 1)
                    if u:
                        pe.wait_ge(att_mx, NST * j + u)
                    for b, (a, e) in enumerate(((0, min(K, HW)), (HW, K))):
                        if e > a:
                            pe.matmul(PS[:, b, 0:e - a], q, UX[rows, KS_, a:e], start=True, stop=True)
                    for b, (a, e) in enumerate(((K - Kw, K - Kw + min(Kw, HW)), (K - Kw + HW, K))):
                        if e > a:
                            pe.matmul(PS[:, 2 + b, 0:e - a], q, UX[rows, KW_, a:e], start=True, stop=True)
                    pe.matmul(PS[:, 3, P:P + NCMP], q, KC[rows, 0:NCMP], start=True, stop=True).then_inc(att_sc, 1)

                def beside(h, a, e):
                    q, half = h // 2, h % 2
                    if a == 0:
                        pe.wait_ge(r1.out, 8 * j + (2 * FIRST + h))
                        pe.wait_ge(r1.lo, LOOPED * j + (FIRST + q + 1))
                    products(pe, 7, WH, WL, (FIRST + q) % 2, half, r1, a, e)

                def turn_p(u, k):
                    qi, g = STEPS[u]
                    if TI[u][k] >= 2:
                        gate(pe, att_ev, nt * j + TI[u][k] - 1)
                    for i, (br, kt, a) in enumerate(tiles(qi)[4 * k:4 * k + 4]):
                        m = NCMP if br == 2 else P
                        last = pe.transpose(PS[0:m, 4 + TI[u][k] % 2, i * P:(i + 1) * P], PB[:, u % 2, a:a + m], IDENT[:])
                    last.then_inc(att_tg, 1)

                def turn_o(u):
                    pe.wait_ge(att_ev, nt * j + OI[u] - 1)
                    pe.wait_ge(att_oo, NST * j + u + 1)
                    pe.transpose(PS[:, 4 + OI[u] % 2, 0:P], OT[:, STEPS[u][0] % 2, :], IDENT[:]).then_inc(att_tg, 1)

                def pv(u, k):
                    qi, g = STEPS[u]
                    pe.wait_ge(att_ev, nt * j + TI[u][k] + 1)
                    if u and k == 0:
                        pe.wait_ge(att_oo, NST * j + u)
                    ts = tiles(qi)
                    for n in range(4 * k, min(4 * k + 4, len(ts))):
                        br, kt, a = ts[n]
                        m = NCMP if br == 2 else P
                        v = VC[0:m, g * HD:(g + 1) * HD] if br == 2 else V[:, kt, br, g * HD:(g + 1) * HD]
                        last = pe.matmul(PS[:, 6, br * HD:(br + 1) * HD], PT[0:m, GI[u][k] % 2, n - 4 * k, :], v,
                                         start=(n == 0 or ts[n - 1][0] != br), stop=(n + 1 == len(ts) or ts[n + 1][0] != br))
                    last.then_inc(att_pg, 1)

                pe.wait_ge(att_q, j + 1)
                scores(0)
                beside(0, 0, 3 * KT)
                for u in range(NST):
                    h, a, e = BESIDE[u]
                    mid = (a + e) // 2
                    if u < NST - 1:
                        scores(u + 1)
                    beside(h, a, mid)
                    pe.wait_ge(att_ex, 3 * NST * j + 3 * u + 3)
                    turn_p(u, 0)
                    if NGR[u] > 1:
                        turn_p(u, 1)
                    beside(h, mid, e)
                    for k in range(NGR[u]):
                        pv(u, k)
                        if k + 2 < NGR[u]:
                            turn_p(u, k + 2)
                    if u - 1 in OI:
                        turn_o(u - 1)
                turn_o(NST - 1)
                pe.wait_ge(att_mx, NST * j + NST)
                pe.wait_ge(att_ev, nt * j + nt)
                pe.wait_ge(att_oo, NST * j + NST)

            Y = [[UX[:, QQ + k, :] for k in range(CC)], [UX[:, LG + k, :] for k in range(CC)], [CV[:, k, :] for k in range(CC)]]

            def merge(br, c, s_, between=None, first=False):
                e = 2 * c + (8 * br + s_)
                slot = (27 + s_) % 2
                pe.wait_ge(r1.lo, e + 28)
                pe.wait_ge(r1.out, 2 * e + 52)
                for half in range(2):
                    products(pe, 2 * slot + half, WH, WL, slot, half, r1)
                if between:
                    between()
                pe.wait_ge(wb_loaded[s_], (32 * c + 32, 16 * c + 144, 16 * c + 208)[br])
                if not first:
                    pe.wait_ge(y_used, 2 * e)
                for half in range(2):
                    for k in range(CC):
                        last = pe.matmul(PS[:, 4 + half, :], WB[:, s_, k, :], Y[br][k][:, half * HW:(half + 1) * HW],
                                         start=(k == 0), stop=(k == CC - 1))
                last.then_inc(y_mm, 1)

            def lru_products(a, c):
                for half in range(2):
                    last = pe.matmul(PS[:, 6 + half, :], WAX[:, a, :], XR[:, half * HW:(half + 1) * HW], start=True, stop=True)
                last.then_inc((lru_r, lru_i)[a], 1)

            def lru(c, first=False):
                def r_part():
                    pe.wait_ge(wax_loaded, 64 * c + 64)
                    pe.wait_ge(lru_x, c + 1)
                    if not first:
                        pe.wait_ge(lru_ab, 3 * c)
                    lru_products(0, c)

                merge(0, c, 0, r_part, first)
                pe.wait_ge(lru_rr, c + 1)
                lru_products(1, c)
                merge(0, c, 1)

            lru(0, True)
            with pe.Fori(1, 4) as c:
                lru(c)

            def ln_sums():
                pe.wait_ge(lru_ab, 12)
                for half in range(2):
                    for c in range(CC):
                        last = pe.matmul(PS[:, 6 + half, :], ONES[:], CV[:, c, half * HW:(half + 1) * HW], start=(c == 0), stop=(c == CC - 1))
                    last.then_inc(ln_sum, 1)

            def ln_vars(half):
                pe.wait_ge(ln_sq, half + 1)
                for c in range(CC):
                    last = pe.matmul(PS[:, 6 + half, :], ONES[:], SQ[:, c, :], start=(c == 0), stop=(c == CC - 1))
                last.then_inc(ln_var, 1)

            pe.wait_ge(y_lru_ready, CC)
            merge(1, 0, 0, ln_sums)
            ln_vars(0)
            merge(1, 0, 1)
            ln_vars(1)
            with pe.Fori(1, 4) as c:
                merge(1, c, 0)
                merge(1, c, 1)
            for n in range(2):
                pe.wait_ge(ln_rec, 2)
                pe.wait_ge(dg_ready, 8 * n + 8)
                if n:
                    pe.wait_ge(gb_ready, 1)
                for b in range(2):
                    last = pe.matmul(PS[:, 6 + b, :], ONES[:], DG[:, 4 * b:4 * b + 4, :].rearrange("p a b -> p (a b)"), start=True, stop=True)
                last.then_inc(gb_mm, 1)
            pe.wait_ge(y_conv_ready, CC)
            with pe.Fori(0, 4) as c:
                merge(2, c, 0)
                merge(2, c, 1)

            pe.wait_ge(m_ready, KT)
            pe.wait_ge(r1.out, 102)
            pe.wait_ge(gb_ready, 2)
            for nh in range(2):
                pe.wait_ge(wo_lo, 2 * nh + 2)
                for tok in range(TT):
                    rows = slice(tok * P, (tok + 1) * P)
                    i = TT * nh + tok
                    if i >= 4:
                        pe.wait_ge(x1_done, i - 3)
                    n = 0
                    for h, w in ((HH, WOH[nh]), (HH, WOL[nh]), (HL, WOH[nh])):
                        for k in range(KT):
                            last = pe.matmul(PS[:, i % 4, :], h[:, k, rows], w[:, k, :], start=(n == 0), stop=(n == 3 * KT - 1))
                            n += 1
                    last.then_inc(wo_mm, 1)
                    if i == TT + 6:
                        turn(XN, f2, 0, 0, range(4))
            turn(XN, f2, 0, 0, range(4, KT))
            turn(XN, f2, 1, 0)
            pe.wait_ge(f2.ready, 16)
            pe.wait_ge(x1_done, 16)

            def out_mm(m):
                pe.wait_ge(f_lo, 2 * m + 2)
                pe.wait_ge(wf_lo, m + 1)
                for tok in range(TT):
                    rows = slice(tok * P, (tok + 1) * P)
                    for nh in range(2):
                        i = 2 * tok + nh
                        if i >= 4:
                            pe.wait_ge(o_added, 16 * m + i - 3)
                        n = 0
                        for h, w in ((FH, WFH), (FH, WFL), (FL, WFH)):
                            for fi in range(2):
                                last = pe.matmul(PS[:, 4 + i % 4, :], h[:, fi, rows], w[:, fi, nh * HW:(nh + 1) * HW],
                                                 start=(n == 0), stop=(n == 5))
                                n += 1
                        last.then_inc(o_mm, 1)

            def ffn(m, first):
                for q in range(4):
                    pe.wait_ge(r3.lo, 4 * m + q + 1)
                    if not (first and q < 2):
                        pe.wait_ge(f_prod, 4 * m + 2 * (q // 2))
                    for half in range(2):
                        products(pe, 2 * (q % 2) + half, WH3, WL3, q % 2, half, r3)
                    if q == 1 and not first:
                        out_mm(m - 1)
                        pe.wait_ge(o_added, 16 * m)

            ffn(0, True)
            with pe.Fori(1, FP) as m:
                ffn(m, False)
            out_mm(FP - 1)

        @block.vector
        def _(dve):
            main = Chain(dve, dve_step)
            link = main.link

            dve.wait_ge(stack_t, 1)
            dve.tensor_copy(COLS[:], PS[:, 0, 0:NROWS])
            dve.tensor_copy(CW[:], PS[:, 1, 0:CC * TAPS].rearrange("p (c t) -> p c t", c=CC))
            link(dve.tensor_copy(LCW[:], PS[:, 2, 0:CC * LTAPS].rearrange("p (c t) -> p c t", c=CC)))
            dve.sem_inc(cols_ready, 1)
            ccol = col("c", 0, 8)

            def mod0(k):
                dve.wait_ge(wm_loaded[k % 4], 16 * (k // 4 + 1))
                if k == 0:
                    ins = dve.tensor_scalar(ACC0[:], WM[:, 0, :], ccol[:, 0:1], None, ALU.mult)
                else:
                    dve.wait_ge(wm_used, k)
                    ins = dve.scalar_tensor_tensor(ACC0[:], WM[:, k % 4, :], ccol[:, k:k + 1], ACC0[:], ALU.mult, ALU.add)
                ins.then_inc(wm_used, 1)

            def rstd(f, half):
                a = slice(4 * half, 4 * half + 4)
                dve.wait_ge(f.square, 4 * half + 4)
                link(dve.tensor_scalar(RTMP[:, a], SSQ[:, a], 1.0 / D, EPS, ALU.mult, ALU.add))
                dve.reciprocal(RTMP[:, a], RTMP[:, a]).then_inc(f.recip, 1)
                dve.wait_ge(f.rstd, half + 1)

            def split(f, half0, ht):
                for b in range(8 * half0, 8 * half0 + 8):
                    half, k = b // KT, b % KT
                    cols = slice(half * HW, (half + 1) * HW)
                    dve.wait_ge(f.plain, b + 1)
                    dve.tensor_copy(HH[:, k, cols], ht[:, b % 2, :]).then_inc(f.hi, 1)
                    dve.wait_ge(f.hi, b + 1)
                    dve.tensor_tensor(HL[:, k, cols], ht[:, b % 2, :], HH[:, k, cols].bitcast(F32), ALU.subtract).then_inc(f.ready, 1)

            mod0(0)
            for i in range(TT):
                if i % 4 == 0:
                    mod0(1 + i // 4)
                    rstd(f1, i // 4)
                dve.tensor_scalar(X[:, i, :], X[:, i, :], RSTD[:, i:i + 1], None, ALU.mult).then_inc(f1.xhat, 1)
            for k in range(3, KT):
                mod0(k)
            dve.wait_ge(wm_used, KT)
            dve.sem_inc(acc0_ready, 1)
            dve.wait_ge(mod0_mm, 1)
            link(dve.tensor_tensor(MODC[:, 0:16], PS[:, 3, 0:16], col("b_mod", 0, 16), ALU.add))
            dve.tensor_copy(GSH, MODC[:, 0:8]).then_inc(mod_ready, 1)
            dve.scalar_tensor_tensor(GSC, MODC[:, 8:16], 1.0, col("norm_mix", 0, 8), ALU.add, ALU.mult).then_inc(mod_ready, 1)
            split(f1, 0, HT)
            split(f1, 1, HT)

            def mod(m):
                for k in range(KT):
                    dve.wait_ge(mp_loaded[k % 2], 64 * m + 16 * (k // 2 + 1))
                    if k == 0:
                        if m:
                            dve.wait_ge(mod_mm, m)
                        ins = dve.tensor_scalar(ACC[:], MP[:, 0, :], ccol[:, 0:1], None, ALU.mult)
                    else:
                        dve.wait_ge(mp_used, KT * m + k)
                        ins = dve.scalar_tensor_tensor(ACC[:], MP[:, k % 2, :], ccol[:, k:k + 1], ACC[:], ALU.mult, ALU.add)
                    ins.then_inc(mp_used, 1)

            def modc(m):
                dve.wait_ge(mod_mm, m + 1)
                dve.tensor_tensor(MODC[:, 8 * m + 16:8 * m + 24], PS[:, 4, 0:8], col("b_mod", 8 * m + 16, 8), ALU.add).then_inc(modc_done, 1)

            def stage(a):
                src = UX[:, KC_ + a, :].rearrange("p (c l) -> p l c", l=CMP_STRIDE)
                dve.wait_ge(r1.out, 2 * a + 2)
                if a:
                    dve.wait_ge(cmp_mm, 1)
                dve.tensor_copy(ST[:, 0:CMP_STRIDE, 0:NCMP], src[:, :, 0:NCMP]).then_inc(st_ready, 1)
                dve.tensor_copy(ST[:, CMP_STRIDE:CMP_LEN, 0:NCMP], src[:, :, 1:NCMP + 1]).then_inc(st_ready, 1)
                dve.wait_ge(pe_turned, a + 1)
                dve.tensor_copy(ST[:, :, NCMP], PS[:, 5, 0:CMP_LEN]).then_inc(st_ready, 1)

            for m in range(3):
                mod(m)
                modc(m)
            stage(0)
            mod(3)
            modc(3)
            lam = col("lru_lam", 0, 4)
            link(dve.tensor_scalar(SPT[0], lam, -1.0, None, ALU.mult))
            dve.tensor_tensor(SPT[1], lam, SPT[0], ALU.max).then_inc(lam_abs, 1)
            stage(1)

            dve.sem_inc(glu_done, 1)
            dve.wait_ge(table_made, 7)
            with dve.Fori(0, 4) as j:
                ch = Chain(dve, att_step, LINKS * j)

                def maxima(u):
                    qi, g = STEPS[u]
                    b, K, Kw = u % 2, P * (qi + 1), P * (min(qi, WIN // P) + 1)
                    if u >= 2:
                        dve.wait_ge(att_tg, nt * j + TI[u - 2][-1] + 1)
                    gate(dve, att_sc, NST * j + u + 1)
                    flat = PS[:].rearrange("p b n -> p (b n)")
                    for n, (o, s_, bias) in enumerate((
                            (PB[:, b, 0:K], flat[:, 0:K], BS[:, S - K:S]),
                            (PB[:, b, S:S + Kw], flat[:, 2 * HW:2 * HW + Kw], BW[:, WIN + P - Kw:WIN + P]),
                            (PB[:, b, S + WIN + P:S + WIN + P + NCMP], PS[:, 3, P:P + NCMP], BC[:, qi, :]))):
                        ins = dve.tensor_tensor_reduce(o, s_, bias, 1.0, -3e38, ALU.add, ALU.max, NM[b][:, n:n + 1])
                    ch.link(ins)
                    dve.tensor_scalar(NM[b], NM[b], NSLOPE[:, g:g + 1], None, ALU.mult).then_inc(att_mx, 1)

                def outputs(u):
                    qi, g = STEPS[u]
                    r = RR[u % 2]
                    dve.wait_ge(att_ex, 3 * NST * j + 3 * u + 3)
                    ch.link(dve.reciprocal(r, DEN[u % 2]))
                    ch.link(dve.tensor_tensor(r, r, GT[:, qi, bass.ds(3 * j + 12 * g, 3)], ALU.mult))
                    if qi == 0:
                        ch.link(dve.tensor_tensor(r[:, 2:3], r[:, 2:3], ROWOK, ALU.mult))
                    dve.wait_ge(att_pg, ng * j + GI[u][-1] + 1)
                    if g == 0 and u >= 4:
                        dve.wait_ge(att_tg, nt * j + OI[u - 3] + 1)
                    o = OT[:, qi % 2, g * HD:(g + 1) * HD]
                    ch.link(dve.tensor_scalar(o, PS[:, 6, 0:HD], r[:, 0:1], None, ALU.mult))
                    ch.link(dve.scalar_tensor_tensor(o, PS[:, 6, HD:2 * HD], r[:, 1:2], o, ALU.mult, ALU.add))
                    dve.scalar_tensor_tensor(o, PS[:, 6, 2 * HD:3 * HD], r[:, 2:3], o, ALU.mult, ALU.add).then_inc(att_oo, 1)

                def glu():
                    for half in range(2):
                        v = CV[:, bass.ds(j + 1, 1), half * HW:(half + 1) * HW]
                        dve.wait_ge(r1.out, 8 * j + (2 * FIRST + 3 + half))
                        dve.tensor_tensor(v, v, SG[:, half, :].unsqueeze(1), ALU.mult).then_inc(glu_done, 1)
                    dve.wait_ge(glu_done, 2 * j + 3)

                def taps(a, e):
                    cb = ROWS["conv_b_dw"][0]
                    for shift in range(a, e):
                        w = CW[:, bass.ds(j, 1), TAPS - 1 - shift].rearrange("p a -> p a")
                        res, src = CV[:, bass.ds(j, 1), shift:S], CV[:, bass.ds(j + 1, 1), 0:S - shift]
                        if shift == 0:
                            ins = dve.tensor_scalar(res, src, w, COLS[:, bass.ds(j + cb, 1)], ALU.mult, ALU.add)
                        else:
                            dve.wait_ge(conv_steps, TAPS * j + shift)
                            ins = dve.scalar_tensor_tensor(res, src, w, res, ALU.mult, ALU.add)
                        ins.then_inc(conv_steps, 1)

                maxima(0)
                done = 0
                for u in range(NST):
                    if u < NST - 1:
                        maxima(u + 1)
                    if u == 6:
                        glu()
                    if u in TAPS_AT:
                        taps(done, done + TAPS_AT[u])
                        done += TAPS_AT[u]
                    outputs(u)
                dve.wait_ge(conv_steps, TAPS * j + TAPS)
                ch.link(dve.tensor_scalar(SLOPE, SLOPE, SLOPES[1] / SLOPES[0], None, ALU.mult))
                ch.link(dve.tensor_scalar(NSLOPE, NSLOPE, SLOPES[1] / SLOPES[0], None, ALU.mult))
                assert ch.n == LINKS

            dve.wait_ge(lam_exp, 1)
            e, z, z2, p = SPT[2], SPT[3], SPT[4], SPT[5]
            link(dve.tensor_scalar(z, e, 2.0, None, ALU.add))
            link(dve.reciprocal(z, z))
            link(dve.tensor_tensor(z, z, e, ALU.mult))
            link(dve.tensor_tensor(z2, z, z, ALU.mult))
            link(dve.tensor_scalar(p, z2, 1.0 / 19, None, ALU.mult))
            for n in range(17, 1, -2):
                link(dve.scalar_tensor_tensor(p, p, 1.0 / n, z2, ALU.add, ALU.mult))
            link(dve.scalar_tensor_tensor(p, p, 1.0, z, ALU.add, ALU.mult))
            link(dve.tensor_scalar(z, SPT[0], 0.0, None, ALU.max))
            link(dve.scalar_tensor_tensor(p, p, 2.0, z, ALU.mult, ALU.add))
            dve.tensor_scalar(NSP8, p, -8.0, None, ALU.mult)
            link(dve.tensor_scalar(SP8, p, 8.0, None, ALU.mult))

            def add_branch(br, c, s_):
                e = 2 * c + (8 * br + s_)
                for half in range(2):
                    cols = slice(half * HW, (half + 1) * HW)
                    dst = (MA, MB)[s_][:, bass.ds(c, 1), cols]
                    ps = PS[:, 4 + half:5 + half, :]
                    dve.wait_ge(r1.out, 2 * e + (54 + half + 1))
                    dve.wait_ge(y_mm, e + 1)
                    if br == 0:
                        dve.tensor_tensor(dst, GM[:, cols].unsqueeze(1), ps, ALU.mult).then_inc(y_used, 1)
                    else:
                        dve.tensor_tensor(YT[:].unsqueeze(1), GM[:, cols].unsqueeze(1), ps, ALU.mult).then_inc(y_used, 1)
                        dve.wait_ge(y_used, 2 * e + half + 1)
                        ins = dve.tensor_tensor(dst, dst, YT[:].unsqueeze(1), ALU.add)
                        ins.then_inc(sum_done, 1)
                        dve.wait_ge(sum_done, 2 * e + (half + 1 - 16))

            N_LRU = 8

            def lru(c):
                ch = Chain(dve, lru_step, N_LRU * c)
                x0 = UX[:, bass.ds(c + LX, 1), :]
                xr, ri, ra = XR[:].unsqueeze(1), RI[:].unsqueeze(1), RA[:].unsqueeze(1)
                lb = ROWS["lru_b_conv"][0]

                def w(n):
                    return LCW[:, bass.ds(c, 1), n].rearrange("p a -> p a")

                ch.link(dve.tensor_scalar(xr, x0, w(3), COLS[:, bass.ds(c + lb, 1)], ALU.mult, ALU.add))
                for sh in range(1, LTAPS):
                    ins = dve.scalar_tensor_tensor(xr[:, :, sh:S], x0[:, :, 0:S - sh], w(3 - sh), xr[:, :, sh:S], ALU.mult, ALU.add)
                    if sh < LTAPS - 1:
                        ch.link(ins)
                    else:
                        ins.then_inc(lru_x, 1)
                        dve.wait_ge(lru_x, c + 1)
                add_branch(0, c, 0)
                dve.wait_ge(lru_ab, 3 * c + 3)
                ch.link(dve.tensor_tensor(RI[:], RI[:], XR[:], ALU.mult))
                ch.link(dve.tensor_tensor(XR[:], RA[:], RA[:], ALU.mult))
                dve.scalar_tensor_tensor(x0, xr, 1.0, x0, ALU.add, ALU.mult).then_inc(lru_v, 1)
                dve.wait_ge(lru_sq, c + 1)
                ch.link(dve.tensor_tensor(ri, ri, x0, ALU.mult))
                ch.link(dve.tensor_tensor_scan(XR[:], RA[:], RI[:], 0.0, ALU.mult, ALU.add))
                lg = UX[:, bass.ds(c + LG, 1), :]
                dve.wait_ge(lru_gelu, c + 1)
                ch.link(dve.tensor_tensor(lg, lg, xr, ALU.mult))
                dve.sem_inc(y_lru_ready, 1)
                add_branch(0, c, 1)
                assert ch.n == N_LRU

            with dve.Fori(0, 4) as c:
                lru(c)

            def over_c(ap):
                return ap.unsqueeze(1).to_broadcast([P, CC, HW])

            for half in range(2):
                cols = slice(half * HW, (half + 1) * HW)
                dve.wait_ge(ln_sum, half + 1)
                dve.scalar_tensor_tensor(CV[:, 0:CC, cols], over_c(PS[:, 6 + half, :]), -1.0 / CONV, CV[:, 0:CC, cols],
                                         ALU.mult, ALU.add).then_inc(ln_cent, 1)
            add_branch(1, 0, 0)
            add_branch(1, 0, 1)
            for half in range(2):
                dve.wait_ge(ln_var, half + 1)
                link(dve.tensor_scalar(RS[:, half, :], PS[:, 6 + half, :], 1.0 / CONV, EPS, ALU.mult, ALU.add))
                dve.reciprocal(RS[:, half, :], RS[:, half, :]).then_inc(ln_rec, 1)
            for half in range(2):
                cols = slice(half * HW, (half + 1) * HW)
                dve.wait_ge(ln_rstd, half + 1)
                dve.tensor_tensor(CV[:, 0:CC, cols], CV[:, 0:CC, cols], over_c(RS[:, half, :]), ALU.mult).then_inc(ln_norm, 1)
            with dve.Fori(1, 4) as c:
                add_branch(1, c, 0)
                add_branch(1, c, 1)

            dve.wait_ge(ln_norm, 2)
            for n, (a, gb) in enumerate(((16, G1B), (40, G2B))):
                if n:
                    dve.wait_ge(gb_mm, 1)
                for k in range(KT):
                    dve.tensor_scalar(DG[:, k, :], IDENT[:], MODC[:, a + k:a + k + 1], None, ALU.mult).then_inc(dg_ready, 1)
                dve.wait_ge(gb_mm, n + 1)
                dve.tensor_copy(gb[:], PS[:, 6:8, :].rearrange("p a b -> p (a b)")).then_inc(gb_ready, 1)
            dve.tensor_copy(GSH2, MODC[:, 24:32])
            link(dve.scalar_tensor_tensor(GSC2, MODC[:, 32:40], 1.0, col("norm_ffn", 0, 8), ALU.add, ALU.mult))

            def scale_wo(q):
                dve.wait_ge(wo_loaded[q % 2], 16 * (q // 2) + 16)
                g = G1B[:, (q // 2) * HW:(q // 2 + 1) * HW].unsqueeze(1).to_broadcast([P, 4, HW])
                dve.tensor_tensor(WOR[:, q % 2], WOR[:, q % 2], g, ALU.mult).then_inc(wo_scaled, 1)

            def lo_wo(q):
                dve.wait_ge(wo_hi, q + 1)
                ks = slice(4 * (q % 2), 4 * (q % 2) + 4)
                dve.tensor_tensor(WOL[q // 2][:, ks, :], WOR[:, q % 2], WOH[q // 2][:, ks, :].bitcast(F32), ALU.subtract).then_inc(wo_lo, 1)

            dve.wait_ge(gb_ready, 1)
            scale_wo(0)
            scale_wo(1)
            add_branch(2, 0, 0)
            add_branch(2, 0, 1)
            lo_wo(0)
            lo_wo(1)
            with dve.Fori(1, 4) as c:
                add_branch(2, c, 0)
                add_branch(2, c, 1)

            for k in range(KT):
                dve.wait_ge(m_hi, k + 1)
                dve.tensor_tensor(HL[:, k, :], (MA, MB)[k // 4][:, k % 4, :], HH[:, k, :].bitcast(F32), ALU.subtract).then_inc(m_ready, 1)
            for q in (2, 3):
                scale_wo(q)
            for q in (2, 3):
                lo_wo(q)

            def add_out(i):
                tok, cols = i % TT, slice((i // TT) * HW, (i // TT + 1) * HW)
                dve.wait_ge(wo_mm, i + 1)
                dve.wait_ge(x1_loaded[tok // 2], 16)
                dve.tensor_tensor(X1[:, tok, cols], X1[:, tok, cols], PS[:, i % 4, :], ALU.add).then_inc(x1_done, 1)

            def xhat(half):
                rstd(f2, half)
                for i in range(4):
                    if half and i == 0:
                        dve.wait_ge(f2.turned, 8)
                    dve.tensor_scalar(XN[:, i, :], X1[:, 4 * half + i, :], RSTD[:, 4 * half + i:4 * half + i + 1], None,
                                      ALU.mult).then_inc(f2.xhat, 1)

            for i in range(2 * TT):
                add_out(i)
                if i == TT + 4:
                    xhat(0)
            split(f2, 0, HT2)
            xhat(1)
            split(f2, 1, HT2)

            def product(m, fi, first):
                for half in range(2):
                    dve.wait_ge(f_gate, 4 * m + 2 * fi + half + 1)
                    dve.wait_ge(r3.mm, 8 * m + 4 * fi + 3 + half)
                    if not (first and fi == 0):
                        dve.wait_ge(f_lo, 2 * m + fi)
                    dve.tensor_tensor(FT[:, half, :], SA[:, half, :], PS[:, 2 + half, :], ALU.mult).then_inc(f_prod, 1)

            def add_ffn(m):
                for i in range(16):
                    tok, cols = i // 2, slice((i % 2) * HW, (i % 2 + 1) * HW)
                    dve.wait_ge(o_mm, 16 * m + i + 1)
                    dve.tensor_tensor(X1[:, tok, cols], X1[:, tok, cols], PS[:, 4 + i % 4, :], ALU.add).then_inc(o_added, 1)

            product(0, 0, True)
            product(0, 1, True)
            with dve.Fori(1, FP) as m:
                product(m, 0, False)
                add_ffn(m - 1)
                product(m, 1, False)
                dve.wait_ge(o_added, 16 * m)
            add_ffn(FP - 1)
            dve.wait_ge(fn_loaded, 16)
            for i in range(TT):
                if i % 4 == 0:
                    rstd(f3, i // 4)
                dve.scalar_tensor_tensor(X1[:, i, :], X1[:, i, :], RSTD[:, i:i + 1], FNB[:], ALU.mult, ALU.mult).then_inc(rows_ready, 1)


_INS = ["x", "c", "w_mod", "b_mod", "norm_mix", "norm_ffn", "w_in", "conv_w_dw", "conv_b_dw", "conv_ln_g",
        "conv_ln_b", "conv_w_out", "nsa_pe_k", "nsa_w_ck1", "nsa_w_ck2", "nsa_pe_v", "nsa_w_cv1", "nsa_w_cv2",
        "nsa_w_out", "lru_w_conv", "lru_b_conv", "lru_w_a", "lru_b_a", "lru_w_x", "lru_b_x", "lru_lam",
        "lru_w_out", "w_merge", "b_merge", "w_out", "w_ffn_in", "w_ffn_out", "final_norm"]


def kernel(**inputs):
    import concourse.bacc as _bacc
    from concourse.bass_utils import run_bass_kernel_spmd as _run

    nc = _bacc.Bacc("TRN2", target_bir_lowering=False, num_devices=1)
    arrays, aps = {}, {}
    for name in _INS:
        a = np.ascontiguousarray(inputs[name])
        arrays[f"in_{name}"] = a
        aps[name] = nc.dram_tensor(f"in_{name}", a.shape, mybir.dt.from_np(a.dtype), kind="ExternalInput").ap()
    out = nc.dram_tensor("out_0", (1, S, D), F32, kind="ExternalOutput").ap()
    build(nc, aps, out)
    r = _run(nc, [arrays], core_ids=[0])
    return r.results[0]["out_0"]
```

```python
from contextlib import ExitStack

import numpy as np
import concourse.bass as bass
from concourse import mybir

F32 = mybir.dt.float32
F32R = mybir.dt.float32r
ALU = mybir.AluOpType
ACT = mybir.ActivationFunctionType
AX = mybir.AxisListType

P = 128
S = 1024
D = 1024
KT = D // P
TT = S // P
HW = 512
EPS = 1e-6
CONV = 512
CC = CONV // P
TAPS = 31
LTAPS = 4
HD = 64
HEADS = 8
CMP_LEN, CMP_STRIDE = 32, 16
NCMP = (S - CMP_LEN) // CMP_STRIDE + 1
WIN = 512
FFN = 2816
FP = FFN // (2 * P)
NEG = -1e30
SLOPES = [2.0 ** (-8.0 * (h + 1) / HEADS) for h in range(HEADS)]

ROWS = {}
_n = 0
for _name, _len in (("b_mod", 48), ("norm_mix", 8), ("norm_ffn", 8), ("conv_b_dw", 4), ("conv_ln_g", 4),
                    ("conv_ln_b", 4), ("lru_b_conv", 4), ("lru_b_a", 4), ("lru_b_x", 4), ("lru_lam", 4),
                    ("b_merge", 24), ("c", 8)):
    ROWS[_name] = (_n, _len)
    _n += _len
NROWS = _n

LX, LG, QQ, KS_, KW_ = 0, 4, 8, 12, 13
KC_, VC_, VS_, VW_, GA_ = 0, 1, 2, 3, 4
NUX = 14
FIRST = 11
LOOPED = 4
KB = 1024


def build(nc, t, out):
    ctx = ExitStack()
    with ctx:
        base = 16512

        def at(name, shape, dt, kb):
            return nc.alloc_sbuf_tensor_at(name, shape, dt, offset=base + int(kb * KB))

        def sem(name):
            return ctx.enter_context(nc.semaphore(name))

        PS = ctx.enter_context(nc.psum_tensor("PS", [P, 8, HW], F32))

        HH = at("HH", [P, KT, S], F32R, 0)
        HL = at("HL", [P, KT, S], F32R, 32)
        CV = at("CV", [P, CC + 1, S], F32, 64)
        UX = at("UX", [P, NUX, S], F32, 84)
        WR = at("WR", [P, KT, P], F32, 158)
        WH = at("WH", [P, 2, KT, P], F32R, 162)
        WL = at("WL", [P, 2, KT, P], F32R, 170)
        X = at("X", [P, TT, D], F32, 84)
        WM = at("WM", [P, KT, D], F32, 116)
        ACC0 = at("ACC0", [P, 2 * D], F32, 196)
        HT = at("HT", [P, 2, HW], F32, 190)
        STK = at("STK", [P, 4, P], F32, 194)
        JUNK = at("JUNK", [P, D], F32, 64)
        MP = at("MP", [P, 2, D], F32, 178)
        ACC = at("ACC", [P, D], F32, 186)
        W1 = at("W1", [P, CMP_LEN // 2, P], F32, 64)
        ST = at("ST", [P, CMP_LEN // 2, NCMP], F32, 104)
        ST2 = at("ST2", [P, 2, CMP_LEN // 2, NCMP], F32, 72)
        PET = at("PET", [P, 2, CMP_LEN // 2], F32, 114)
        HID = at("HID", [P, 2, NCMP], F32, 112)
        W2 = at("W2", [P, 2, HD], F32, 112.5)
        PEROW = at("PEROW", [P, 2, P], F32, 113)
        V = at("V", [P, TT, 2, P], F32, 140)
        GT = at("GT", [P, TT, 3 * HEADS], F32, 148)
        KC = at("KC", [P, HD], F32, 148.75)
        VC = at("VC", [P, P], F32, 149)
        BC = at("BC", [P, TT, NCMP], F32, 149.5)
        BS = at("BS", [P, S], F32, 151.5)
        BW = at("BW", [P, WIN + P], F32, 155.5)
        PB = at("PB", [P, 2, 1728], F32, 178)
        QS = at("QS", [P, S], F32, 191.5)
        OT = at("OT", [P, 2, P], F32, 195.5)
        PT = at("PT", [P, 2, 4, P], F32, 196.5)
        SG = at("SG", [P, 2, HW], F32, 112)
        GMS = at("GMS", [P, S], F32, 80)
        GMH = [at("GMH0", [P, HW], F32, 156), at("GMH1", [P, HW], F32, 202)]
        WB = at("WB", [P, 2, CC, P], F32, 148)
        YT = at("YT", [P, HW], F32, 156)
        MA = at("MA", [P, 4, S], F32, 132)
        MB = at("MB", [P, 4, S], F32, 178)
        XR = at("XR", [P, S], F32, 152)
        RA = at("RA", [P, S], F32, 194)
        RI = at("RI", [P, S], F32, 198)
        SQ = at("SQ", [P, CC, HW], F32, 116)
        RS = at("RS", [P, 2, HW], F32, 128)
        YH = [None, at("YLH", [P, CC, S], F32R, 84), at("YCH", [P, CC, S], F32R, 116)]
        YL = [None, at("YLL", [P, CC, S], F32R, 100), at("YCL", [P, CC, S], F32R, 64)]
        WBH = at("WBH", [P, 2, CC, P], F32R, 152)
        WBL = at("WBL", [P, 2, CC, P], F32R, 148)
        DG = at("DG", [P, KT, P], F32, 124)
        G1B = at("G1B", [P, D], F32, 196)
        G2B = at("G2B", [P, D], F32, 200)
        WOA = at("WOA", [P, KT, HW], F32, 100)
        WOR = at("WOR", [P, KT, HW], F32, 116)
        WOH = [at("WOH0", [P, KT, HW], F32R, 84), at("WOH1", [P, KT, HW], F32R, 132)]
        WOL = [at("WOL0", [P, KT, HW], F32R, 100), at("WOL1", [P, KT, HW], F32R, 180)]
        X1 = at("X1", [P, TT, D], F32, 148)
        XN = at("XN", [P, 4, D], F32, 64)
        HT2 = at("HT2", [P, 2, HW], F32, 80)
        JUNK2 = at("JUNK2", [P, D], F32, 124)
        WR3 = at("WR3", [P, 2, KT, P], F32, 116)
        WH3 = at("WH3", [P, 2, KT, P], F32R, 84)
        WL3 = at("WL3", [P, 2, KT, P], F32R, 92)
        WFR = at("WFR", [P, 2, D], F32, 100)
        WFH = at("WFH", [P, 2, D], F32R, 108)
        WFL = at("WFL", [P, 2, D], F32R, 132)
        FH = at("FH", [P, 2, S], F32R, 140)
        FL = at("FL", [P, 2, S], F32R, 180)
        SA = at("SA", [P, 2, HW], F32, 188)
        FT = at("FT", [P, 2, HW], F32, 192)
        FNB = at("FNB", [P, D], F32, 64)
        CO = 204.0
        IDENT = at("IDENT", [P, P], F32, CO)
        ONES = at("ONES", [P, P], F32, CO + 0.5)
        COLS = at("COLS", [P, NROWS], F32, CO + 1.0)
        CW = at("CW", [P, CC, TAPS], F32, CO + 1.5)
        LCW = at("LCW", [P, CC, LTAPS], F32, CO + 2.0)
        MODC = at("MODC", [P, 48], F32, CO + 2.0625)
        SM = at("SM", [P, 128], F32, CO + 2.25)
        WAX = at("WAX", [P, 2, P], F32, CO + 2.78125)

        def gm(br, half):
            return GMH[half][:] if br == 0 else GMS[:, half * HW:(half + 1) * HW]

        def sm(a, n):
            return SM[:, a:a + n]

        SSQ, RSTD, RTMP = sm(0, 8), sm(8, 8), sm(16, 8)
        GSC, GSH = sm(24, 8), sm(32, 8)
        SPT = [sm(40 + 4 * i, 4) for i in range(6)]
        SP8, NSP8 = sm(64, 4), sm(68, 4)
        ROWOK = sm(72, 1)
        CB = sm(73, 4)
        SLOPE, NSLOPE, QSC = sm(77, 2), sm(98, 2), sm(79, 1)
        NM = [sm(80, 3), sm(83, 3)]
        DEN = [sm(86, 3), sm(89, 3)]
        RR = [sm(92, 3), sm(95, 3)]
        GSC2, GSH2 = sm(100, 8), sm(108, 8)

        def col(name, i=0, n=1):
            a = ROWS[name][0] + i
            return COLS[:, a:a + n]

        const_zero, const_set, table_made, wax_loaded = sem("const_zero"), sem("const_set"), sem("table_made"), sem("wax_loaded")
        stack_loaded, stack_t, c_loaded, c_turned = sem("stack_loaded"), sem("stack_t"), sem("c_loaded"), sem("c_turned")
        x_loaded = [sem(f"x_loaded{i}") for i in range(4)]
        wm_loaded = [sem(f"wm_loaded{i}") for i in range(KT)]
        wm_used, acc0_ready, mod0_mm, mod_ready = sem("wm_used"), sem("acc0_ready"), sem("mod0_mm"), sem("mod_ready")
        dve_step, act_step = sem("dve_step"), sem("act_step")

        class FormSems:

            def __init__(s, n):
                s.square, s.recip, s.rstd = sem(n + "_square"), sem(n + "_recip"), sem(n + "_rstd")
                s.xhat, s.turned, s.plain = sem(n + "_xhat"), sem(n + "_turned"), sem(n + "_plain")
                s.hi, s.ready = sem(n + "_hi"), sem(n + "_ready")

        f1, f2, f3 = FormSems("h1"), FormSems("h2"), FormSems("final")

        class RingSems:

            def __init__(s, n):
                s.loaded = [sem(n + "_loaded0"), sem(n + "_loaded1")]
                s.hi, s.lo, s.mm, s.out = sem(n + "_hi"), sem(n + "_lo"), sem(n + "_mm"), sem(n + "_out")

        r1, r3 = RingSems("in"), RingSems("ffn")
        mp_loaded = [sem("mp_loaded0"), sem("mp_loaded1")]
        mp_used, mod_mm, modc_done = sem("mp_used"), sem("mod_mm"), sem("modc_done")
        vt_turned, v_ready = sem("vt_turned"), sem("v_ready")
        w1_loaded, w2_loaded = [sem("w1_loaded_k"), sem("w1_loaded_v")], sem("w2_loaded")
        pe_turned, st_ready, cmp_mm, hid_ready, cmp2_mm, kvc_ready = (
            sem("cmp_" + n) for n in ("pe_turned", "st", "mm", "hid", "mm2", "ready"))
        st_crossed = sem("cmp_st_crossed")
        att_q, att_qsc, att_sc, att_mx, att_ex, att_tg, att_ev, att_pg, att_oo = (
            sem("att_" + n) for n in ("q", "qsc", "sc", "mx", "ex", "tg", "ev", "pg", "oo"))
        att_step, gated, glu_done, conv_steps = sem("att_step"), sem("gated"), sem("glu_done"), sem("conv_steps")
        lam_abs, lam_exp = sem("lam_abs"), sem("lam_exp")
        lru_x, lru_r, lru_rr, lru_i, lru_ab, lru_v, lru_sq, lru_gelu, y_lru_ready = (
            sem("lru_" + n) for n in ("x", "r", "rr", "i", "ab", "v", "sq", "gelu", "y"))
        ln_sum, ln_cent, ln_sq, ln_var, ln_rec, ln_rstd, ln_norm, y_conv_ready = (
            sem("ln_" + n) for n in ("sum", "cent", "sq", "var", "rec", "rstd", "norm", "y"))
        wb_loaded, wb_hi, wb_lo = [sem("wb_loaded0"), sem("wb_loaded1")], sem("wb_hi"), sem("wb_lo")
        y_hi, y_lo = sem("y_hi"), sem("y_lo")
        y_mm, y_used, sum_done, lru_step = sem("y_mm"), sem("y_used"), sem("sum_done"), sem("lru_step")
        dg_ready, gb_mm, gb_ready = sem("dg_ready"), sem("gb_mm"), sem("gb_ready")
        m_hi, m_ready = sem("m_hi"), sem("m_ready")
        wo_loaded = [sem("wo_loaded0"), sem("wo_loaded1")]
        wo_scaled, wo_hi, wo_lo, wo_mm, x1_done = (sem("wo_" + n) for n in ("scaled", "hi", "lo", "mm", "x1"))
        x1_loaded = [sem(f"x1_loaded{i}") for i in range(4)]
        wf_loaded, wf_scaled, wf_hi, wf_lo = (sem("wf_" + n) for n in ("loaded", "scaled", "hi", "lo"))
        f_gate, f_prod, f_hi, f_lo = (sem("f_" + n) for n in ("gate", "prod", "hi", "lo"))
        o_mm, o_added = sem("o_mm"), sem("o_added")
        fn_loaded, rows_ready, out_stored = sem("fn_loaded"), sem("rows_ready"), sem("out_stored")

        def products(pe, bank, w, wl, slot, half, r, a=0, e=3 * KT):
            for n in range(a, e):
                wt, h = ((w, HH), (w, HL), (wl, HH))[n // KT]
                k = n % KT
                last = pe.matmul(PS[:, bank, :], wt[:, slot, k, :], h[:, k, half * HW:(half + 1) * HW],
                                 start=(n == 0), stop=(n == 3 * KT - 1))
            if e == 3 * KT:
                last.then_inc(r.mm, 1)

        def gate(eng, s, value):
            eng.wait_ge(s, value)
            eng.sem_inc(gated, 1)

        class Chain:

            def __init__(c, eng, s, base=0):
                c.eng, c.s, c.base, c.n = eng, s, base, 0

            def link(c, ins):
                c.n += 1
                ins.then_inc(c.s, 1)
                c.eng.wait_ge(c.s, c.base + c.n)

        STEPS = [(qi, g) for qi in reversed(range(TT)) for g in range(2)]
        NST = len(STEPS)

        def tiles(qi):
            lo = max(0, qi - WIN // P)
            return [(0, k, P * k) for k in range(qi + 1)] + \
                   [(1, k, S + P * (k - lo)) for k in range(lo, qi + 1)] + [(2, 0, S + WIN + P)]

        NGR = [-(-len(tiles(qi)) // 4) for qi, g in STEPS]
        GI, TI, OI = [], [], {}
        ng = nt = 0
        for u in range(NST):
            GI.append(list(range(ng, ng + NGR[u])))
            TI.append(list(range(nt, nt + NGR[u])))
            ng, nt = ng + NGR[u], nt + NGR[u]
            if u % 2 == 0 and u:
                OI[u - 1] = nt
                nt += 1
        OI[NST - 1] = nt
        nt += 1
        assert ng % 2 == 0 and nt % 2 == 0
        BESIDE = [(1 + u // 3, 8 * (u % 3), 8 * (u % 3) + 8) for u in range(6)] + \
                 [(3 + v // 2, 12 * (v % 2), 12 * (v % 2) + 12) for v in range(8)] + [(7, 0, 6), (7, 6, 12)]
        TAIL = ((12, 18), (18, 24))
        ENDS = {u: h for u, (h, a, e) in enumerate(BESIDE) if e == 3 * KT}
        GLU_AT = 9
        LINKS = 5 * NST + 2 + 2
        NEAR_AT = {GLU_AT + 1: (0, 3), GLU_AT + 2: (3, 6), GLU_AT + 3: (6, 8), GLU_AT + 4: (8, 10)}
        NEAR = 10
        FAR_AT = [(u * (TAPS - NEAR) // (GLU_AT + 1) + NEAR, (u + 1) * (TAPS - NEAR) // (GLU_AT + 1) + NEAR) for u in range(GLU_AT + 1)]
        for h in range(HEADS):
            assert SLOPES[h] == 2.0 ** round(np.log2(SLOPES[h]))

        w_in = t["w_in"][0].rearrange("(k p) n -> p k n", p=P)
        w_mod = t["w_mod"][0].rearrange("(k p) n -> k p n", p=P)
        x_t = t["x"][0].rearrange("(t p) d -> p t d", p=P)
        KV = 2 * CONV + HEADS * HD
        LCOL = KV + 6 * P + 3 * HEADS
        CHUNKS = [(KV, KC_), (KV + P, VC_), (KV + 3 * P, VS_), (KV + 5 * P, VW_), (KV + 6 * P, GA_), (KV + 2 * P, KS_),
                  (KV + 4 * P, KW_)] + [(None, QQ + j) for j in range(4)]
        LANDS = [16 * (i + 1) + 16 * max(0, i - 6) for i in range(FIRST)]
        EXTRA = 16 * 4

        LAST_TILES = ((0, 4), (4, 6), (6, 8))
        M_ORDER = [k for c in range(4) for k in (c, c + 4)]

        block = ctx.enter_context(nc.Block())

        @block.sync
        def _(sp):
            sp.dma_start(STK[0:KT, 3, :], t["c"].rearrange("a (r p) -> (a r) p", p=P)).then_inc(c_loaded, 16)
            for i in range(4):
                sp.dma_start(X[:, 2 * i:2 * i + 2, :], x_t[:, 2 * i:2 * i + 2, :]).then_inc(x_loaded[i], 16)
            for n in range(2 * KT):
                k = n % KT
                if n >= KT:
                    sp.wait_ge(wm_used, k + 1)
                sp.dma_start(WM[:, k, :], w_mod[k, :, (n // KT) * D:(n // KT + 1) * D]).then_inc(wm_loaded[k], 16)

            def load_first(i):
                c0, u = CHUNKS[i]
                if i:
                    sp.wait_ge(r1.lo, i)
                if c0 is None:
                    for g in range(2):
                        a = 2 * CONV + g * 4 * HD + (u - QQ) * HD
                        sp.dma_start(WR[:, :, g * HD:(g + 1) * HD], w_in[:, :, a:a + HD]).then_inc(r1.loaded[0], 16)
                else:
                    sp.dma_start(WR[:], w_in[:, :, c0:c0 + P]).then_inc(r1.loaded[0], 16)

            def load_mod(m, h):
                for k in range(4 * h, 4 * h + 4):
                    if m or k >= 2:
                        sp.wait_ge(mp_used, KT * m + k - 1)
                    sp.dma_start(MP[:, k % 2, :], w_mod[k, :, (m + 2) * D:(m + 3) * D]).then_inc(mp_loaded[k % 2], 16)

            def load_w1(a):
                sp.dma_start(W1[:], t[f"nsa_w_c{'kv'[a]}1"][0].rearrange("(l p) n -> p l n", p=P)).then_inc(w1_loaded[a], 16)

            for i in range(FIRST):
                load_first(i)
                if 1 <= i <= 8:
                    load_mod((i - 1) // 2, (i - 1) % 2)
                if i == 3:
                    sp.wait_ge(f1.square, TT)
                    load_w1(0)
                    sp.wait_ge(f1.turned, 16)
                    for a, kv in enumerate("kv"):
                        sp.dma_start(W2[:, a, :], t[f"nsa_w_c{kv}2"][0]).then_inc(w2_loaded, 16)
                        sp.dma_start(PEROW[0:CMP_LEN // 2, a, :], t[f"nsa_pe_{kv}"][0].rearrange("(l o) d -> l (o d)", o=2)).then_inc(w2_loaded, 16)
                if i == 8:
                    sp.wait_ge(cmp_mm, 1)
                    load_w1(1)

            with sp.Fori(0, 4) as j:
                for q, c0 in enumerate((0, CONV, LCOL, LCOL + CONV)):
                    sp.wait_ge(r1.lo, LOOPED * j + FIRST + q)
                    sp.dma_start(WR[:], w_in[:, :, bass.ds(j * P + c0, P)]).then_inc(r1.loaded[0], 16)

            wm = t["w_merge"][0].rearrange("(k p) n -> p k n", p=P)
            wy = [None] + [t[n][0].rearrange("(k p) n -> p k n", p=P) for n in ("lru_w_out", "conv_w_out")]
            wg = t["nsa_w_out"][0].rearrange("(g j d) n -> g d j n", g=2, d=HD)

            def load_gate_chunk(br, c, s_):
                gate(sp, r1.lo, 2 * c + (8 * br + s_ + 27))
                sp.dma_start(WR[:], wm[:, :, bass.ds(c * P + (s_ * 4 * P + (1, 2, 0)[br] * D), P)]).then_inc(r1.loaded[0], 16)

            def load_output_chunk(br, c, s_, first=False):
                if not first:
                    gate(sp, y_mm, 2 * c + (8 * br + s_ - 1))
                cols = bass.ds(c * P + s_ * 4 * P, P)
                if br == 0:
                    for g in range(2):
                        sp.dma_start(WB[g * HD:(g + 1) * HD, s_], wg[g, :, :, cols]).then_inc(wb_loaded[s_], 16)
                else:
                    sp.dma_start(WB[:, s_], wy[br][:, :, cols]).then_inc(wb_loaded[s_], 16)

            def load_merge(br, c):
                for s_ in range(2):
                    load_gate_chunk(br, c, s_)
                    load_output_chunk(br, c, s_)

            def load_wax(c, first=False):
                if first:
                    sp.wait_ge(const_zero, 2)
                else:
                    sp.wait_ge(lru_i, c)
                for a, w in enumerate((t["lru_w_a"], t["lru_w_x"])):
                    for i in range(2):
                        src = w[0, bass.ds(2 * c + i, 1)].rearrange("a i j -> (a i) j")
                        sp.dma_start(WAX[i * HD:(i + 1) * HD, a, i * HD:(i + 1) * HD], src).then_inc(wax_loaded, 16)

            load_wax(0, True)
            load_gate_chunk(0, 0, 0)
            load_gate_chunk(0, 0, 1)
            sp.wait_ge(att_ev, 4 * nt)
            load_output_chunk(0, 0, 0, True)
            load_output_chunk(0, 0, 1, True)
            with sp.Fori(1, 4) as c:
                load_gate_chunk(0, c, 0)
                load_wax(c)
                load_output_chunk(0, c, 0)
                load_gate_chunk(0, c, 1)
                load_output_chunk(0, c, 1)
            with sp.Fori(0, 4) as c:
                load_merge(1, c)
            wo = t["w_out"][0].rearrange("(k p) n -> p k n", p=P)

            def load_wo(q):
                ks = slice(4 * (q % 2), 4 * (q % 2) + 4)
                sp.dma_start((WOA, WOR)[q // 2][:, ks, :], wo[:, ks, (q // 2) * HW:(q // 2 + 1) * HW]).then_inc(wo_loaded[q % 2], 16)

            load_merge(2, 0)
            sp.wait_ge(y_mm, 16)
            load_wo(0)
            load_wo(1)
            with sp.Fori(1, 4) as c:
                load_merge(2, c)
            sp.wait_ge(y_mm, 24)
            load_wo(2)
            load_wo(3)
            sp.wait_ge(m_ready, KT)
            for i in range(4):
                sp.dma_start(X1[:, 2 * i:2 * i + 2, :], x_t[:, 2 * i:2 * i + 2, :]).then_inc(x1_loaded[i], 16)
            wfi = t["w_ffn_in"][0].rearrange("(k p) n -> p k n", p=P)
            wfo = t["w_ffn_out"][0].rearrange("(m f p) n -> m p f n", f=2, p=P)
            sp.wait_ge(wo_lo, 4)

            def load_ffn(m, first):
                for q in range(4):
                    if not (first and q < 2):
                        gate(sp, r3.lo, 4 * m + q - 1)
                    sp.dma_start(WR3[:, q % 2], wfi[:, :, bass.ds((2 * m + q // 2) * P + (q % 2) * FFN, P)]).then_inc(r3.loaded[q % 2], 16)
                    if q == 1:
                        if first:
                            sp.wait_ge(wo_mm, TT)
                        else:
                            sp.wait_ge(wf_lo, m)
                        sp.dma_start(WFR[:], wfo[bass.ds(m, 1), :, :, :].rearrange("a p f n -> p (a f) n")).then_inc(wf_loaded, 16)

            load_ffn(0, True)
            with sp.Fori(1, FP) as m:
                load_ffn(m, False)
            sp.wait_ge(f2.turned, 16)
            sp.dma_start(FNB[:], t["final_norm"].partition_broadcast(P)).then_inc(fn_loaded, 16)
            o_t = out[0].rearrange("(t p) d -> p t d", p=P)
            for i in range(TT):
                sp.wait_ge(rows_ready, i + 1)
                sp.dma_start(o_t[:, i, :], X1[:, i, :]).then_inc(out_stored, 16)
            sp.wait_ge(out_stored, 16 * TT)

        @block.gpsimd
        def _(pool):
            pool.memset(IDENT[:], 0.0).then_inc(const_zero, 1)
            pool.memset(WAX[:], 0.0).then_inc(const_zero, 1)
            pool.memset(ONES[:], 1.0).then_inc(const_set, 1)
            pool.memset(ROWOK, 1.0).then_inc(const_set, 1)
            for g in range(2):
                pool.memset(SLOPE[:, g:g + 1], SLOPES[4 * g]).then_inc(const_set, 1)
                pool.memset(NSLOPE[:, g:g + 1], -SLOPES[4 * g]).then_inc(const_set, 1)
            for g in range(2):
                pool.wait_ge(const_set, 6 + g)
                pool.memset(QSC[g * HD:(g + 1) * HD, :], HD ** -0.5 / SLOPES[4 * g]).then_inc(const_set, 1)
            pool.wait_ge(const_set, 8)
            pool.wait_ge(const_zero, 2)
            pool.affine_select(out=IDENT[:], in_=IDENT[:], compare_op=ALU.not_equal, fill=1.0, base=0,
                               pattern=[[-1, P]], channel_multiplier=1).then_inc(const_set, 1)
            pool.wait_ge(const_set, 9)
            pool.affine_select(out=ROWOK, in_=ROWOK, compare_op=ALU.is_ge, fill=0.0, base=-(CMP_LEN - 1),
                               pattern=[[0, 1]], channel_multiplier=1).then_inc(const_set, 1)
            for o, pat, b in ((BS[:], [[1, S]], -(S - P)), (BW[:], [[1, WIN + P]], -WIN),
                              (BC[:], [[-P, TT], [CMP_STRIDE, NCMP]], CMP_LEN - 1)):
                pool.iota(o, pat, base=b, channel_multiplier=-1, allow_small_or_imprecise_dtypes=True).then_inc(table_made, 1)
            pool.wait_ge(table_made, 3)
            for o, pat, b in ((BS[:], [[-1, S]], S - P), (BW[:], [[-1, WIN + P]], WIN),
                              (BC[:], [[P, TT], [-CMP_STRIDE, NCMP]], -(CMP_LEN - 1))):
                pool.affine_select(out=o, in_=o, compare_op=ALU.is_ge, fill=NEG, base=b, pattern=pat,
                                   channel_multiplier=1).then_inc(table_made, 1)
            pool.wait_ge(table_made, 6)
            pool.affine_select(out=BW[:], in_=BW[:], compare_op=ALU.is_ge, fill=NEG, base=-1,
                               pattern=[[1, WIN + P]], channel_multiplier=-1).then_inc(table_made, 1)

            def lo(i, slot):
                pool.wait_ge(r1.hi, i + 1)
                pool.tensor_tensor(WL[:, slot], WR[:], WH[:, slot].bitcast(F32), ALU.subtract).then_inc(r1.lo, 1)

            def wb_low(i, s_):
                pool.wait_ge(wb_hi, i + 1)
                pool.tensor_tensor(WBL[:, s_], WB[:, s_], WBH[:, s_].bitcast(F32), ALU.subtract).then_inc(wb_lo, 1)

            with pool.Fori(0, 17) as m:
                lo(2 * m, 0)
                lo(2 * m + 1, 1)
            lo(34, 0)
            with pool.Fori(0, 8) as m:
                lo(2 * m + 35, 1)
                wb_low(2 * m, 0)
                lo(2 * m + 36, 0)
                wb_low(2 * m + 1, 1)

            def lo3(i, slot):
                pool.wait_ge(r3.hi, i + 1)
                pool.tensor_tensor(WL3[:, slot], WR3[:, slot], WH3[:, slot].bitcast(F32), ALU.subtract).then_inc(r3.lo, 1)

            def scale(m):
                pool.wait_ge(wf_loaded, 16 * m + 16)
                pool.tensor_tensor(WFR[:], WFR[:], G2B[:].unsqueeze(1).to_broadcast([P, 2, D]), ALU.mult).then_inc(wf_scaled, 1)

            lo3(0, 0)
            lo3(1, 1)
            pool.wait_ge(gb_ready, 2)
            scale(0)

            def ffn(m, last):
                for fi in range(2):
                    if not (last and fi):
                        lo3(4 * m + 2 * fi + 2, 0)
                        lo3(4 * m + 2 * fi + 3, 1)
                    pool.wait_ge(f_hi, 2 * m + fi + 1)
                    pool.tensor_tensor(FL[:, fi, :], FT[:].rearrange("p a b -> p (a b)"), FH[:, fi, :].bitcast(F32),
                                       ALU.subtract).then_inc(f_lo, 1)
                    if fi == 0:
                        pool.wait_ge(wf_hi, m + 1)
                        pool.tensor_tensor(WFL[:], WFR[:], WFH[:].bitcast(F32), ALU.subtract).then_inc(wf_lo, 1)
                    elif not last:
                        scale(m + 1)

            with pool.Fori(0, FP - 1) as m:
                ffn(m, False)
            ffn(FP - 1, True)

        @block.scalar
        def _(act):
            def stats(src, f, half, junk, waits):
                for i in range(4 * half, 4 * half + 4):
                    waits(i)
                    if i:
                        act.wait_ge(f.square, i)
                    act.activation(junk[:], src[:, i, :], ACT.Square, accum_out=SSQ[:, i:i + 1]).then_inc(f.square, 1)
                act.wait_ge(f.recip, half + 1)
                act.activation(RSTD[:, 4 * half:4 * half + 4], RTMP[:, 4 * half:4 * half + 4], ACT.Sqrt).then_inc(f.rstd, 1)

            def form(f, half, scale, shift, ht):
                for b in range(8 * half, 8 * half + 8):
                    k = b % KT
                    act.wait_ge(f.turned, b + 1)
                    if b >= 2:
                        act.wait_ge(f.ready, b - 1)
                    act.activation(ht[:, b % 2, :], PS[:, 4 + b % 4, :], ACT.Identity,
                                   bias=shift[:, k:k + 1], scale=scale[:, k:k + 1]).then_inc(f.plain, 1)

            for name, (a, n) in ROWS.items():
                if name != "c":
                    act.dma_start(STK[a:a + n, 0, :], t[name][0:1, :].rearrange("a (r p) -> (a r) p", p=P)).then_inc(stack_loaded, 16)
            for c in range(CC):
                act.dma_start(STK[TAPS * c:TAPS * (c + 1), 1, :], t["conv_w_dw"][0, :, c * P:(c + 1) * P]).then_inc(stack_loaded, 16)
                act.dma_start(STK[LTAPS * c:LTAPS * (c + 1), 2, :], t["lru_w_conv"][0, :, c * P:(c + 1) * P]).then_inc(stack_loaded, 16)
            for half in range(2):
                stats(X, f1, half, JUNK, lambda i: act.wait_ge(x_loaded[i // 2], 16))
                act.wait_ge(f1.square, 4 * half + 4)
                act.wait_ge(f1.rstd, half + 1)
                for i in range(4 * half, 4 * half + 4):
                    act.activation(X[:, i, :], X[:, i, :], ACT.Copy, scale=RSTD[:, i:i + 1]).then_inc(f1.xhat, 1)

            def hi(i, slot, loaded):
                act.wait_ge(r1.loaded[0], loaded)
                act.activation(WH[:, slot], WR[:], ACT.Copy).then_inc(r1.hi, 1)

            def put(i, dst, bank, func=ACT.Copy):
                for half in range(2):
                    act.wait_ge(r1.mm, 1 + 2 * half if i == 0 else 2 * i + 1 + half)
                    act.activation(dst[:, half * HW:(half + 1) * HW], PS[:, bank + half, :], func).then_inc(r1.out, 1)

            hi(0, 0, LANDS[0])
            act.wait_ge(mod_ready, 2)
            form(f1, 0, GSC, GSH, HT)
            hi(1, 1, LANDS[1])
            form(f1, 1, GSC, GSH, HT)
            ch = Chain(act, act_step)

            def hidden(a):
                act.wait_ge(cmp_mm, a + 1)
                ch.link(act.activation(CB[:, a:a + 1], PS[:, 7, 0:1], ACT.Copy))
                if a:
                    act.wait_ge(cmp2_mm, 1)
                act.activation(HID[:], PS[:, 6, 0:2 * NCMP].rearrange("p (g n) -> p g n", g=2), ACT.Gelu_apprx_tanh,
                               bias=CB[:, a:a + 1]).then_inc(hid_ready, 1)

            def cross(a):
                act.wait_ge(st_ready, 5 * a + 4)
                if a:
                    act.wait_ge(cmp_mm, 1)
                for g in range(2):
                    o = 1 - g
                    act.dma_start(ST2[o * HD:(o + 1) * HD, g, :, :], ST[g * HD:(g + 1) * HD, :, :]).then_inc(st_crossed, 16)

            for i in range(FIRST):
                put(i, UX[:, CHUNKS[i][1], :], 2 * (i % 2))
                if i != 5:
                    hi(i + 2, i % 2, LANDS[i + 2] if i + 2 < FIRST else 16 * (i + 3) + EXTRA)
                if i == 5:
                    for b in range(4):
                        act.wait_ge(vt_turned, b + 1)
                        act.activation(V[:, 4 * (b % 2):4 * (b % 2) + 4, b // 2, :], PS[:, 4 + b, :].rearrange("p (t f) -> p t f", t=4),
                                       ACT.Copy).then_inc(v_ready, 1)
                    act.wait_ge(vt_turned, 5)
                    logits = PS[:, 4, 0:TT * 3 * HEADS].rearrange("p (a b) -> p a b", b=3)
                    gates = GT[:].rearrange("p t (h b) -> p (t h) b", b=3)
                    act.activation(gates[:, :, 0:2], logits[:, :, 1:3], ACT.Sigmoid).then_inc(v_ready, 1)
                    act.activation(gates[:, :, 2:3], logits[:, :, 0:1], ACT.Sigmoid).then_inc(v_ready, 1)
                    hi(i + 2, i % 2, LANDS[i + 2])
                    cross(0)
                if i == 6:
                    hidden(0)
                if i == 7:
                    act.wait_ge(cmp2_mm, 1)
                    act.activation(KC[:, 0:NCMP], PS[:, 5, 0:NCMP], ACT.Copy).then_inc(kvc_ready, 1)
                    cross(1)
                if i == 9:
                    hidden(1)
            act.wait_ge(cmp2_mm, 2)
            act.activation(VC[0:NCMP, :], PS[0:NCMP, 5, 0:P], ACT.Copy).then_inc(kvc_ready, 1)

            act.wait_ge(r1.out, 2 * FIRST)
            act.wait_ge(const_set, 10)
            act.activation(QS[:], UX[:, QQ, :], ACT.Copy, scale=QSC).then_inc(att_q, 1)
            act.wait_ge(att_q, 1)
            with act.Fori(0, 4) as j:
                def exps(u):
                    qi, g = STEPS[u]
                    b, K, Kw = u % 2, P * (qi + 1), P * (min(qi, WIN // P) + 1)
                    act.wait_ge(att_mx, NST * j + u + 1)
                    for n, (a, e) in enumerate(((0, K), (S, S + Kw), (S + WIN + P, S + WIN + P + NCMP))):
                        act.activation(PB[:, b, a:e], PB[:, b, a:e], ACT.Exp, bias=NM[b][:, n:n + 1], scale=SLOPE[:, g:g + 1],
                                       accum_out=DEN[b][:, n:n + 1]).then_inc(att_ex, 1)

                def evac(u):
                    qi, g = STEPS[u]
                    n = len(tiles(qi))
                    for k in range(NGR[u]):
                        m = min(4, n - 4 * k)
                        if GI[u][k] >= 2:
                            act.wait_ge(att_pg, ng * j + GI[u][k] - 1)
                        act.wait_ge(att_tg, nt * j + TI[u][k] + 1)
                        act.activation(PT[:, GI[u][k] % 2, 0:m, :], PS[:, 4 + TI[u][k] % 2, 0:m * P].rearrange("p (a b) -> p a b", b=P),
                                       ACT.Copy).then_inc(att_ev, 1)

                def put_o(u):
                    qi = STEPS[u][0]
                    gate(act, att_tg, nt * j + OI[u] + 1)
                    act.activation(UX[:, bass.ds(j + QQ, 1), qi * P:(qi + 1) * P], PS[:, 4 + OI[u] % 2, 0:P], ACT.Copy).then_inc(att_ev, 1)

                def put_half(h):
                    q, half = h // 2, h % 2
                    if q == 1 and half == 0:
                        act.wait_ge(glu_done, 2 * j + 1)
                    if q == 3 and half == 0:
                        act.wait_ge(glu_done, 2 * j + 3)
                    cols = slice(half * HW, (half + 1) * HW)
                    dst = (CV[:, bass.ds(j + 1, 1), cols], SG[:, half, :], UX[:, bass.ds(j + LX, 1), cols], UX[:, bass.ds(j + LG, 1), cols])[q]
                    gate(act, r1.mm, 8 * j + (2 * FIRST + h + 1))
                    act.activation(dst, PS[:, 7, :], ACT.Sigmoid if q == 1 else ACT.Copy).then_inc(r1.out, 1)
                    if half:
                        hi(None, (FIRST + q) % 2, 64 * j + (16 * (FIRST + q + 3) + EXTRA))

                def next_queries():
                    act.activation(QSC, QSC, ACT.Copy, scale=SLOPES[0] / SLOPES[1]).then_inc(att_qsc, 1)
                    act.wait_ge(att_sc, NST * j + NST)
                    gate(act, att_qsc, j + 1)
                    act.activation(QS[:], UX[:, bass.ds(j + QQ + 1, 1), :], ACT.Copy, scale=QSC).then_inc(att_q, 1)

                put_half(0)
                exps(0)
                for u in range(NST):
                    if u - 1 in ENDS:
                        put_half(ENDS[u - 1])
                    if u == NST - 1:
                        next_queries()
                    evac(u)
                    if u - 1 in OI:
                        put_o(u - 1)
                    if u < NST - 1:
                        exps(u + 1)
                put_o(NST - 1)
                put_half(7)
                act.wait_ge(att_q, j + 2)

            def sig(br, c, s_, first=False):
                e = 2 * c + (8 * br + s_)
                name_at = (1, 2, 0)[br] * KT + 4 * s_ + ROWS["b_merge"][0]
                bias = COLS[:, bass.ds(c + name_at, 1)]
                if br:
                    act.wait_ge(wb_loaded[s_], 16 * c + (80 + 64 * br))
                    act.activation(WBH[:, s_], WB[:, s_], ACT.Copy).then_inc(wb_hi, 1)
                for half in range(2):
                    if not first:
                        act.wait_ge(y_used, 2 * e + half - 1)
                    gate(act, r1.mm, 2 * e + (54 + half + 1))
                    act.activation(gm(br, half), PS[:, 2 * ((27 + s_) % 2) + half, :], ACT.Sigmoid,
                                   bias=bias).then_inc(r1.out, 1)
                if not (br == 2 and isinstance(c, int) and c == 3):
                    hi(None, (27 + s_) % 2, 16 * e + (16 * 30 + EXTRA))

            act.wait_ge(lam_abs, 1)
            act.activation(SPT[2], SPT[1], ACT.Exp, scale=-1.0).then_inc(lam_exp, 1)

            def lru(c, first=False):
                sig(0, c, 0, first)
                gate(act, lru_r, c + 1)
                ba, bx = ROWS["lru_b_a"][0], ROWS["lru_b_x"][0]
                act.activation(RA[:], PS[:, 6:8, :], ACT.Sigmoid, bias=COLS[:, bass.ds(c + ba, 1)]).then_inc(lru_rr, 1)
                gate(act, lru_i, c + 1)
                act.activation(RI[:], PS[:, 6:8, :], ACT.Sigmoid, bias=COLS[:, bass.ds(c + bx, 1)]).then_inc(lru_ab, 1)
                x0 = UX[:, bass.ds(c + LX, 1), :]
                act.activation(x0, RA[:], ACT.Tanh, scale=SP8[:, bass.ds(c, 1)]).then_inc(lru_ab, 1)
                gate(act, lru_ab, 3 * c + 2)
                act.activation(RA[:], RA[:], ACT.Exp, scale=NSP8[:, bass.ds(c, 1)]).then_inc(lru_ab, 1)
                lg = UX[:, bass.ds(c + LG, 1), :]
                act.activation(lg, lg, ACT.Gelu_apprx_tanh).then_inc(lru_gelu, 1)
                gate(act, lru_v, c + 1)
                act.activation(x0, x0, ACT.Sqrt).then_inc(lru_sq, 1)
                sig(0, c, 1)

            act.wait_ge(lru_x, 1)
            lru(0, True)
            with act.Fori(1, 4) as c:
                lru(c)

            act.wait_ge(y_lru_ready, CC)
            act.activation(YH[1][:], UX[:, LG:LG + CC, :], ACT.Copy).then_inc(y_hi, 1)
            act.wait_ge(conv_steps, CC * TAPS)
            sig(1, 0, 0)
            for half in range(2):
                cols = slice(half * HW, (half + 1) * HW)
                act.wait_ge(ln_cent, half + 1)
                if half:
                    act.wait_ge(ln_var, 1)
                else:
                    act.wait_ge(y_mm, 8)
                act.activation(SQ[:], CV[:, 0:CC, cols], ACT.Square).then_inc(ln_sq, 1)
            sig(1, 0, 1)
            for half in range(2):
                act.wait_ge(ln_rec, half + 1)
                act.activation(RS[:, half, :], RS[:, half, :], ACT.Sqrt).then_inc(ln_rstd, 1)
            sig(1, 1, 0)
            sig(1, 1, 1)
            for c in range(CC):
                act.wait_ge(ln_norm, 2)
                act.activation(CV[:, c, :], CV[:, c, :], ACT.Silu, bias=col("conv_ln_b", c),
                               scale=col("conv_ln_g", c)).then_inc(y_conv_ready, 1)
            act.wait_ge(gb_mm, 2)
            act.wait_ge(y_conv_ready, CC)
            act.activation(YH[2][:], CV[:, 0:CC, :], ACT.Copy).then_inc(y_hi, 1)
            with act.Fori(2, 4) as c:
                sig(1, c, 0)
                sig(1, c, 1)

            def wo_hi_part(q):
                act.wait_ge(wo_scaled, q + 1)
                ks = slice(4 * (q % 2), 4 * (q % 2) + 4)
                act.activation(WOH[q // 2][:, ks, :], (WOA, WOR)[q // 2][:, ks, :], ACT.Copy).then_inc(wo_hi, 1)

            sig(2, 0, 0)
            sig(2, 0, 1)
            wo_hi_part(0)
            wo_hi_part(1)
            with act.Fori(1, 3) as c:
                sig(2, c, 0)
                sig(2, c, 1)
            for s_ in range(2):
                sig(2, 3, s_)

            act.wait_ge(r1.mm, 102)
            for k in M_ORDER:
                act.wait_ge(sum_done, 32 if k == KT - 1 else 18 + 4 * (k % 4) + 2 * (k // 4))
                m = (MA, MB)[k // 4][:, k % 4, :]
                act.activation(HH[:, k, :], m, ACT.Copy).then_inc(m_hi, 1)
            act.wait_ge(m_ready, KT)
            act.wait_ge(y_mm, 24)
            wo_hi_part(2)
            wo_hi_part(3)

            def ffn_hi(slot, loaded, mm=None):
                act.wait_ge(r3.loaded[slot], loaded)
                if mm is not None:
                    act.wait_ge(r3.mm, mm)
                act.activation(WH3[:, slot], WR3[:, slot], ACT.Copy).then_inc(r3.hi, 1)

            for half in range(2):
                stats(X1, f2, half, JUNK2, lambda i: act.wait_ge(x1_done, TT + i + 1))
                form(f2, half, GSC2, GSH2, HT2)
                if half == 0:
                    ffn_hi(0, 16)
                    ffn_hi(1, 16)

            def ffn(m, first, last):
                for fi in range(2):
                    for half in range(2):
                        act.wait_ge(r3.mm, 1 + 2 * half if first and fi == 0 else 8 * m + 4 * fi + half + 1)
                        if not (first and fi == 0):
                            act.wait_ge(f_prod, 4 * m + 2 * fi - 1 + half)
                        act.activation(SA[:, half, :], PS[:, half, :], ACT.Silu).then_inc(f_gate, 1)
                    if not (last and fi):
                        ffn_hi(0, 32 * m + 16 * fi + 32)
                        ffn_hi(1, 32 * m + 16 * fi + 32, 8 * m + 4 * fi + 4)
                    act.wait_ge(f_prod, 4 * m + 2 * fi + 2)
                    if not first:
                        act.wait_ge(o_mm, 16 * m)
                    act.activation(FH[:, fi, :], FT[:].rearrange("p a b -> p (a b)"), ACT.Copy).then_inc(f_hi, 1)
                    if fi == 0:
                        act.wait_ge(wf_scaled, m + 1)
                        act.activation(WFH[:], WFR[:], ACT.Copy).then_inc(wf_hi, 1)

            ffn(0, True, False)
            with act.Fori(1, FP - 1) as m:
                ffn(m, False, False)
            ffn(FP - 1, False, True)
            for n, (a, e) in enumerate(LAST_TILES):
                for i in range(a, e):
                    act.wait_ge(o_added, 16 * (FP - 1) + 2 * i + 2)
                    if i:
                        act.wait_ge(f3.square, i)
                    act.activation(JUNK2[:], X1[:, i, :], ACT.Square, accum_out=SSQ[:, i:i + 1]).then_inc(f3.square, 1)
                act.wait_ge(f3.recip, n + 1)
                act.activation(RSTD[:, a:e], RTMP[:, a:e], ACT.Sqrt).then_inc(f3.rstd, 1)

        @block.tensor
        def _(pe):
            pe.wait_ge(c_loaded, 16)
            pe.wait_ge(const_set, 9)
            pe.transpose(PS[:, 3, 16:16 + KT], STK[0:KT, 3, :], IDENT[0:KT, 0:KT]).then_inc(c_turned, 1)

            def turn(src, f, half, at0, blocks=range(KT)):
                pe.wait_ge(f.xhat, 4 * half + 4)
                for b in (8 * half + k for k in blocks):
                    k = b % KT
                    if b >= 4:
                        pe.wait_ge(f.plain, b - 3)
                    for i in range(4):
                        last = pe.transpose(PS[:, 4 + b % 4, i * P:(i + 1) * P], src[:, at0 + i, k * P:(k + 1) * P], IDENT[:])
                    last.then_inc(f.turned, 1)

            turn(X, f1, 0, 0, range(4))
            pe.wait_ge(stack_loaded, 16 * (len(ROWS) - 1 + 2 * CC))
            nr = NROWS - KT
            pe.transpose(PS[:, 0, 0:nr], STK[0:nr, 0, :], IDENT[0:nr, 0:nr])
            pe.transpose(PS[:, 1, 0:CC * TAPS], STK[0:CC * TAPS, 1, :], IDENT[0:CC * TAPS, 0:CC * TAPS])
            pe.transpose(PS[:, 2, 0:CC * LTAPS], STK[0:CC * LTAPS, 2, :], IDENT[0:CC * LTAPS, 0:CC * LTAPS]).then_inc(stack_t, 1)
            for j in range(16):
                if j % KT == 0:
                    pe.wait_ge(acc0_ready, j // KT + 1)
                last = pe.matmul(PS[:, 3, j:j + 1], ACC0[:, j * P:(j + 1) * P], ONES[:, 0:1], start=True, stop=True)
            last.then_inc(mod0_mm, 1)
            turn(X, f1, 0, 0, range(4, KT))
            turn(X, f1, 1, 4, range(4))

            def compress_in(a):
                nl = CMP_LEN // 2
                pe.wait_ge(w2_loaded, 16 * 4)
                pe.wait_ge(v_ready, 4)
                if a:
                    pe.wait_ge(kvc_ready, 1)
                    pe.wait_ge(hid_ready, 1)
                pe.transpose(PS[:, 5, 0:nl], PEROW[0:nl, a, :], IDENT[0:nl, 0:nl]).then_inc(pe_turned, 1)
                pe.wait_ge(w1_loaded[a], 16)
                pe.wait_ge(st_ready, 5 * a + 5)
                pe.wait_ge(st_crossed, 32 * a + 32)
                for l in range(nl):
                    pe.matmul(PS[:, 6, 0:2 * NCMP], W1[:, l, :], ST2[:, :, l, :], start=(l == 0), stop=(l == nl - 1))
                for l in range(nl):
                    last = pe.matmul(PS[:, 7, 0:1], W1[:, l, :], PET[:, a, l:l + 1], start=(l == 0), stop=(l == nl - 1))
                last.then_inc(cmp_mm, 1)

            def compress_out(a):
                pe.wait_ge(hid_ready, a + 1)
                for g in range(2):
                    if a == 0:
                        last = pe.matmul(PS[g * HD:(g + 1) * HD, 5, 0:NCMP], W2[:, 0, :], HID[:, g, 0:NCMP], start=True, stop=True)
                    else:
                        last = pe.matmul(PS[0:NCMP, 5, g * HD:(g + 1) * HD], HID[:, g, 0:NCMP], W2[:, 1, :], start=True, stop=True)
                last.then_inc(cmp2_mm, 1)

            for i in range(FIRST):
                pe.wait_ge(r1.lo, i + 1)
                if i >= 2:
                    pe.wait_ge(r1.out, 2 * (i - 1))
                if i == 0:
                    pe.wait_ge(f1.ready, 8)
                    pe.wait_ge(mod_ready, 2)
                    products(pe, 0, WH, WL, 0, 0, r1, 0, 12)
                    turn(X, f1, 1, 4, range(4, 6))
                    products(pe, 0, WH, WL, 0, 0, r1, 12, 24)
                    turn(X, f1, 1, 4, range(6, KT))
                    continue
                if i == 1:
                    products(pe, 2, WH, WL, 1, 0, r1)
                    pe.wait_ge(f1.ready, 16)
                    for slot in range(2):
                        products(pe, 2 * slot + 1, WH, WL, slot, 1, r1)
                for half in range(2 if i > 1 else 0):
                    products(pe, 2 * (i % 2) + half, WH, WL, i % 2, half, r1)
                if i % 2 and i < 8:
                    m = i // 2
                    pe.wait_ge(mp_used, KT * (m + 1))
                    if m == 3:
                        pe.wait_ge(v_ready, 6)
                    for k in range(KT):
                        last = pe.matmul(PS[:, 4, k:k + 1], ACC[:, k * P:(k + 1) * P], ONES[:, 0:1], start=True, stop=True)
                    last.then_inc(mod_mm, 1)
                if i == 5:
                    pe.wait_ge(r1.out, 10)
                    pe.wait_ge(modc_done, 3)
                    for b in range(4):
                        for k in range(4):
                            tok = 4 * (b % 2) + k
                            last = pe.transpose(PS[:, 4 + b, k * P:(k + 1) * P], UX[:, VS_ + b // 2, tok * P:(tok + 1) * P], IDENT[:])
                        last.then_inc(vt_turned, 1)
                    n = 3 * HEADS
                    pe.wait_ge(v_ready, 1)
                    for tok in range(TT):
                        last = pe.transpose(PS[:, 4, tok * n:(tok + 1) * n], UX[0:n, GA_, tok * P:(tok + 1) * P], IDENT[0:n, 0:n])
                    last.then_inc(vt_turned, 1)
                if i == 6:
                    compress_in(0)
                if i == 7:
                    compress_out(0)
                if i == 9:
                    compress_in(1)
            compress_out(1)

            pe.wait_ge(kvc_ready, 2)
            pe.wait_ge(r1.out, 2 * FIRST)
            pe.wait_ge(modc_done, 4)
            pe.wait_ge(table_made, 7)
            with pe.Fori(0, 4) as j:
                def scores(u):
                    qi, g = STEPS[u]
                    rows = slice(g * HD, (g + 1) * HD)
                    q = QS[rows, qi * P:(qi + 1) * P]
                    K, Kw = P * (qi + 1), P * (min(qi, WIN // P) + 1)
                    if u:
                        pe.wait_ge(att_mx, NST * j + u)
                    for b, (a, e) in enumerate(((0, min(K, HW)), (HW, K))):
                        if e > a:
                            pe.matmul(PS[:, b, 0:e - a], q, UX[rows, KS_, a:e], start=True, stop=True)
                    for b, (a, e) in enumerate(((K - Kw, K - Kw + min(Kw, HW)), (K - Kw + HW, K))):
                        if e > a:
                            pe.matmul(PS[:, 2 + b, 0:e - a], q, UX[rows, KW_, a:e], start=True, stop=True)
                    pe.matmul(PS[:, 3, P:P + NCMP], q, KC[rows, 0:NCMP], start=True, stop=True).then_inc(att_sc, 1)

                def beside(h, a, e):
                    q, half = h // 2, h % 2
                    if a == 0:
                        pe.wait_ge(r1.out, 8 * j + (2 * FIRST + h))
                        pe.wait_ge(r1.lo, LOOPED * j + (FIRST + q + 1))
                    products(pe, 7, WH, WL, (FIRST + q) % 2, half, r1, a, e)

                def turn_p(u, k):
                    qi, g = STEPS[u]
                    if TI[u][k] >= 2:
                        gate(pe, att_ev, nt * j + TI[u][k] - 1)
                    for i, (br, kt, a) in enumerate(tiles(qi)[4 * k:4 * k + 4]):
                        m = NCMP if br == 2 else P
                        last = pe.transpose(PS[0:m, 4 + TI[u][k] % 2, i * P:(i + 1) * P], PB[:, u % 2, a:a + m], IDENT[:])
                    last.then_inc(att_tg, 1)

                def turn_o(u):
                    pe.wait_ge(att_ev, nt * j + OI[u] - 1)
                    pe.wait_ge(att_oo, NST * j + u + 1)
                    pe.transpose(PS[:, 4 + OI[u] % 2, 0:P], OT[:, STEPS[u][0] % 2, :], IDENT[:]).then_inc(att_tg, 1)

                def pv(u, k):
                    qi, g = STEPS[u]
                    pe.wait_ge(att_ev, nt * j + TI[u][k] + 1)
                    if u and k == 0:
                        pe.wait_ge(att_oo, NST * j + u)
                    ts = tiles(qi)
                    for n in range(4 * k, min(4 * k + 4, len(ts))):
                        br, kt, a = ts[n]
                        m = NCMP if br == 2 else P
                        v = VC[0:m, g * HD:(g + 1) * HD] if br == 2 else V[:, kt, br, g * HD:(g + 1) * HD]
                        last = pe.matmul(PS[:, 6, br * HD:(br + 1) * HD], PT[0:m, GI[u][k] % 2, n - 4 * k, :], v,
                                         start=(n == 0 or ts[n - 1][0] != br), stop=(n + 1 == len(ts) or ts[n + 1][0] != br))
                    last.then_inc(att_pg, 1)

                pe.wait_ge(att_q, j + 1)
                scores(0)
                beside(0, 0, 3 * KT)
                for u in range(NST):
                    h, a, e = BESIDE[u]
                    mid = (a + e) // 2
                    if u < NST - 1:
                        scores(u + 1)
                    beside(h, a, mid)
                    pe.wait_ge(att_ex, 3 * NST * j + 3 * u + 3)
                    turn_p(u, 0)
                    if NGR[u] > 1:
                        turn_p(u, 1)
                    beside(h, mid, e)
                    for k in range(NGR[u]):
                        pv(u, k)
                        if k + 2 < NGR[u]:
                            turn_p(u, k + 2)
                    if u - 1 in OI:
                        turn_o(u - 1)
                beside(7, *TAIL[0])
                turn_o(NST - 1)
                beside(7, *TAIL[1])
                pe.wait_ge(att_mx, NST * j + NST)
                pe.wait_ge(att_ev, nt * j + nt)
                pe.wait_ge(att_oo, NST * j + NST)

            def merge(br, c, s_, between=None, first=False):
                e = 2 * c + (8 * br + s_)
                slot = (27 + s_) % 2
                pe.wait_ge(r1.lo, e + 28)
                pe.wait_ge(r1.out, 2 * e + 52)
                for half in range(2):
                    products(pe, 2 * slot + half, WH, WL, slot, half, r1)
                if between:
                    between()
                if br == 0:
                    pe.wait_ge(wb_loaded[s_], 32 * c + 32)
                    terms = [(WB, UX[:, QQ:QQ + CC, :])]
                else:
                    pe.wait_ge(wb_lo, e - 7)
                    pe.wait_ge(y_lo, br)
                    terms = [(WBH, YH[br]), (WBH, YL[br]), (WBL, YH[br])]
                if not first:
                    pe.wait_ge(y_used, 2 * e)
                nk = CC * len(terms)
                for half in range(2):
                    for n in range(nk):
                        w, y = terms[n // CC]
                        last = pe.matmul(PS[:, 4 + half, :], w[:, s_, n % CC, :], y[:, n % CC, half * HW:(half + 1) * HW],
                                         start=(n == 0), stop=(n == nk - 1))
                last.then_inc(y_mm, 1)

            def lru_products(a, c):
                for half in range(2):
                    last = pe.matmul(PS[:, 6 + half, :], WAX[:, a, :], XR[:, half * HW:(half + 1) * HW], start=True, stop=True)
                last.then_inc((lru_r, lru_i)[a], 1)

            def lru(c, first=False):
                def r_part():
                    pe.wait_ge(wax_loaded, 64 * c + 64)
                    pe.wait_ge(lru_x, c + 1)
                    if not first:
                        pe.wait_ge(lru_ab, 3 * c)
                    lru_products(0, c)

                merge(0, c, 0, r_part, first)
                pe.wait_ge(lru_rr, c + 1)
                lru_products(1, c)
                merge(0, c, 1)

            lru(0, True)
            with pe.Fori(1, 4) as c:
                lru(c)

            def ln_sums():
                pe.wait_ge(lru_ab, 12)
                pe.wait_ge(conv_steps, CC * TAPS)
                for half in range(2):
                    for c in range(CC):
                        last = pe.matmul(PS[:, 6 + half, :], ONES[:], CV[:, c, half * HW:(half + 1) * HW], start=(c == 0), stop=(c == CC - 1))
                    last.then_inc(ln_sum, 1)

            def ln_vars(half):
                pe.wait_ge(ln_sq, half + 1)
                for c in range(CC):
                    last = pe.matmul(PS[:, 6 + half, :], ONES[:], SQ[:, c, :], start=(c == 0), stop=(c == CC - 1))
                last.then_inc(ln_var, 1)

            pe.wait_ge(y_lru_ready, CC)
            merge(1, 0, 0, ln_sums)
            ln_vars(0)
            merge(1, 0, 1)
            ln_vars(1)

            def spread(n):
                pe.wait_ge(ln_rec, 2)
                pe.wait_ge(dg_ready, 8 * n + 8)
                if n:
                    pe.wait_ge(gb_ready, 1)
                for b in range(2):
                    last = pe.matmul(PS[:, 6 + b, :], ONES[:], DG[:, 4 * b:4 * b + 4, :].rearrange("p a b -> p (a b)"), start=True, stop=True)
                last.then_inc(gb_mm, 1)

            for n in range(2):
                merge(1, 1, n, lambda: spread(n))
            with pe.Fori(2, 4) as c:
                merge(1, c, 0)
                merge(1, c, 1)
            with pe.Fori(0, 4) as c:
                merge(2, c, 0)
                merge(2, c, 1)

            pe.wait_ge(r1.out, 102)
            pe.wait_ge(gb_ready, 2)

            def rows_out(nh, tok, k, n):
                last = None
                for z, (h, w) in enumerate(((HH, WOH[nh]), (HH, WOL[nh]), (HL, WOH[nh]))):
                    last = pe.matmul(PS[:, tok % 4, :], h[:, k, tok * P:(tok + 1) * P], w[:, k, :],
                                     start=(n + z == 0), stop=(n == KT - 1 and z == 2))
                return last

            pe.wait_ge(wo_lo, 2)
            for n, k in enumerate(M_ORDER):
                pe.wait_ge(m_ready, n + 1)
                for tok in range(4):
                    last = rows_out(0, tok, k, n)
                    if n == KT - 1:
                        last.then_inc(wo_mm, 1)
            for nh in range(2):
                if nh:
                    pe.wait_ge(wo_lo, 4)
                for tok in range(4 * (1 - nh), TT):
                    i = TT * nh + tok
                    pe.wait_ge(x1_done, i - 3)
                    for k in range(KT):
                        last = rows_out(nh, tok, k, k)
                    last.then_inc(wo_mm, 1)
                    if i in (TT + 5, TT + 6):
                        turn(XN, f2, 0, 0, range(4) if i == TT + 5 else range(4, KT))
            pe.wait_ge(x1_done, 16)

            def out_mm(m):
                pe.wait_ge(f_lo, 2 * m + 2)
                pe.wait_ge(wf_lo, m + 1)
                for tok in range(TT):
                    rows = slice(tok * P, (tok + 1) * P)
                    for nh in range(2):
                        i = 2 * tok + nh
                        if i >= 4:
                            pe.wait_ge(o_added, 16 * m + i - 3)
                        n = 0
                        for h, w in ((FH, WFH), (FH, WFL), (FL, WFH)):
                            for fi in range(2):
                                last = pe.matmul(PS[:, 4 + i % 4, :], h[:, fi, rows], w[:, fi, nh * HW:(nh + 1) * HW],
                                                 start=(n == 0), stop=(n == 5))
                                n += 1
                        last.then_inc(o_mm, 1)

            def start(q):
                if q == 0:
                    pe.wait_ge(f2.ready, 8)
                    products(pe, 0, WH3, WL3, 0, 0, r3)
                    turn(XN, f2, 1, 0, range(4))
                else:
                    products(pe, 2, WH3, WL3, 1, 0, r3, 0, 12)
                    turn(XN, f2, 1, 0, range(4, 6))
                    products(pe, 2, WH3, WL3, 1, 0, r3, 12, 24)
                    turn(XN, f2, 1, 0, range(6, KT))
                    pe.wait_ge(f2.ready, 16)
                    for slot in range(2):
                        products(pe, 2 * slot + 1, WH3, WL3, slot, 1, r3)

            def ffn(m, first):
                for q in range(4):
                    pe.wait_ge(r3.lo, 4 * m + q + 1)
                    if not (first and q < 2):
                        pe.wait_ge((f_gate, f_prod)[q % 2], 4 * m + 2 * (q // 2))
                    if first and q < 2:
                        start(q)
                        continue
                    for half in range(2):
                        products(pe, 2 * (q % 2) + half, WH3, WL3, q % 2, half, r3)
                    if q == 1 and not first:
                        out_mm(m - 1)
                    if q == 2 and not first:
                        pe.wait_ge(o_added, 16 * m)

            ffn(0, True)
            with pe.Fori(1, FP) as m:
                ffn(m, False)
            out_mm(FP - 1)

        @block.vector
        def _(dve):
            main = Chain(dve, dve_step)
            link = main.link

            ccol = col("c", 0, 8)
            dve.wait_ge(c_turned, 1)
            link(dve.tensor_copy(ccol, PS[:, 3, 16:16 + KT]))

            def mod0(n):
                k, acc = n % KT, ACC0[:, (n // KT) * D:(n // KT + 1) * D]
                dve.wait_ge(wm_loaded[k], 16 * (n // KT + 1))
                if k == 0:
                    ins = dve.tensor_scalar(acc, WM[:, k, :], ccol[:, 0:1], None, ALU.mult)
                else:
                    dve.wait_ge(wm_used, n)
                    ins = dve.scalar_tensor_tensor(acc, WM[:, k, :], ccol[:, k:k + 1], acc, ALU.mult, ALU.add)
                ins.then_inc(wm_used, 1)
                if k == KT - 1:
                    dve.wait_ge(wm_used, n + 1)
                    dve.sem_inc(acc0_ready, 1)

            def rstd(f, half):
                a = slice(4 * half, 4 * half + 4)
                dve.wait_ge(f.square, 4 * half + 4)
                link(dve.tensor_scalar(RTMP[:, a], SSQ[:, a], 1.0 / D, EPS, ALU.mult, ALU.add))
                dve.reciprocal(RTMP[:, a], RTMP[:, a]).then_inc(f.recip, 1)
                dve.wait_ge(f.rstd, half + 1)

            def split(f, half0, ht, blocks=range(KT)):
                for b in (8 * half0 + k for k in blocks):
                    half, k = b // KT, b % KT
                    cols = slice(half * HW, (half + 1) * HW)
                    dve.wait_ge(f.plain, b + 1)
                    dve.tensor_copy(HH[:, k, cols], ht[:, b % 2, :]).then_inc(f.hi, 1)
                    dve.wait_ge(f.hi, b + 1)
                    dve.tensor_tensor(HL[:, k, cols], ht[:, b % 2, :], HH[:, k, cols].bitcast(F32), ALU.subtract).then_inc(f.ready, 1)

            for n in range(2 * KT):
                mod0(n)
                if n in (3, 9):
                    rstd(f1, n // 9)
            dve.wait_ge(stack_t, 1)
            dve.tensor_copy(COLS[:, 0:NROWS - KT], PS[:, 0, 0:NROWS - KT])
            dve.tensor_copy(CW[:], PS[:, 1, 0:CC * TAPS].rearrange("p (c t) -> p c t", c=CC))
            link(dve.tensor_copy(LCW[:], PS[:, 2, 0:CC * LTAPS].rearrange("p (c t) -> p c t", c=CC)))
            dve.wait_ge(mod0_mm, 1)
            link(dve.tensor_tensor(MODC[:, 0:16], PS[:, 3, 0:16], col("b_mod", 0, 16), ALU.add))
            dve.tensor_copy(GSH, MODC[:, 0:8]).then_inc(mod_ready, 1)
            dve.scalar_tensor_tensor(GSC, MODC[:, 8:16], 1.0, col("norm_mix", 0, 8), ALU.add, ALU.mult).then_inc(mod_ready, 1)
            split(f1, 0, HT)
            split(f1, 1, HT)

            def mod(m):
                for k in range(KT):
                    dve.wait_ge(mp_loaded[k % 2], 64 * m + 16 * (k // 2 + 1))
                    if k == 0:
                        if m:
                            dve.wait_ge(mod_mm, m)
                        ins = dve.tensor_scalar(ACC[:], MP[:, 0, :], ccol[:, 0:1], None, ALU.mult)
                    else:
                        dve.wait_ge(mp_used, KT * m + k)
                        ins = dve.scalar_tensor_tensor(ACC[:], MP[:, k % 2, :], ccol[:, k:k + 1], ACC[:], ALU.mult, ALU.add)
                    ins.then_inc(mp_used, 1)

            def modc(m):
                dve.wait_ge(mod_mm, m + 1)
                dve.tensor_tensor(MODC[:, 8 * m + 16:8 * m + 24], PS[:, 4, 0:8], col("b_mod", 8 * m + 16, 8), ALU.add).then_inc(modc_done, 1)

            def stage(a):
                nl = CMP_LEN // 2
                dve.wait_ge(r1.out, 2 * a + 2)
                if a:
                    dve.wait_ge(st_crossed, 32)
                    dve.wait_ge(cmp_mm, 1)
                for g in range(2):
                    rows = slice(g * HD, (g + 1) * HD)
                    src = UX[rows, KC_ + a, :].rearrange("p (c l o) -> p o l c", o=2, l=nl // 2)
                    for o, dst in ((g, ST2[rows, g]), (1 - g, ST[rows])):
                        for h in range(2):
                            ls = slice(h * nl // 2, (h + 1) * nl // 2)
                            ins = dve.tensor_copy(dst[:, ls, :], src[:, o, :, h:h + NCMP])
                        ins.then_inc(st_ready, 1)
                dve.wait_ge(pe_turned, a + 1)
                dve.tensor_copy(PET[:, a, :], PS[:, 5, 0:nl]).then_inc(st_ready, 1)

            for m in range(3):
                mod(m)
                modc(m)
            stage(0)
            mod(3)
            modc(3)
            lam = col("lru_lam", 0, 4)
            link(dve.tensor_scalar(SPT[0], lam, -1.0, None, ALU.mult))
            dve.tensor_tensor(SPT[1], lam, SPT[0], ALU.max).then_inc(lam_abs, 1)
            stage(1)

            dve.sem_inc(glu_done, 1)
            dve.wait_ge(table_made, 7)
            def tap(c, shift, first=False):
                w = CW[:, bass.ds(c, 1), TAPS - 1 - shift].rearrange("p a -> p a")
                res, src = CV[:, bass.ds(c, 1), shift:S], CV[:, bass.ds(c + 1, 1), 0:S - shift]
                if not first:
                    dve.wait_ge(conv_steps, TAPS * c + shift)
                if shift == 0:
                    ins = dve.tensor_scalar(res, src, w, COLS[:, bass.ds(c + ROWS["conv_b_dw"][0], 1)], ALU.mult, ALU.add)
                else:
                    ins = dve.scalar_tensor_tensor(res, src, w, res, ALU.mult, ALU.add)
                ins.then_inc(conv_steps, 1)

            def pair(j, first):
                ch = Chain(dve, att_step, LINKS * j)

                def maxima(u):
                    qi, g = STEPS[u]
                    b, K, Kw = u % 2, P * (qi + 1), P * (min(qi, WIN // P) + 1)
                    if u >= 2:
                        dve.wait_ge(att_tg, nt * j + TI[u - 2][-1] + 1)
                    gate(dve, att_sc, NST * j + u + 1)
                    flat = PS[:].rearrange("p b n -> p (b n)")
                    for n, (o, s_, bias) in enumerate((
                            (PB[:, b, 0:K], flat[:, 0:K], BS[:, S - K:S]),
                            (PB[:, b, S:S + Kw], flat[:, 2 * HW:2 * HW + Kw], BW[:, WIN + P - Kw:WIN + P]),
                            (PB[:, b, S + WIN + P:S + WIN + P + NCMP], PS[:, 3, P:P + NCMP], BC[:, qi, :]))):
                        ins = dve.tensor_tensor_reduce(o, s_, bias, 1.0, -3e38, ALU.add, ALU.max, NM[b][:, n:n + 1])
                    ch.link(ins)
                    dve.tensor_scalar(NM[b], NM[b], NSLOPE[:, g:g + 1], None, ALU.mult).then_inc(att_mx, 1)

                def outputs(u):
                    qi, g = STEPS[u]
                    r = RR[u % 2]
                    dve.wait_ge(att_ex, 3 * NST * j + 3 * u + 3)
                    ch.link(dve.reciprocal(r, DEN[u % 2]))
                    ch.link(dve.tensor_tensor(r, r, GT[:, qi, bass.ds(3 * j + 12 * g, 3)], ALU.mult))
                    if qi == 0:
                        ch.link(dve.tensor_tensor(r[:, 2:3], r[:, 2:3], ROWOK, ALU.mult))
                    dve.wait_ge(att_pg, ng * j + GI[u][-1] + 1)
                    if g == 0 and u >= 4:
                        dve.wait_ge(att_tg, nt * j + OI[u - 3] + 1)
                    o = OT[:, qi % 2, g * HD:(g + 1) * HD]
                    ch.link(dve.tensor_scalar(o, PS[:, 6, 0:HD], r[:, 0:1], None, ALU.mult))
                    ch.link(dve.scalar_tensor_tensor(o, PS[:, 6, HD:2 * HD], r[:, 1:2], o, ALU.mult, ALU.add))
                    dve.scalar_tensor_tensor(o, PS[:, 6, 2 * HD:3 * HD], r[:, 2:3], o, ALU.mult, ALU.add).then_inc(att_oo, 1)

                def glu():
                    for half in range(2):
                        v = CV[:, bass.ds(j + 1, 1), half * HW:(half + 1) * HW]
                        dve.wait_ge(r1.out, 8 * j + (2 * FIRST + 3 + half))
                        dve.tensor_tensor(v, v, SG[:, half, :].unsqueeze(1), ALU.mult).then_inc(glu_done, 1)
                    dve.wait_ge(glu_done, 2 * j + 3)

                maxima(0)
                for u in range(NST):
                    if u < NST - 1:
                        maxima(u + 1)
                    if u <= GLU_AT and not first:
                        for shift in range(*FAR_AT[u]):
                            tap(j - 1, shift)
                    if u == GLU_AT:
                        glu()
                    if u in NEAR_AT:
                        for shift in range(*NEAR_AT[u]):
                            tap(j, shift, first and shift == 0)
                    outputs(u)
                dve.wait_ge(conv_steps, TAPS * j + NEAR)
                ch.link(dve.tensor_scalar(SLOPE, SLOPE, SLOPES[1] / SLOPES[0], None, ALU.mult))
                ch.link(dve.tensor_scalar(NSLOPE, NSLOPE, SLOPES[1] / SLOPES[0], None, ALU.mult))
                assert ch.n == LINKS

            pair(0, True)
            with dve.Fori(1, 4) as j:
                pair(j, False)

            dve.wait_ge(lam_exp, 1)
            e, z, z2, p = SPT[2], SPT[3], SPT[4], SPT[5]
            link(dve.tensor_scalar(z, e, 2.0, None, ALU.add))
            link(dve.reciprocal(z, z))
            link(dve.tensor_tensor(z, z, e, ALU.mult))
            link(dve.tensor_tensor(z2, z, z, ALU.mult))
            link(dve.tensor_scalar(p, z2, 1.0 / 19, None, ALU.mult))
            for n in range(17, 1, -2):
                link(dve.scalar_tensor_tensor(p, p, 1.0 / n, z2, ALU.add, ALU.mult))
            link(dve.scalar_tensor_tensor(p, p, 1.0, z, ALU.add, ALU.mult))
            link(dve.tensor_scalar(z, SPT[0], 0.0, None, ALU.max))
            link(dve.scalar_tensor_tensor(p, p, 2.0, z, ALU.mult, ALU.add))
            dve.tensor_scalar(NSP8, p, -8.0, None, ALU.mult)
            link(dve.tensor_scalar(SP8, p, 8.0, None, ALU.mult))

            def add_branch(br, c, s_):
                e = 2 * c + (8 * br + s_)
                for half in range(2):
                    cols = slice(half * HW, (half + 1) * HW)
                    dst = (MA, MB)[s_][:, bass.ds(c, 1), cols]
                    ps = PS[:, 4 + half:5 + half, :]
                    dve.wait_ge(r1.out, 2 * e + (54 + half + 1))
                    dve.wait_ge(y_mm, e + 1)
                    if br == 0:
                        dve.tensor_tensor(dst, gm(br, half).unsqueeze(1), ps, ALU.mult).then_inc(y_used, 1)
                    else:
                        dve.tensor_tensor(YT[:].unsqueeze(1), gm(br, half).unsqueeze(1), ps, ALU.mult).then_inc(y_used, 1)
                        dve.wait_ge(y_used, 2 * e + half + 1)
                        ins = dve.tensor_tensor(dst, dst, YT[:].unsqueeze(1), ALU.add)
                        ins.then_inc(sum_done, 1)
                        dve.wait_ge(sum_done, 2 * e + (half + 1 - 16))

            N_LRU = 8

            def lru(c, taps=()):
                ch = Chain(dve, lru_step, N_LRU * c)
                x0 = UX[:, bass.ds(c + LX, 1), :]
                xr, ri, ra = XR[:].unsqueeze(1), RI[:].unsqueeze(1), RA[:].unsqueeze(1)
                lb = ROWS["lru_b_conv"][0]

                def w(n):
                    return LCW[:, bass.ds(c, 1), n].rearrange("p a -> p a")

                ch.link(dve.tensor_scalar(xr, x0, w(3), COLS[:, bass.ds(c + lb, 1)], ALU.mult, ALU.add))
                for sh in range(1, LTAPS):
                    ins = dve.scalar_tensor_tensor(xr[:, :, sh:S], x0[:, :, 0:S - sh], w(3 - sh), xr[:, :, sh:S], ALU.mult, ALU.add)
                    if sh < LTAPS - 1:
                        ch.link(ins)
                    else:
                        ins.then_inc(lru_x, 1)
                        dve.wait_ge(lru_x, c + 1)
                add_branch(0, c, 0)
                dve.wait_ge(lru_ab, 3 * c + 3)
                ch.link(dve.tensor_tensor(RI[:], RI[:], XR[:], ALU.mult))
                ch.link(dve.tensor_tensor(XR[:], RA[:], RA[:], ALU.mult))
                dve.scalar_tensor_tensor(x0, xr, 1.0, x0, ALU.add, ALU.mult).then_inc(lru_v, 1)
                dve.wait_ge(lru_sq, c + 1)
                ch.link(dve.tensor_tensor(ri, ri, x0, ALU.mult))
                ch.link(dve.tensor_tensor_scan(XR[:], RA[:], RI[:], 0.0, ALU.mult, ALU.add))
                lg = UX[:, bass.ds(c + LG, 1), :]
                dve.wait_ge(lru_gelu, c + 1)
                ch.link(dve.tensor_tensor(lg, lg, xr, ALU.mult))
                dve.sem_inc(y_lru_ready, 1)
                for shift in taps:
                    tap(CC - 1, shift)
                add_branch(0, c, 1)
                assert ch.n == N_LRU

            left = TAPS - NEAR
            for c in range(CC):
                lru(c, range(NEAR + left * c // CC, NEAR + left * (c + 1) // CC))
            dve.wait_ge(y_hi, 1)
            dve.tensor_tensor(YL[1][:], UX[:, LG:LG + CC, :], YH[1][:].bitcast(F32), ALU.subtract).then_inc(y_lo, 1)
            dve.wait_ge(conv_steps, CC * TAPS)

            def diagonals(n):
                for k in range(KT):
                    a = (16, 40)[n] + k
                    dve.tensor_scalar(DG[:, k, :], IDENT[:], MODC[:, a:a + 1], None, ALU.mult).then_inc(dg_ready, 1)

            def spread_rows(n):
                dve.wait_ge(gb_mm, n + 1)
                dve.tensor_copy((G1B, G2B)[n][:], PS[:, 6:8, :].rearrange("p a b -> p (a b)")).then_inc(gb_ready, 1)

            diagonals(0)

            def over_c(ap):
                return ap.unsqueeze(1).to_broadcast([P, CC, HW])

            for half in range(2):
                cols = slice(half * HW, (half + 1) * HW)
                dve.wait_ge(ln_sum, half + 1)
                dve.scalar_tensor_tensor(CV[:, 0:CC, cols], over_c(PS[:, 6 + half, :]), -1.0 / CONV, CV[:, 0:CC, cols],
                                         ALU.mult, ALU.add).then_inc(ln_cent, 1)
            add_branch(1, 0, 0)
            add_branch(1, 0, 1)
            for half in range(2):
                dve.wait_ge(ln_var, half + 1)
                link(dve.tensor_scalar(RS[:, half, :], PS[:, 6 + half, :], 1.0 / CONV, EPS, ALU.mult, ALU.add))
                dve.reciprocal(RS[:, half, :], RS[:, half, :]).then_inc(ln_rec, 1)
            for half in range(2):
                cols = slice(half * HW, (half + 1) * HW)
                dve.wait_ge(ln_rstd, half + 1)
                dve.tensor_tensor(CV[:, 0:CC, cols], CV[:, 0:CC, cols], over_c(RS[:, half, :]), ALU.mult).then_inc(ln_norm, 1)
            spread_rows(0)
            diagonals(1)
            add_branch(1, 1, 0)
            spread_rows(1)
            add_branch(1, 1, 1)
            dve.wait_ge(y_hi, 2)
            dve.tensor_tensor(YL[2][:], CV[:, 0:CC, :], YH[2][:].bitcast(F32), ALU.subtract).then_inc(y_lo, 1)
            with dve.Fori(2, 4) as c:
                add_branch(1, c, 0)
                add_branch(1, c, 1)

            dve.tensor_copy(GSH2, MODC[:, 24:32])
            link(dve.scalar_tensor_tensor(GSC2, MODC[:, 32:40], 1.0, col("norm_ffn", 0, 8), ALU.add, ALU.mult))

            def scale_wo(q):
                dve.wait_ge(wo_loaded[q % 2], 16 * (q // 2) + 16)
                g = G1B[:, (q // 2) * HW:(q // 2 + 1) * HW].unsqueeze(1).to_broadcast([P, 4, HW])
                raw = (WOA, WOR)[q // 2][:, 4 * (q % 2):4 * (q % 2) + 4, :]
                dve.tensor_tensor(raw, raw, g, ALU.mult).then_inc(wo_scaled, 1)

            def lo_wo(q):
                dve.wait_ge(wo_hi, q + 1)
                ks = slice(4 * (q % 2), 4 * (q % 2) + 4)
                dve.tensor_tensor(WOL[q // 2][:, ks, :], (WOA, WOR)[q // 2][:, ks, :], WOH[q // 2][:, ks, :].bitcast(F32),
                                  ALU.subtract).then_inc(wo_lo, 1)

            dve.wait_ge(gb_ready, 1)
            add_branch(2, 0, 0)
            add_branch(2, 0, 1)
            scale_wo(0)
            scale_wo(1)
            lo_wo(0)
            lo_wo(1)
            with dve.Fori(1, 3) as c:
                add_branch(2, c, 0)
                add_branch(2, c, 1)

            def m_lo(ks):
                for k in ks:
                    dve.wait_ge(m_hi, M_ORDER.index(k) + 1)
                    dve.tensor_tensor(HL[:, k, :], (MA, MB)[k // 4][:, k % 4, :], HH[:, k, :].bitcast(F32), ALU.subtract).then_inc(m_ready, 1)

            add_branch(2, 3, 0)
            m_lo(M_ORDER[:4])
            add_branch(2, 3, 1)
            m_lo(M_ORDER[4:])
            for q in (2, 3):
                scale_wo(q)
            for q in (2, 3):
                lo_wo(q)

            def add_out(i):
                tok, cols = i % TT, slice((i // TT) * HW, (i // TT + 1) * HW)
                dve.wait_ge(wo_mm, i + 1)
                dve.wait_ge(x1_loaded[tok // 2], 16)
                dve.tensor_tensor(X1[:, tok, cols], X1[:, tok, cols], PS[:, i % 4, :], ALU.add).then_inc(x1_done, 1)

            def xhat(half):
                rstd(f2, half)
                for i in range(4):
                    if half and i == 0:
                        dve.wait_ge(f2.turned, 8)
                    dve.tensor_scalar(XN[:, i, :], X1[:, 4 * half + i, :], RSTD[:, 4 * half + i:4 * half + i + 1], None,
                                      ALU.mult).then_inc(f2.xhat, 1)

            for i in range(2 * TT):
                add_out(i)
                if i == TT + 3:
                    xhat(0)
                if i in (TT + 5, TT + 6):
                    split(f2, 0, HT2, range(4) if i == TT + 5 else range(4, KT))
            xhat(1)
            split(f2, 1, HT2)

            def product(m, fi, first):
                for half in range(2):
                    dve.wait_ge(f_gate, 4 * m + 2 * fi + half + 1)
                    dve.wait_ge(r3.mm, 8 * m + 4 * fi + 3 + half)
                    if not (first and fi == 0):
                        dve.wait_ge(f_lo, 2 * m + fi)
                    dve.tensor_tensor(FT[:, half, :], SA[:, half, :], PS[:, 2 + half, :], ALU.mult).then_inc(f_prod, 1)

            def add_ffn(m, after=None):
                for i in range(16):
                    tok, cols = i // 2, slice((i % 2) * HW, (i % 2 + 1) * HW)
                    dve.wait_ge(o_mm, 16 * m + i + 1)
                    dve.tensor_tensor(X1[:, tok, cols], X1[:, tok, cols], PS[:, 4 + i % 4, :], ALU.add).then_inc(o_added, 1)
                    if after and i % 2:
                        after(tok)

            product(0, 0, True)
            product(0, 1, True)
            with dve.Fori(1, FP) as m:
                product(m, 0, False)
                add_ffn(m - 1)
                product(m, 1, False)
                dve.wait_ge(o_added, 16 * m)

            def last_rstd(n):
                a, e = LAST_TILES[n]
                dve.wait_ge(f3.square, e)
                link(dve.tensor_scalar(RTMP[:, a:e], SSQ[:, a:e], 1.0 / D, EPS, ALU.mult, ALU.add))
                dve.reciprocal(RTMP[:, a:e], RTMP[:, a:e]).then_inc(f3.recip, 1)
                dve.wait_ge(f3.rstd, n + 1)

            def last_row(i):
                dve.wait_ge(o_added, 16 * (FP - 1) + 2 * i + 2)
                dve.scalar_tensor_tensor(X1[:, i, :], X1[:, i, :], RSTD[:, i:i + 1], FNB[:], ALU.mult, ALU.mult).then_inc(rows_ready, 1)

            def after(tok):
                if tok == 4:
                    last_rstd(0)
                if tok >= 4:
                    last_row(tok - 4)
                if tok == TT - 1:
                    last_rstd(1)

            dve.wait_ge(fn_loaded, 16)
            add_ffn(FP - 1, after)
            last_row(4)
            last_row(5)
            last_rstd(2)
            last_row(6)
            last_row(7)


_INS = ["x", "c", "w_mod", "b_mod", "norm_mix", "norm_ffn", "w_in", "conv_w_dw", "conv_b_dw", "conv_ln_g",
        "conv_ln_b", "conv_w_out", "nsa_pe_k", "nsa_w_ck1", "nsa_w_ck2", "nsa_pe_v", "nsa_w_cv1", "nsa_w_cv2",
        "nsa_w_out", "lru_w_conv", "lru_b_conv", "lru_w_a", "lru_b_a", "lru_w_x", "lru_b_x", "lru_lam",
        "lru_w_out", "w_merge", "b_merge", "w_out", "w_ffn_in", "w_ffn_out", "final_norm"]


def kernel(**inputs):
    import concourse.bacc as _bacc
    from concourse.bass_utils import run_bass_kernel_spmd as _run

    nc = _bacc.Bacc("TRN2", target_bir_lowering=False, num_devices=1)
    arrays, aps = {}, {}
    for name in _INS:
        a = np.ascontiguousarray(inputs[name])
        arrays[f"in_{name}"] = a
        aps[name] = nc.dram_tensor(f"in_{name}", a.shape, mybir.dt.from_np(a.dtype), kind="ExternalInput").ap()
    out = nc.dram_tensor("out_0", (1, S, D), F32, kind="ExternalOutput").ap()
    build(nc, aps, out)
    r = _run(nc, [arrays], core_ids=[0])
    return r.results[0]["out_0"]
```
